# Optimizing a Trainium2 kernel written in Bass

```python
import math
import jax, jax.numpy as jnp
from jax import lax
import numpy as np

D_MODEL = 1024
BATCH = 1
SEQ = 512
DEPTH = 1

RET_HEADS = 4
RET_DK = 128
RET_DV = 256
RET_CHUNK = 128
DIFF_HEADS = 4
DIFF_DK = 128
DIFF_DV = 256
Q_BLOCK = 128
ROPE_THETA = 10000.0
N_GROUPS = 4
EXPERTS_PER_GROUP = 8
N_EXPERTS = 32
TOP_K = 2
D_EXPERT = 512
MOE_BLOCK = 128
EPS = 1e-6

RET_QK = 512
RET_V = 1024
DIFF_QK = 1024
DIFF_V = 1024
IN_OFFSETS = (512, 1024, 2048, 3072, 4096, 5120, 6144, 7168)
D_IN = 8192


def rmsnorm(x, g):
    xf = x.astype(jnp.float32)
    y = xf * lax.rsqrt(jnp.mean(xf * xf, axis=-1, keepdims=True) + EPS)
    return (y * g.astype(jnp.float32)).astype(x.dtype)

def head_rms(o):
    of = o.astype(jnp.float32)
    return of * lax.rsqrt(jnp.mean(of * of, axis=-1, keepdims=True) + EPS)

def apply_rope(t, positions):
    d = t.shape[-1]
    inv = ROPE_THETA ** (-jnp.arange(0, d, 2, dtype=jnp.float32) / d)
    ang = positions.astype(jnp.float32)[:, :, None] * inv
    cos = jnp.cos(ang)[:, :, None, :]
    sin = jnp.sin(ang)[:, :, None, :]
    tf = t.astype(jnp.float32)
    t1, t2 = tf[..., : d // 2], tf[..., d // 2:]
    return jnp.concatenate([t1 * cos - t2 * sin, t2 * cos + t1 * sin], axis=-1).astype(t.dtype)

def retention(q, k, v):
    B, S, H, dk = q.shape
    dv = v.shape[-1]
    C = RET_CHUNK
    N = S // C
    gamma = 1.0 - jnp.exp2(-5.0 - jnp.arange(H, dtype=jnp.float32))
    log_g = jnp.log(gamma)
    idx = jnp.arange(C, dtype=jnp.float32)
    rel = idx[:, None] - idx[None, :]
    dmask = jnp.where(rel >= 0, jnp.exp(log_g[:, None, None] * jnp.maximum(rel, 0.0)), 0.0)
    zeta = jnp.exp(log_g[:, None] * (C - 1 - idx)).T
    xi = jnp.exp(log_g[:, None] * (idx + 1)).T
    chunk_decay = jnp.exp(log_g * C)
    qc = q.astype(jnp.float32).reshape(B, N, C, H, dk)
    kc = k.astype(jnp.float32).reshape(B, N, C, H, dk) * (dk ** -0.5)
    vc = v.astype(jnp.float32).reshape(B, N, C, H, dv)
    s = jnp.einsum('bnihd,bnjhd->bnhij', qc, kc) * dmask
    o_in = jnp.einsum('bnhij,bnjhe->bnihe', s, vc)
    kv = jnp.einsum('bnjhd,bnjhe->bnhde', kc * zeta[None, None, :, :, None], vc)

    def step(state, kv_n):
        return chunk_decay[None, :, None, None] * state + kv_n, state

    _, state_prev = lax.scan(step, jnp.zeros((B, H, dk, dv), jnp.float32), jnp.swapaxes(kv, 0, 1))
    o_cross = jnp.einsum('bnihd,nbhde->bnihe', qc * xi[None, None, :, :, None], state_prev)
    return (o_in + o_cross).reshape(B, S, H, dv)

def diff_attention(q, k, v, lam):
    B, S, H, _, dk = q.shape
    dv = v.shape[-1]
    nq = S // Q_BLOCK
    qb = jnp.moveaxis(q.reshape(B, nq, Q_BLOCK, H, 2, dk), 1, 0)
    kpos = jnp.arange(S)
    scale = dk ** -0.5
    neg = jnp.finfo(jnp.float32).min

    def block(args):
        i, qi = args
        s = jnp.einsum('bqhcd,bkhcd->bhcqk', qi, k).astype(jnp.float32) * scale
        qpos = i * Q_BLOCK + jnp.arange(Q_BLOCK)
        s = jnp.where(kpos[None, :] <= qpos[:, None], s, neg)
        p = jax.nn.softmax(s, axis=-1)
        a = p[:, :, 0] - lam * p[:, :, 1]
        return jnp.einsum('bhqk,bkhe->bqhe', a.astype(v.dtype), v)

    o = lax.map(block, (jnp.arange(nq), qb))
    return jnp.moveaxis(o, 0, 1).reshape(B, S, H, dv)

def hierarchical_moe(h, w_rg, b_rg, w_re, b_re, w1, w3, w2):
    T, D = h.shape
    gp = jax.nn.softmax(jnp.dot(h, w_rg).astype(jnp.float32) + b_rg, axis=-1)
    g_top, g_idx = lax.top_k(gp, 1)
    el_all = (jnp.dot(h, w_re).astype(jnp.float32) + b_re).reshape(T, N_GROUPS, EXPERTS_PER_GROUP)
    el = jnp.take_along_axis(el_all, g_idx[:, :, None], axis=1)[:, 0]
    e_val, e_idx = lax.top_k(el, TOP_K)
    weights = (g_top * jax.nn.softmax(e_val, axis=-1)).astype(h.dtype)
    expert = g_idx * EXPERTS_PER_GROUP + e_idx

    flat_e = expert.reshape(-1)
    A = flat_e.shape[0]
    order = jnp.argsort(flat_e)
    sorted_e = flat_e[order]
    counts = jnp.bincount(flat_e, length=N_EXPERTS)
    starts = jnp.cumsum(counts) - counts
    padded = ((counts + MOE_BLOCK - 1) // MOE_BLOCK) * MOE_BLOCK
    pad_ends = jnp.cumsum(padded)
    pad_starts = pad_ends - padded
    dest = pad_starts[sorted_e] + (jnp.arange(A) - starts[sorted_e])
    n_blocks = -(-A // MOE_BLOCK) + N_EXPERTS
    P = n_blocks * MOE_BLOCK
    row_token = jnp.full((P,), T, jnp.int32).at[dest].set((order // TOP_K).astype(jnp.int32))
    block_e = jnp.minimum(jnp.searchsorted(pad_ends, jnp.arange(n_blocks) * MOE_BLOCK, side='right'),
                          N_EXPERTS - 1)
    h_pad = jnp.concatenate([h, jnp.zeros((1, D), h.dtype)], axis=0)[row_token]
    h_pad = h_pad.reshape(n_blocks, MOE_BLOCK, D)

    def expert_block(args):
        xb, e = args
        return jnp.dot(jax.nn.silu(jnp.dot(xb, w1[e])) * jnp.dot(xb, w3[e]), w2[e])

    y_pad = lax.map(expert_block, (h_pad, block_e)).reshape(P, D)
    dest_of_flat = jnp.zeros((A,), jnp.int32).at[order].set(dest.astype(jnp.int32))
    y_assign = y_pad[dest_of_flat].reshape(T, TOP_K, D)
    return jnp.sum(y_assign * weights[:, :, None], axis=1)

def first_inputs(seed: int = 0) -> dict:
    key = jax.random.key(seed)
    ks = jax.random.split(key, 24)
    f32 = jnp.float32
    D = D_MODEL

    def nrm(k, shape, scale):
        return jax.random.normal(k, shape, f32) * scale

    return {
        "x": nrm(ks[0], (BATCH, SEQ, D), 1.0),
        "c": nrm(ks[1], (BATCH, D), 1.0),
        "positions": jnp.broadcast_to(jnp.arange(SEQ, dtype=jnp.int32)[None, :], (BATCH, SEQ)),
        "w_ada": nrm(ks[2], (DEPTH, D, 6 * D), D ** -0.5),
        "b_ada": nrm(ks[3], (DEPTH, 6 * D), 0.02),
        "norm_mix": 1.0 + nrm(ks[4], (DEPTH, D), 0.02),
        "w_in": nrm(ks[5], (DEPTH, D, D_IN), D ** -0.5),
        "w_ret_o": nrm(ks[6], (DEPTH, RET_V, D), RET_V ** -0.5),
        "w_diff_o": nrm(ks[7], (DEPTH, DIFF_V, D), DIFF_V ** -0.5),
        "lam_q1": nrm(ks[8], (DEPTH, DIFF_DK), 0.1),
        "lam_k1": nrm(ks[9], (DEPTH, DIFF_DK), 0.1),
        "lam_q2": nrm(ks[10], (DEPTH, DIFF_DK), 0.1),
        "lam_k2": nrm(ks[11], (DEPTH, DIFF_DK), 0.1),
        "diff_norm": 1.0 + nrm(ks[12], (DEPTH, DIFF_DV), 0.02),
        "w_out": nrm(ks[13], (DEPTH, D, D), D ** -0.5),
        "norm_ffn": 1.0 + nrm(ks[14], (DEPTH, D), 0.02),
        "w_router_group": nrm(ks[15], (DEPTH, D, N_GROUPS), D ** -0.5),
        "b_router_group": nrm(ks[16], (DEPTH, N_GROUPS), 0.01),
        "w_router_expert": nrm(ks[17], (DEPTH, D, N_GROUPS * EXPERTS_PER_GROUP), D ** -0.5),
        "b_router_expert": nrm(ks[18], (DEPTH, N_GROUPS * EXPERTS_PER_GROUP), 0.01),
        "w_exp_gate": nrm(ks[19], (DEPTH, N_EXPERTS, D, D_EXPERT), D ** -0.5),
        "w_exp_up": nrm(ks[20], (DEPTH, N_EXPERTS, D, D_EXPERT), D ** -0.5),
        "w_exp_down": nrm(ks[21], (DEPTH, N_EXPERTS, D_EXPERT, D), D_EXPERT ** -0.5),
        "norm_final": 1.0 + nrm(ks[22], (D,), 0.02),
    }

def first_block(x, c, positions, w_ada, b_ada, norm_mix, w_in, w_ret_o, w_diff_o,
              lam_q1, lam_k1, lam_q2, lam_k2, diff_norm, w_out, norm_ffn,
              w_router_group, b_router_group, w_router_expert, b_router_expert,
              w_exp_gate, w_exp_up, w_exp_down, norm_final):
    B, S, D = x.shape
    for l in range(DEPTH):
        lambda_init = 0.8 - 0.6 * math.exp(-0.3 * l)
        mod = (jnp.dot(jax.nn.silu(c), w_ada[l]) + b_ada[l])[:, None, :]
        sh1, sc1, g1, sh2, sc2, g2 = jnp.split(mod, 6, axis=-1)

        h = rmsnorm(x, norm_mix[l]) * (1.0 + sc1) + sh1
        proj = jnp.dot(h, w_in[l])
        rq, rk, rv, rg, dq, dk, dv, gate_r, gate_d = jnp.split(proj, list(IN_OFFSETS), axis=-1)

        rq = apply_rope(rq.reshape(B, S, RET_HEADS, RET_DK), positions)
        rk = apply_rope(rk.reshape(B, S, RET_HEADS, RET_DK), positions)
        ro = retention(rq, rk, rv.reshape(B, S, RET_HEADS, RET_DV))
        ro = head_rms(ro).reshape(B, S, RET_V).astype(x.dtype) * jax.nn.silu(rg)
        ret_out = jnp.dot(ro, w_ret_o[l])

        dq = apply_rope(dq.reshape(B, S, 2 * DIFF_HEADS, DIFF_DK), positions).reshape(B, S, DIFF_HEADS, 2, DIFF_DK)
        dk = apply_rope(dk.reshape(B, S, 2 * DIFF_HEADS, DIFF_DK), positions).reshape(B, S, DIFF_HEADS, 2, DIFF_DK)
        lam = (jnp.exp(jnp.sum(lam_q1[l].astype(jnp.float32) * lam_k1[l].astype(jnp.float32)))
               - jnp.exp(jnp.sum(lam_q2[l].astype(jnp.float32) * lam_k2[l].astype(jnp.float32)))
               + lambda_init)
        do = diff_attention(dq, dk, dv.reshape(B, S, DIFF_HEADS, DIFF_DV), lam)
        do = head_rms(do) * diff_norm[l].astype(jnp.float32) * (1.0 - lambda_init)
        diff_out = jnp.dot(do.reshape(B, S, DIFF_V).astype(x.dtype), w_diff_o[l])

        merged = jax.nn.sigmoid(gate_r) * ret_out + jax.nn.sigmoid(gate_d) * diff_out
        x = x + g1 * jnp.dot(merged, w_out[l])

        h2 = rmsnorm(x, norm_ffn[l]) * (1.0 + sc2) + sh2
        y = hierarchical_moe(h2.reshape(B * S, D), w_router_group[l], b_router_group[l],
                             w_router_expert[l], b_router_expert[l],
                             w_exp_gate[l], w_exp_up[l], w_exp_down[l]).reshape(B, S, D)
        x = x + g2 * y
    return rmsnorm(x, norm_final)


CHUNK = 64
D_MIX = D_MODEL
ATTN_HEADS = 8
ATTN_KV_HEADS = 2
HEAD_DIM = 64
ATTN_GROUP = ATTN_HEADS // ATTN_KV_HEADS
WINDOW = 128
WIN_CHUNKS = WINDOW // CHUNK
BAND = (WIN_CHUNKS + 1) * CHUNK
D_ATTN = ATTN_HEADS * HEAD_DIM
D_KV = ATTN_KV_HEADS * HEAD_DIM
POOL_WINDOWS = (2, 4, 8, 16)
POOL_GROUPS = len(POOL_WINDOWS)
D_POOL = D_MIX - D_ATTN
POOL_GROUP_DIM = D_POOL // POOL_GROUPS
D_IN_2 = D_ATTN + 2 * D_KV + D_POOL
REL_BUCKETS = 32
REL_MAX_DIST = 128
PEER_KEYS = 128
PEER_EXPERTS = PEER_KEYS * PEER_KEYS
PEER_HEADS = 8
PEER_TOPK = 16
PEER_QDIM = 256
PEER_HALF = PEER_QDIM // 2
PEER_TOKEN_BLOCK = 128
NEG_INF = -1e30


def rms_norm(x, g):
    xf = x.astype(jnp.float32)
    y = xf * lax.rsqrt(jnp.mean(xf * xf, axis=-1, keepdims=True) + EPS)
    return (y * g.astype(jnp.float32)).astype(x.dtype)

def t5_bucket(rel):
    nb = REL_BUCKETS // 2
    max_exact = nb // 2
    base = jnp.where(rel > 0, nb, 0)
    n = jnp.abs(rel)
    nf = jnp.maximum(n, 1).astype(jnp.float32)
    large = max_exact + (jnp.log(nf / max_exact) / math.log(REL_MAX_DIST / max_exact)
                         * (nb - max_exact)).astype(jnp.int32)
    large = jnp.minimum(large, nb - 1)
    return base + jnp.where(n < max_exact, n, large)

def band_bias(rel_bias):
    i = jnp.arange(CHUNK)[:, None]
    j = jnp.arange(BAND)[None, :]
    rel = (j - WIN_CHUNKS * CHUNK) - i
    b = jnp.take(rel_bias, t5_bucket(rel), axis=0)
    b = jnp.transpose(b, (2, 0, 1)).astype(jnp.float32)
    return b.reshape(ATTN_KV_HEADS, ATTN_GROUP, CHUNK, BAND)

def to_band(t, n_chunks):
    pad = [(0, 0), (WIN_CHUNKS, 0)] + [(0, 0)] * (t.ndim - 2)
    tp = jnp.pad(t, pad)
    return jnp.concatenate([tp[:, i:i + n_chunks] for i in range(WIN_CHUNKS + 1)], axis=2)

def swa_attention(q, k, v, q_norm_g, k_norm_g, sinks, rel_bias):
    B, S, _ = q.shape
    nc = S // CHUNK
    q = rms_norm(q.reshape(B, S, ATTN_HEADS, HEAD_DIM), q_norm_g)
    k = rms_norm(k.reshape(B, S, ATTN_KV_HEADS, HEAD_DIM), k_norm_g)
    v = v.reshape(B, S, ATTN_KV_HEADS, HEAD_DIM)
    qc = q.reshape(B, nc, CHUNK, ATTN_KV_HEADS, ATTN_GROUP, HEAD_DIM)
    kb = to_band(k.reshape(B, nc, CHUNK, ATTN_KV_HEADS, HEAD_DIM), nc)
    vb = to_band(v.reshape(B, nc, CHUNK, ATTN_KV_HEADS, HEAD_DIM), nc)
    s = jnp.einsum('bcqhgd,bckhd->bchgqk', qc, kb,
                   preferred_element_type=jnp.float32) * (HEAD_DIM ** -0.5)
    s = s + band_bias(rel_bias)[None, None]
    key_chunk = jnp.arange(nc)[:, None] - WIN_CHUNKS + jnp.arange(BAND)[None, :] // CHUNK
    valid = (key_chunk >= 0)[None, :, None, None, None, :]
    s = jnp.where(valid, s, NEG_INF)
    sink = sinks.astype(jnp.float32).reshape(1, 1, ATTN_KV_HEADS, ATTN_GROUP, 1, 1)
    m = jnp.maximum(jnp.max(s, axis=-1, keepdims=True), sink)
    p = jnp.exp(s - m)
    p = p / (jnp.sum(p, axis=-1, keepdims=True) + jnp.exp(sink - m))
    o = jnp.einsum('bchgqk,bckhd->bcqhgd', p.astype(vb.dtype), vb)
    return o.reshape(B, S, D_ATTN)

def causal_mean(xg, w):
    S = xg.shape[1]
    cs = jnp.pad(jnp.cumsum(xg, axis=1), ((0, 0), (1, 0), (0, 0)))
    t = jnp.arange(S)
    lo = jnp.maximum(t + 1 - w, 0)
    total = cs[:, 1:] - jnp.take(cs, lo, axis=1)
    cnt = jnp.minimum(t + 1, w).astype(jnp.float32)
    return total / cnt[None, :, None]

def pool_mixer(p, pool_w, pool_scale):
    B, S, _ = p.shape
    pf = p.astype(jnp.float32).reshape(B, S, POOL_GROUPS, POOL_GROUP_DIM)
    pooled = jnp.stack([causal_mean(pf[:, :, g], w) for g, w in enumerate(POOL_WINDOWS)], axis=2)
    d = (pooled - pf).astype(p.dtype)
    o = jnp.einsum('bsgc,gcd->bsgd', d, pool_w)
    o = o * pool_scale.reshape(POOL_GROUPS, POOL_GROUP_DIM)
    return o.reshape(B, S, D_POOL)

def peer(h, wq, subkeys, u_tab, v_tab):
    B, S, D = h.shape
    T = B * S
    ht = h.reshape(T, D)
    q = (ht @ wq).reshape(T, PEER_HEADS, 2, PEER_HALF)
    sc = jnp.einsum('thpd,hpnd->thpn', q, subkeys, preferred_element_type=jnp.float32)
    v1, i1 = lax.top_k(sc[:, :, 0], PEER_TOPK)
    v2, i2 = lax.top_k(sc[:, :, 1], PEER_TOPK)
    cand = (v1[..., :, None] + v2[..., None, :]).reshape(T, PEER_HEADS, PEER_TOPK * PEER_TOPK)
    best, pos = lax.top_k(cand, PEER_TOPK)
    e1 = jnp.take_along_axis(i1, pos // PEER_TOPK, axis=-1)
    e2 = jnp.take_along_axis(i2, pos % PEER_TOPK, axis=-1)
    experts = (e1 * PEER_KEYS + e2).reshape(T, PEER_HEADS * PEER_TOPK)
    gates = jax.nn.softmax(best, axis=-1).reshape(T, PEER_HEADS * PEER_TOPK).astype(h.dtype)

    def block(args):
        xb, eb, gb = args
        u = jnp.take(u_tab, eb, axis=0)
        vv = jnp.take(v_tab, eb, axis=0)
        act = jax.nn.gelu(jnp.einsum('tkd,td->tk', u, xb), approximate=False)
        return jnp.einsum('tk,tkd->td', gb * act, vv)

    nb = T // PEER_TOKEN_BLOCK
    out = lax.map(block, (ht.reshape(nb, PEER_TOKEN_BLOCK, D),
                          experts.reshape(nb, PEER_TOKEN_BLOCK, -1),
                          gates.reshape(nb, PEER_TOKEN_BLOCK, -1)))
    return out.reshape(B, S, D)

def second_inputs(seed: int = 0) -> dict:
    key = jax.random.key(seed)
    ks = jax.random.split(key, 15)
    n = jax.random.normal
    L = DEPTH
    return {
        "x": n(ks[0], (BATCH, SEQ, D_MODEL), jnp.float32),
        "norm1_g": 1.0 + 0.02 * n(ks[1], (L, D_MODEL), jnp.float32),
        "w_in": n(ks[2], (L, D_MODEL, D_IN_2), jnp.float32) * D_MODEL ** -0.5,
        "q_norm_g": 1.0 + 0.02 * n(ks[3], (L, HEAD_DIM), jnp.float32),
        "k_norm_g": 1.0 + 0.02 * n(ks[4], (L, HEAD_DIM), jnp.float32),
        "attn_sinks": 0.5 * n(ks[5], (L, ATTN_HEADS), jnp.float32),
        "rel_bias": 0.5 * n(ks[6], (REL_BUCKETS, ATTN_HEADS), jnp.float32),
        "pool_w": n(ks[7], (L, POOL_GROUPS, POOL_GROUP_DIM, POOL_GROUP_DIM), jnp.float32) * POOL_GROUP_DIM ** -0.5,
        "pool_scale": 1.0 + 0.02 * n(ks[8], (L, D_POOL), jnp.float32),
        "w_out": n(ks[9], (L, D_MIX, D_MODEL), jnp.float32) * D_MIX ** -0.5,
        "norm2_g": 1.0 + 0.02 * n(ks[10], (L, D_MODEL), jnp.float32),
        "peer_wq": n(ks[11], (L, D_MODEL, PEER_HEADS * PEER_QDIM), jnp.float32) * D_MODEL ** -0.5,
        "peer_subkeys": n(ks[12], (L, PEER_HEADS, 2, PEER_KEYS, PEER_HALF), jnp.float32) * PEER_HALF ** -0.5,
        "peer_u": n(ks[13], (L, PEER_EXPERTS, D_MODEL), jnp.float32) * D_MODEL ** -0.5,
        "peer_v": n(ks[14], (L, PEER_EXPERTS, D_MODEL), jnp.float32) * (PEER_HEADS * PEER_TOPK) ** -0.5,
    }

def second_block(x, norm1_g, w_in, q_norm_g, k_norm_g, attn_sinks, rel_bias, pool_w, pool_scale,
              w_out, norm2_g, peer_wq, peer_subkeys, peer_u, peer_v):
    for l in range(DEPTH):
        h = rms_norm(x, norm1_g[l])
        y = h @ w_in[l]
        q = y[..., :D_ATTN]
        k = y[..., D_ATTN:D_ATTN + D_KV]
        v = y[..., D_ATTN + D_KV:D_ATTN + 2 * D_KV]
        p = y[..., D_ATTN + 2 * D_KV:]
        a = swa_attention(q, k, v, q_norm_g[l], k_norm_g[l], attn_sinks[l], rel_bias)
        b = pool_mixer(p, pool_w[l], pool_scale[l])
        x = x + jnp.concatenate([a, b], axis=-1) @ w_out[l]
        h2 = rms_norm(x, norm2_g[l])
        x = x + peer(h2, peer_wq[l], peer_subkeys[l], peer_u[l], peer_v[l])
    return x


def setup_inputs(seed=0):
    out = dict(first_inputs(seed))
    for name, value in second_inputs(seed + 1).items():
        if name != "x":
            out[name + "_2"] = value
    return out


def reference(
    x, c, positions, w_ada, b_ada, norm_mix, w_in, w_ret_o, w_diff_o, lam_q1, lam_k1, lam_q2,
    lam_k2, diff_norm, w_out, norm_ffn, w_router_group, b_router_group, w_router_expert,
    b_router_expert, w_exp_gate, w_exp_up, w_exp_down, norm_final, norm1_g_2, w_in_2,
    q_norm_g_2, k_norm_g_2, attn_sinks_2, rel_bias_2, pool_w_2, pool_scale_2, w_out_2,
    norm2_g_2, peer_wq_2, peer_subkeys_2, peer_u_2, peer_v_2,
):
    x = first_block(
        x, c, positions, w_ada, b_ada, norm_mix, w_in, w_ret_o, w_diff_o, lam_q1, lam_k1,
        lam_q2, lam_k2, diff_norm, w_out, norm_ffn, w_router_group, b_router_group,
        w_router_expert, b_router_expert, w_exp_gate, w_exp_up, w_exp_down, norm_final,
    )
    return second_block(
        x, norm1_g_2, w_in_2, q_norm_g_2, k_norm_g_2, attn_sinks_2, rel_bias_2, pool_w_2,
        pool_scale_2, w_out_2, norm2_g_2, peer_wq_2, peer_subkeys_2, peer_u_2, peer_v_2,
    )


_drawn_inputs = setup_inputs


def setup_inputs(seed=0):
    import zlib

    import numpy as np

    out = dict(_drawn_inputs(seed))
    spreads = {}
    factors = {'lam_q1': 3.571,
     'lam_k1': 4.196,
     'lam_q2': 3.612,
     'lam_k2': 2.946,
     'diff_norm': 4.716,
     'b_router_group': 16.313,
     'b_router_expert': 4.253,
     'norm_final': 2.711,
     'norm1_g_2': 4.753,
     'q_norm_g_2': 8.0,
     'k_norm_g_2': 8.0,
     'attn_sinks_2': 8.0,
     'pool_scale_2': 14.675,
     'norm2_g_2': 64.0,
     'rel_bias_2': 4.399}
    for name, (base, spread) in spreads.items():
        noise = np.random.default_rng([zlib.crc32(name.encode()), seed]).standard_normal(out[name].shape)
        drawn = base * np.exp(spread * noise) if base else spread * noise
        out[name] = __import__('jax').numpy.asarray(drawn.astype(out[name].dtype))
    for name, factor in factors.items():
        out[name] = (out[name] * factor).astype(out[name].dtype)
    return out
```

```python
from contextlib import ExitStack

import concourse.bass as bass
from concourse import mybir

F32 = mybir.dt.float32
I32 = mybir.dt.int32
U32 = mybir.dt.uint32
ACT = mybir.ActivationFunctionType
ALU = mybir.AluOpType
AX = mybir.AxisListType

P = 128
T = 512
TT = T // P
D = 1024
DC = D // P
HEADS = 4
DV = 256
EPS = 1e-6
LAMBDA_INIT = 0.2
ATT_SCALE = float(P) ** -0.5
RING = 4
SLAB = 4096
EXPERTS = 32
GROUPS = 4
SLOTS = 128
OVER = 7
BLOCKS = EXPERTS + OVER + 1
ROWS = 2 * T
SWA_HEADS = 8
HD = 64
BAND = 256
VEC = 384
PH = 8
TOPK = 16
PK = 128
NEG = -1.0e30
LOWEST = -3.0e38

(S_RQ, S_RK, S_RV, S_RG, S_RO, S_GR, S_DQ, S_DK, S_DV, S_DO, S_GD, S_OUT) = (
    0, 1, 2, 4, 6, 8, 10, 12, 14, 16, 18, 20)
S_MOE = 22
S_IN2 = S_MOE + 3 * EXPERTS
S_OUT2 = S_IN2 + 3
S_WQ = S_OUT2 + 2
S_U = S_WQ + 4
S_V = S_U + PK // 4
S_END = S_V + PK // 4

C_IDENT, C_ONES, C_HALVES, C_CAUSAL, C_BEFORE, C_IOTA = 0, 128, 256, 384, 512, 640
C_INV, C_SIGN, C_TOKEN, C_COUNT, C_MASK = 768, 769, 770, 774, 774 + 64
C_END = C_MASK + BAND


class Chain:

    def __init__(self, sem):
        self.sem, self.n = sem, 0

    def __call__(self, engine, instruction):
        instruction.then_inc(self.sem, 1)
        self.n += 1
        engine.wait_ge(self.sem, self.n)


class Names:

    def begin(self, first_slab):
        self.first_slab = first_slab
        self.emptied_before = self.emptied_after

    def tile(self, s, j):
        return 4 * (s - self.first_slab) + j

    def wait_product(self, engine, s, j):
        engine.wait_ge(self.products, 4 * s + j + 1)

    def wait_bank(self, engine, s, j):
        if self.tile(s, j) >= 4:
            self.wait_emptied(engine, self.tile(s, j) - 3)

    def wait_emptied(self, engine, n):
        engine.wait_ge(self.emptied, self.emptied_before + n)

    def end(self, tiles):
        self.emptied_after = self.emptied_before + tiles


def bcast(ap, where, n):
    dims = list(ap.shape)
    return ap.unsqueeze(where).to_broadcast(dims[:where] + [n] + dims[where:])


def load_slabs(m, sp, until):
    def one(s, slot):
        if isinstance(s, int):
            if s >= RING:
                sp.wait_ge(m.products, 4 * (s - RING + 1))
            src = m.weights[s]
        else:
            sp.wait_ge(m.products, 4 * s - 4 * (RING - 1))
            src = m.weights[bass.ds(s, 1)].rearrange("a p n -> (a p) n")
        sp.dma_start(m.ring[:, slot, :], src).then_inc(m.slab_loaded[slot], 16)

    while m.issued < until and (m.issued % RING or m.issued < RING):
        one(m.issued, m.issued % RING)
        m.issued += 1
    turns = (until - m.issued) // RING
    if turns >= 2:
        first = m.issued
        with sp.Fori(0, turns) as turn:
            for slot in range(RING):
                one(turn * RING + (first + slot), slot)
        m.issued += turns * RING
    while m.issued < until:
        one(m.issued, m.issued % RING)
        m.issued += 1


def wait_slab(m, engine, s):
    engine.wait_ge(m.slab_loaded[s % RING], 16 * (s // RING + 1))


def pe_features(m, pe, s, acts, tiles=4):
    wait_slab(m, pe, s)
    for j in range(tiles):
        m.wait_bank(pe, s, j)
        for k in range(DC):
            mm = pe.matmul(m.bank[j][:, :], m.ring[:, s % RING, (j * DC + k) * P:(j * DC + k + 1) * P],
                           acts[:, k, :], start=(k == 0), stop=(k == DC - 1))
        mm.then_inc(m.products, 1)


def pe_tokens(m, pe, s, acts):
    wait_slab(m, pe, s)
    for j in range(TT):
        m.wait_bank(pe, s, j)
        for k in range(DC):
            mm = pe.matmul(m.bank[j][:, :], acts[:, k, j * P:(j + 1) * P],
                           m.ring[:, s % RING, k * 512:(k + 1) * 512], start=(k == 0), stop=(k == DC - 1))
        mm.then_inc(m.products, 1)


def stage_modulation(nc, m):
    with ExitStack() as own:
        sb = lambda name, shape, dt=F32: own.enter_context(nc.sbuf_tensor(name, shape, dt))
        ada = sb("ada_w", [P, 3, SLAB])
        c_row = sb("c_row", [P, D])
        c_act = sb("c_act", [P, D])
        junk = sb("ada_junk", [P, D])
        b_ada = sb("b_ada", [P, 48])
        raw = sb("mod_raw", [P, 48])
        pos = sb("pos", [P, T], I32)
        ang = sb("ang", [P, T])
        turn = sb("turn", [P, T])
        mag = sb("mag", [P, T])
        halfpi = sb("halfpi", [P, 1])
        lam_in = sb("lam_in", [P, 4, P])
        lam_p = sb("lam_p", [P, P])
        lam_s = sb("lam_s", [P, 2])
        lam_e = sb("lam_e", [P, 2])
        rel = sb("rel", [32, SWA_HEADS])
        rel_wide = sb("rel_wide", [32, SWA_HEADS, P])
        buckets = sb("buckets", [32, VEC])
        by_distance = sb("by_distance", [P, 2, VEC])

        small = m.sem("mod_small")
        xin = m.sem("mod_x")
        ada_loaded = [m.sem(f"ada_loaded{i}") for i in range(3)]
        ada_used = m.sem("ada_used")
        c_ready = m.sem("c_ready")
        ang_ready = m.sem("ang_ready")
        sin_ready = m.sem("sin_ready")
        lam_ready = m.sem("lam_ready")
        lam_exp = m.sem("lam_exp")
        wide_ready = m.sem("wide_ready")
        dist_mm = m.sem("dist_mm")
        dist_sb = m.sem("dist_sb")
        dist_out = [m.sem(f"dist_out{i}") for i in range(2)]
        block = own.enter_context(nc.Block(no_gpsimd_drain=True))
        d = m.dram
        loads = [(c_row[:, :], d.c.to_broadcast([P, D])), (b_ada[:, :], d.b_ada),
                 (pos[:, :], d.positions.to_broadcast([P, T])), (m.const[:, :], d.const),
                 (m.vec[:, :, :], d.vec), (m.dn[:, :], d.diff_norm), (m.small[:, :], d.small),
                 (m.sinks[:, :], d.sinks.to_broadcast([P, SWA_HEADS])), (rel[:, :], d.rel_bias),
                 (buckets[:, :], d.buckets)]
        loads += [(lam_in[:, i, :], a.to_broadcast([P, P])) for i, a in enumerate(d.lams)]

        @block.sync
        def _(sp):
            sp.dma_start(m.xT[:, :, :], d.x).then_inc(xin, 16)
            for s in range(12):
                if s >= 3:
                    sp.wait_ge(ada_used, s - 2)
                sp.dma_start(ada[:, s % 3, :], d.w_ada[s]).then_inc(ada_loaded[s % 3], 16)
            load_slabs(m, sp, RING)
            sp.wait_ge(xin, 16)

        @block.scalar
        def _(act):
            for dst, src in loads:
                act.dma_start(dst, src).then_inc(small, 16)
            act.wait_ge(small, 16 * len(loads))
            act.activation(c_act[:, :], c_row[:, :], ACT.Silu).then_inc(c_ready, 1)
            act.wait_ge(ang_ready, 1)
            act.activation(m.rot_sin[:, :], ang[:, :], ACT.Sin).then_inc(sin_ready, 1)
            act.wait_ge(ang_ready, 2)
            act.activation(m.rot_cos[:, :], mag[:, :], ACT.Sin, bias=halfpi[:, :], scale=-1.0).then_inc(sin_ready, 1)
            act.wait_ge(lam_ready, 1)
            act.activation(lam_e[:, :], lam_s[:, :], ACT.Exp).then_inc(lam_exp, 1)
            for h in range(SWA_HEADS):
                act.wait_ge(dist_mm, h + 1)
                if h >= 2:
                    act.wait_ge(dist_out[h % 2], 16 * (h // 2))
                act.activation(by_distance[:, h % 2, :], m.bank[h % 4][:, 0:VEC], ACT.Copy).then_inc(dist_sb, 1)
                act.wait_ge(dist_sb, h + 1)
                act.dma_start(d.by_distance[h], by_distance[:, h % 2, :]).then_inc(dist_out[h % 2], 16)
            for i in range(2):
                act.wait_ge(dist_out[i], 16 * SWA_HEADS // 2)

        @block.tensor
        def _(pe):
            pe.wait_ge(wide_ready, 1)
            pe.wait_ge(small, 16 * len(loads))
            for h in range(SWA_HEADS):
                if h >= 4:
                    pe.wait_ge(dist_sb, h - 3)
                pe.matmul(m.bank[h % 4][:, 0:VEC], rel_wide[:, h, :], buckets[:, :],
                          start=True, stop=True).then_inc(dist_mm, 1)

        @block.vector
        def _(dve):
            chain = lambda instruction: m.chain(dve, instruction)
            dve.memset(m.eps[:, :], EPS)
            dve.memset(halfpi[:, :], 1.5707963267948966)
            dve.wait_ge(small, 16 * len(loads))
            chain(dve.tensor_copy(turn[:, :], pos[:, :]))
            chain(dve.tensor_scalar(ang[:, :], turn[:, :], m.const[:, C_INV:C_INV + 1], None, ALU.mult))
            chain(dve.tensor_scalar(turn[:, :], ang[:, :], 0.15915494309189535, 12582912.0, ALU.mult, ALU.add))
            chain(dve.tensor_scalar(turn[:, :], turn[:, :], 12582912.0, None, ALU.subtract))
            for part in (-6.28125, -0.0019340515136718750, -1.2556659146019e-06):
                chain(dve.scalar_tensor_tensor(out=ang[:, :], in0=turn[:, :], scalar=part, in1=ang[:, :],
                                               op0=ALU.mult, op1=ALU.add))
            chain(dve.tensor_scalar(ang[:, :], ang[:, :], 3.1415925, -3.1415925, ALU.min, ALU.max))
            dve.scalar_tensor_tensor(out=mag[:, :], in0=ang[:, :], scalar=-1.0, in1=ang[:, :], op0=ALU.mult,
                                     op1=ALU.max).then_inc(ang_ready, 2)
            chain(dve.tensor_copy(rel_wide[:, :, :], bcast(rel[:, :], 2, P)))
            dve.sem_inc(wide_ready, 1)
            for i in range(2):
                chain(dve.tensor_tensor(lam_p[:, :], lam_in[:, 2 * i, :], lam_in[:, 2 * i + 1, :], ALU.mult))
                chain(dve.tensor_reduce(lam_s[:, i:i + 1], lam_p[:, :], AX.X, ALU.add))
            dve.sem_inc(lam_ready, 1)
            dve.wait_ge(sin_ready, 2)
            chain(dve.tensor_scalar(m.rot_sin[:, :], m.rot_sin[:, :], m.const[:, C_SIGN:C_SIGN + 1], None, ALU.mult))
            dve.wait_ge(lam_exp, 1)
            chain(dve.tensor_tensor(m.neg_lam[:, :], lam_e[:, 1:2], lam_e[:, 0:1], ALU.subtract))
            chain(dve.tensor_scalar(m.neg_lam[:, :], m.neg_lam[:, :], LAMBDA_INIT, None, ALU.subtract))
            dve.tensor_scalar(m.dn[:, :], m.dn[:, :], 1.0 - LAMBDA_INIT, None, ALU.mult)
            dve.wait_ge(c_ready, 1)
            for s in range(12):
                dve.wait_ge(ada_loaded[s % 3], 16 * (s // 3 + 1))
                for j in range(4):
                    n = 4 * s + j
                    chain(dve.tensor_tensor_reduce(
                        out=junk[:, :], in0=ada[:, s % 3, j * D:(j + 1) * D], in1=c_act[:, :], scale=1.0,
                        scalar=0.0, op0=ALU.mult, op1=ALU.add, accum_out=raw[:, n:n + 1]))
                dve.sem_inc(ada_used, 1)
            chain(dve.tensor_tensor(m.mod[:, :], raw[:, :], b_ada[:, :], ALU.add))
            for v, at in ((0, 8), (1, 32)):
                chain(dve.tensor_scalar(raw[:, 0:8], m.mod[:, at:at + 8], 1.0, None, ALU.add))
                chain(dve.tensor_tensor(m.scale[:, v, :], raw[:, 0:8], m.vec[:, v, :], ALU.mult))


def stage_norm(nc, m, name, src, dst, scale, shift=None):
    squares, total, root, scaled = m.norm_sems
    n = m.norms
    m.norms += 1
    with ExitStack() as own:
        rstd = own.enter_context(nc.sbuf_tensor(name + "_rstd", [P, T], F32))
        block = own.enter_context(nc.Block(no_gpsimd_drain=True))

        @block.scalar
        def _(act):
            for k in range(DC):
                act.activation(dst[:, k, :], src[:, k, :], ACT.Square).then_inc(squares, 1)
            act.wait_ge(total, n + 1)
            act.activation(rstd[:, :], m.bank[4][:, :], ACT.Sqrt, bias=m.eps[:, :], scale=1.0 / D).then_inc(root, 1)
            if shift is not None:
                for k in range(DC):
                    act.wait_ge(scaled, n * DC + k + 1)
                    act.activation(dst[:, k, :], dst[:, k, :], ACT.Identity, bias=shift[:, k:k + 1])

        @block.tensor
        def _(pe):
            for k in range(DC):
                pe.wait_ge(squares, n * DC + k + 1)
                mm = pe.matmul(m.bank[4][:, :], m.ones, dst[:, k, :], start=(k == 0), stop=(k == DC - 1))
            mm.then_inc(total, 1)

        @block.vector
        def _(dve):
            dve.wait_ge(root, n + 1)
            m.chain(dve, dve.reciprocal(rstd[:, :], rstd[:, :]))
            for k in range(DC):
                dve.scalar_tensor_tensor(out=dst[:, k, :], in0=src[:, k, :], scalar=scale[:, k:k + 1],
                                         in1=rstd[:, :], op0=ALU.mult, op1=ALU.mult).then_inc(scaled, 1)


def stage_project(nc, m, name, rotated, values, acts, vals):
    m.begin(rotated[0][0])
    with ExitStack() as own:
        straight = own.enter_context(nc.sbuf_tensor(name + "_straight", [P, T], F32))
        crossed = own.enter_context(nc.sbuf_tensor(name + "_crossed", [P, T], F32))
        block = own.enter_context(nc.Block(no_gpsimd_drain=True))
        half = P // 2

        @block.sync
        def _(sp):
            load_slabs(m, sp, values[-1][0] + 1 + RING)

        @block.tensor
        def _(pe):
            for s, _, _ in rotated:
                pe_features(m, pe, s, acts)
            for s, _ in values:
                pe_tokens(m, pe, s, acts)

        @block.vector
        def _(dve):
            chain = lambda instruction: m.chain(dve, instruction)
            for s, dst, chunk in rotated:
                for j in range(4):
                    m.wait_product(dve, s, j)
                    acc = m.bank[j]
                    dve.tensor_tensor(straight[:, :], acc[:, :], m.rot_cos[:, :], ALU.mult)
                    dve.tensor_tensor(crossed[0:half, :], acc[half:P, :], m.rot_sin[half:P, :], ALU.mult)
                    chain(dve.tensor_tensor(crossed[half:P, :], acc[0:half, :], m.rot_sin[0:half, :], ALU.mult))
                    chain(dve.tensor_tensor(dst[:, chunk + j, :], straight[:, :], crossed[:, :], ALU.add))
                    dve.sem_inc(m.emptied, 1)

        @block.scalar
        def _(act):
            m.wait_emptied(act, 4 * len(rotated))
            for s, column in values:
                for j in range(TT):
                    m.wait_product(act, s, j)
                    act.activation(vals[:, j, column:column + 512], m.bank[j][:, :], ACT.Copy).then_inc(m.emptied, 1)
    m.end(4 * (len(rotated) + len(values)))


def head_norm_act(m, act, o_banks, ss_bank, squares, std, h, s):
    act.wait_ge(s.out_ready, h + 1)
    if h >= 1:
        act.wait_ge(s.total, h)
    for c in range(2):
        act.activation(squares[:, c, :], o_banks[c][:, :], ACT.Square).then_inc(s.squares, 1)
    act.wait_ge(s.total, h + 1)
    if h >= 1:
        act.wait_ge(s.normed, h)
    act.activation(std[:, :], ss_bank[:, :], ACT.Sqrt, bias=m.eps[:, :], scale=1.0 / DV).then_inc(s.root, 1)


def stage_retention(nc, m, qT, kT, vals, roT):
    with ExitStack() as own:
        sb = lambda name, shape: own.enter_context(nc.sbuf_tensor(name, shape, F32))
        decay = sb("decay", [P, HEADS, T])
        probs = sb("ret_probs", [P, 2, TT, T])
        squares = sb("ret_sq", [P, 2, T])
        std = sb("ret_std", [P, T])
        s = Names()
        s.decay, s.scores, s.weighted, s.out_ready, s.squares, s.total, s.root, s.normed = (
            m.sem(f"ret_{x}") for x in ("decay", "scores", "weighted", "out", "squares", "total", "root", "normed"))
        block = own.enter_context(nc.Block(no_gpsimd_drain=True))
        score_bank = [m.bank[i] for i in (0, 1, 4, 5)]
        o_bank = [m.bank[6], m.bank[7]]
        ss_bank = m.bank[2]

        @block.sync
        def _(sp):
            sp.dma_start(decay[:, :, :], m.dram.decay).then_inc(s.decay, 16)
            sp.wait_ge(s.decay, 16)

        @block.tensor
        def _(pe):
            def scores(h):
                if h >= 1:
                    pe.wait_ge(s.weighted, TT * h)
                for j in range(TT):
                    pe.matmul(score_bank[j][:, 0:T - j * P], kT[:, h, j * P:(j + 1) * P], qT[:, h, j * P:T],
                              start=True, stop=True).then_inc(s.scores, 1)

            scores(0)
            for h in range(HEADS):
                if h + 1 < HEADS:
                    scores(h + 1)
                pe.wait_ge(s.weighted, TT * (h + 1))
                if h >= 1:
                    pe.wait_ge(s.normed, h)
                for c in range(2):
                    for j in range(TT):
                        mm = pe.matmul(o_bank[c][:, j * P:T], vals[:, j, h * DV + c * P:h * DV + (c + 1) * P],
                                       probs[:, h % 2, j, j * P:T], start=(j == 0), stop=(j == TT - 1))
                mm.then_inc(s.out_ready, 1)
                pe.wait_ge(s.squares, 2 * (h + 1))
                if h >= 1:
                    pe.wait_ge(s.root, h)
                for c in range(2):
                    mm = pe.matmul(ss_bank[:, :], m.ones, squares[:, c, :], start=(c == 0), stop=(c == 1))
                mm.then_inc(s.total, 1)

        @block.scalar
        def _(act):
            for h in range(HEADS):
                head_norm_act(m, act, o_bank, ss_bank, squares, std, h, s)

        @block.vector
        def _(dve):
            chain = lambda instruction: m.chain(dve, instruction)
            dve.wait_ge(s.decay, 16)

            def weigh(h):
                if h >= 2:
                    dve.wait_ge(s.out_ready, h - 1)
                for j in range(TT):
                    dve.wait_ge(s.scores, TT * h + j + 1)
                    dve.tensor_tensor(probs[:, h % 2, j, j * P:T], score_bank[j][:, 0:T - j * P],
                                      decay[:, h, 0:T - j * P], ALU.mult).then_inc(s.weighted, 1)

            weigh(0)
            for h in range(HEADS):
                if h + 1 < HEADS:
                    weigh(h + 1)
                dve.wait_ge(s.root, h + 1)
                chain(dve.reciprocal(std[:, :], std[:, :]))
                for c in range(2):
                    last = dve.tensor_tensor(roT[:, 2 * h + c, :], o_bank[c][:, :], std[:, :], ALU.mult)
                last.then_inc(s.normed, 1)


def stage_linear(nc, m, name, jobs):
    m.begin(jobs[0][0])
    gates = {"times_silu": ACT.Silu, "times_sigmoid": ACT.Sigmoid, "add_sigmoid_times": ACT.Sigmoid}
    with ExitStack() as own:
        gate = own.enter_context(nc.sbuf_tensor(name + "_gate", [P, 2, T], F32))
        gate_ready, gate_used, g0 = m.gate_ready, m.gate_used, m.gates
        block = own.enter_context(nc.Block(no_gpsimd_drain=True))
        tiles = [(job, j) for job in jobs for j in range(4)]

        @block.sync
        def _(sp):
            load_slabs(m, sp, min(jobs[-1][0] + 1 + RING, S_END))

        @block.tensor
        def _(pe):
            for s, acts, before, _, _ in jobs:
                if before:
                    m.wait_emptied(pe, 4 * before)
                pe_features(m, pe, s, acts)

        @block.scalar
        def _(act):
            g = 0
            for (s, _, _, kind, _), j in tiles:
                if kind in gates:
                    m.wait_product(act, s, j)
                    if g >= 2:
                        act.wait_ge(gate_used, g0 + g - 1)
                    act.activation(gate[:, g % 2, :], m.bank[j][:, :], gates[kind]).then_inc(gate_ready, 1)
                    g += 1

        @block.vector
        def _(dve):
            chain = lambda instruction: m.chain(dve, instruction)
            g = 0
            for (s, _, _, kind, ops), j in tiles:
                dst, at = ops[0], ops[1] + j
                out = dst[:, at, :]
                m.wait_product(dve, s, j)
                if kind in gates:
                    dve.wait_ge(gate_ready, g0 + g + 1)
                    gated = out if kind != "add_sigmoid_times" else ops[2][:, at, :]
                    chain(dve.tensor_tensor(gated, gated, gate[:, g % 2, :], ALU.mult))
                    dve.sem_inc(gate_used, 1)
                    if kind == "add_sigmoid_times":
                        chain(dve.tensor_tensor(out, out, gated, ALU.add))
                    g += 1
                elif kind == "copy":
                    chain(dve.tensor_copy(out, m.bank[j][:, :]))
                elif kind == "add":
                    chain(dve.tensor_tensor(out, m.bank[j][:, :], out, ALU.add))
                elif kind == "add_scaled":
                    chain(dve.scalar_tensor_tensor(out=out, in0=m.bank[j][:, :], scalar=ops[2][:, at:at + 1],
                                                   in1=out, op0=ALU.mult, op1=ALU.add))
                dve.sem_inc(m.emptied, 1)
    m.gates += sum(4 for job in jobs if job[3] in gates)
    m.end(len(tiles))


def stage_diff(nc, m, qT, kT, vals, doT):
    units = [(h, t) for h in range(HEADS) for t in range(TT)]
    with ExitStack() as own:
        sb = lambda name, shape: own.enter_context(nc.sbuf_tensor(name, shape, F32))
        p = sb("diff_p", [P, 2, 2, T])
        aT = sb("diff_aT", [P, TT, T])
        st = sb("diff_st", [P, 2, 8])
        squares = sb("diff_sq", [P, 2, T])
        std = sb("diff_std", [P, T])
        s = Names()
        (s.scores, s.maxed, s.probs, s.mixed, s.turned, s.turned_sb, s.out_ready, s.squares, s.total, s.root,
         s.normed) = (m.sem(f"diff_{x}") for x in ("scores", "maxed", "probs", "mixed", "turned", "turned_sb", "out",
                                                    "squares", "total", "root", "normed"))
        block = own.enter_context(nc.Block(no_gpsimd_drain=True))
        s_bank = lambda u, c: m.bank[2 * (u % 2) + c]
        t_bank, ss_bank = m.bank[4], m.bank[5]
        o_bank = [m.bank[6], m.bank[7]]

        @block.tensor
        def _(pe):
            def scores(u):
                h, t = units[u]
                if u >= 2:
                    pe.wait_ge(s.probs, 2 * (u - 1))
                for c in range(2):
                    mm = pe.matmul(s_bank(u, c)[:, 0:(t + 1) * P], qT[:, 2 * h + c, t * P:(t + 1) * P],
                                   kT[:, 2 * h + c, 0:(t + 1) * P], start=True, stop=True)
                mm.then_inc(s.scores, 1)

            def turn(u):
                h, t = units[u]
                pe.wait_ge(s.mixed, u + 1)
                if u >= 1:
                    pe.wait_ge(s.turned_sb, u)
                for j in range(t + 1):
                    mm = pe.transpose(t_bank[:, j * P:(j + 1) * P], p[:, u % 2, 0, j * P:(j + 1) * P], m.ident)
                mm.then_inc(s.turned, 1)

            def output(h):
                pe.wait_ge(s.turned_sb, TT * (h + 1))
                if h >= 1:
                    pe.wait_ge(s.normed, h)
                for c in range(2):
                    for j in range(TT):
                        mm = pe.matmul(o_bank[c][:, j * P:T], vals[:, j, h * DV + c * P:h * DV + (c + 1) * P],
                                       aT[:, j, j * P:T], start=(j == 0), stop=(j == TT - 1))
                mm.then_inc(s.out_ready, 1)

            def total(h):
                pe.wait_ge(s.squares, 2 * (h + 1))
                if h >= 1:
                    pe.wait_ge(s.root, h)
                for c in range(2):
                    mm = pe.matmul(ss_bank[:, :], m.ones, squares[:, c, :], start=(c == 0), stop=(c == 1))
                mm.then_inc(s.total, 1)

            scores(0)
            for u, (h, t) in enumerate(units):
                if u + 1 < len(units):
                    scores(u + 1)
                if t == 0 and h >= 1:
                    output(h - 1)
                turn(u)
                if t == 1 and h >= 1:
                    total(h - 1)
            output(HEADS - 1)
            total(HEADS - 1)

        @block.scalar
        def _(act):
            def squares_of(h):
                act.wait_ge(s.out_ready, h + 1)
                if h >= 1:
                    act.wait_ge(s.total, h)
                for c in range(2):
                    act.activation(squares[:, c, :], o_bank[c][:, :], ACT.Square).then_inc(s.squares, 1)

            def root_of(h):
                act.wait_ge(s.total, h + 1)
                if h >= 1:
                    act.wait_ge(s.normed, h)
                act.activation(std[:, :], ss_bank[:, :], ACT.Sqrt, bias=m.eps[:, :], scale=1.0 / DV).then_inc(s.root, 1)

            for u, (h, t) in enumerate(units):
                act.wait_ge(s.maxed, u + 1)
                if u >= 2:
                    act.wait_ge(s.mixed, u - 1)
                for c in range(2):
                    act.activation(p[:, u % 2, c, 0:(t + 1) * P], s_bank(u, c)[:, 0:(t + 1) * P], ACT.Exp,
                                   bias=st[:, u % 2, 2 + c:3 + c], scale=ATT_SCALE,
                                   accum_out=st[:, u % 2, 4 + c:5 + c]).then_inc(s.probs, 1)
                act.wait_ge(s.turned, u + 1)
                if t == 0 and h >= 1:
                    act.wait_ge(s.out_ready, h)
                act.activation(aT[:, 0:t + 1, t * P:(t + 1) * P],
                               t_bank[:, 0:(t + 1) * P].rearrange("p (j q) -> p j q", q=P), ACT.Copy).then_inc(s.turned_sb, 1)
                if t == 0 and h >= 1:
                    squares_of(h - 1)
                if t == 2 and h >= 1:
                    root_of(h - 1)
            squares_of(HEADS - 1)
            root_of(HEADS - 1)

        @block.vector
        def _(dve):
            chain = lambda instruction: m.chain(dve, instruction)

            def normed(h):
                dve.wait_ge(s.root, h + 1)
                chain(dve.reciprocal(std[:, :], std[:, :]))
                for c in range(2):
                    last = dve.scalar_tensor_tensor(out=doT[:, 2 * h + c, :], in0=o_bank[c][:, :],
                                                    scalar=m.dn[:, c:c + 1], in1=std[:, :], op0=ALU.mult, op1=ALU.mult)
                last.then_inc(s.normed, 1)

            def softmax_max(u):
                h, t = units[u]
                dve.wait_ge(s.scores, u + 1)
                if u >= 2:
                    dve.wait_ge(s.probs, 2 * (u - 1))
                for c in range(2):
                    bank = s_bank(u, c)
                    link = dve.tensor_tensor(bank[:, t * P:(t + 1) * P], bank[:, t * P:(t + 1) * P], m.causal, ALU.add)
                    if c:
                        chain(link)
                for c in range(2):
                    link = dve.tensor_reduce(st[:, u % 2, c:c + 1], s_bank(u, c)[:, 0:(t + 1) * P], AX.X, ALU.max)
                    if c:
                        chain(link)
                dve.tensor_scalar(st[:, u % 2, 2:4], st[:, u % 2, 0:2], -ATT_SCALE, None, ALU.mult).then_inc(s.maxed, 1)

            softmax_max(0)
            for u, (h, t) in enumerate(units):
                if u + 1 < len(units):
                    softmax_max(u + 1)
                w = (t + 1) * P
                dve.wait_ge(s.probs, 2 * (u + 1))
                chain(dve.reciprocal(st[:, u % 2, 6:8], st[:, u % 2, 4:6]))
                mixed = p[:, u % 2, 0, 0:w]
                dve.tensor_scalar(mixed, mixed, st[:, u % 2, 6:7], None, ALU.mult)
                chain(dve.tensor_scalar(st[:, u % 2, 7:8], st[:, u % 2, 7:8], m.neg_lam[:, :], None, ALU.mult))
                dve.scalar_tensor_tensor(out=mixed, in0=p[:, u % 2, 1, 0:w], scalar=st[:, u % 2, 7:8], in1=mixed,
                                         op0=ALU.mult, op1=ALU.add).then_inc(s.mixed, 1)
                if t == 3 and h >= 1:
                    normed(h - 1)
            normed(HEADS - 1)


def stage_route(nc, m, hT):
    E = EXPERTS
    with ExitStack() as own:
        sb = lambda name, shape, dt=F32: own.enter_context(nc.sbuf_tensor("rt_" + name, shape, dt))
        w_r = sb("w", [P, DC, 36])
        b_r = sb("b", [P, 36])
        logits = sb("logits", [P, TT, 36])
        group = sb("group", [P, TT, 8])
        top = sb("top", [P, TT, 8])
        top_e = sb("top_e", [P, TT, 8])
        where = sb("where", [P, TT, 8], U32)
        where_e = sb("where_e", [P, TT, 8], U32)
        gidx = sb("gidx", [P, TT])
        gexp = sb("gexp", [P, TT, GROUPS])
        gsum = sb("gsum", [P, TT])
        gmask = sb("gmask", [P, TT, GROUPS])
        e_in = sb("e_in", [P, TT, E])
        picked = sb("picked", [P, 2, TT])
        hot = sb("hot", [P, 2, TT, E])
        both = sb("both", [P, TT, E])
        rank = sb("rank", [P, TT, E])
        count = sb("count", [P, E])
        over = sb("over", [P, E])
        scan = sb("scan", [P, 2, E])
        tmp = sb("tmp", [P, TT, E])
        r = sb("r", [P, 2, TT])
        q = sb("q", [P, 2, TT])
        ov = sb("ov", [P, 2, TT])
        one = sb("one", [P, 2, TT])
        dest = sb("dest", [P, 2, TT])
        dest_t = sb("dest_t", [P, 2, TT], U32)
        ids = sb("ids", [P, TT], I32)
        zeros = sb("zeros", [P, BLOCKS], I32)
        whose = sb("whose", [P, 2, 8])
        whose_t = sb("whose_t", [P, 8, E])
        rows = sb("rows", [P, 2, D])
        blank = sb("blank", [P, D])

        loads, lg, bias_done, gx_ready, gx_done, hot_ready, ranked, dest_ready, zeroed, scattered, table = (
            m.sem(f"rt_{x}") for x in ("loads", "lg", "bias", "gx_ready", "gx_done", "hot", "ranked", "dest", "zeroed",
                                       "scattered", "table"))
        turned, rows_ready = m.sem("rt_turned"), m.sem("rt_rows")
        rows_out = [m.sem(f"rt_rows_out{i}") for i in range(2)]
        block = own.enter_context(nc.Block(no_gpsimd_drain=True))
        d = m.dram
        iota = m.const[:, C_IOTA:C_IOTA + P]

        @block.sync
        def _(sp):
            sp.dma_start(w_r[:, :, :], d.w_router).then_inc(loads, 16)
            sp.dma_start(b_r[:, :], d.b_router.to_broadcast([P, 36])).then_inc(loads, 16)
            for t in range(TT):
                sp.wait_ge(rows_ready, 2 * (t + 1))
                sp.dma_start(d.h_rows[t * P:(t + 1) * P, :], rows[:, t % 2, :]).then_inc(rows_out[t % 2], 16)
            for i in range(2):
                sp.wait_ge(rows_out[i], 16 * TT // 2)

        @block.tensor
        def _(pe):
            pe.wait_ge(loads, 32)
            for t in range(TT):
                for k in range(DC):
                    mm = pe.matmul(m.bank[0][:, t * 36:t * 36 + 36], hT[:, k, t * P:(t + 1) * P], w_r[:, k, :],
                                   start=(k == 0), stop=(k == DC - 1))
            mm.then_inc(lg, 1)
            for t in range(TT):
                if t >= 1:
                    pe.wait_ge(rows_ready, 2 * t)
                for k in range(DC):
                    mm = pe.transpose(m.bank[4 + k // 4][:, (k % 4) * P:(k % 4 + 1) * P], hT[:, k, t * P:(t + 1) * P],
                                      m.ident)
                    if k % 4 == 3:
                        mm.then_inc(turned, 1)
            pe.wait_ge(hot_ready, 1)
            for t in range(TT):
                for u in range(t + 1):
                    mm = pe.matmul(m.bank[1][:, t * E:(t + 1) * E], m.before if u == t else m.ones, both[:, u, :],
                                   start=(u == 0), stop=(u == t))
            for u in range(TT):
                mm = pe.matmul(m.bank[2][:, 0:E], m.ones, both[:, u, :], start=(u == 0), stop=(u == TT - 1))
            mm.then_inc(ranked, 1)

        @block.scalar
        def _(act):
            for t in range(TT):
                if t >= 2:
                    act.wait_ge(rows_out[t % 2], 16 * (t // 2))
                for i in range(2):
                    act.wait_ge(turned, 2 * t + i + 1)
                    act.activation(rows[:, t % 2, i * 512:(i + 1) * 512], m.bank[4 + i][:, :], ACT.Copy).then_inc(rows_ready, 1)
            act.wait_ge(gx_ready, 1)
            act.activation(gexp[:, :, :], gexp[:, :, :], ACT.Exp).then_inc(gx_done, 1)
            act.activation(m.pair_w[:, 1, :], m.pair_w[:, 1, :], ACT.Exp).then_inc(gx_done, 1)

        @block.vector
        def _(dve):
            chain = lambda instruction: m.chain(dve, instruction)
            chain(dve.memset(group[:, :, :], LOWEST))
            dve.wait_ge(lg, 1)
            dve.wait_ge(loads, 32)
            chain(dve.tensor_tensor(logits[:, :, :], m.bank[0][:, 0:4 * 36].rearrange("p (t e) -> p t e", e=36),
                                    bcast(b_r[:, :], 1, TT), ALU.add))
            chain(dve.tensor_copy(group[:, :, 0:GROUPS], logits[:, :, 0:GROUPS]))
            for t in range(TT):
                last = dve.max(out=top[:, t, :], in_=group[:, t, :])
            chain(last)
            for t in range(TT):
                last = dve.max_index(where[:, t, :], top[:, t, :], group[:, t, :])
            chain(last)
            chain(dve.tensor_copy(gidx[:, :], where[:, :, 0]))
            chain(dve.tensor_tensor(gmask[:, :, :], bcast(iota[:, 0:GROUPS], 1, TT), bcast(gidx[:, :], 2, GROUPS), ALU.is_equal))
            chain(dve.tensor_scalar(gmask[:, :, :], gmask[:, :, :], 1.0, 1.0e30, ALU.subtract, ALU.mult))
            for t in range(TT):
                last = dve.tensor_tensor(e_in[:, t, :].rearrange("p (g e) -> p g e", g=GROUPS),
                                         logits[:, t, GROUPS:36].rearrange("p (g e) -> p g e", g=GROUPS),
                                         bcast(gmask[:, t, :], 2, E // GROUPS), ALU.add)
            chain(last)
            for t in range(TT):
                last = dve.max(out=top_e[:, t, :], in_=e_in[:, t, :])
            chain(last)
            for t in range(TT):
                last = dve.max_index(where_e[:, t, :], top_e[:, t, :], e_in[:, t, :])
            chain(last)
            chain(dve.tensor_copy(picked[:, :, :], where_e[:, :, 0:2].rearrange("p t k -> p k t")))
            for k in range(2):
                last = dve.tensor_tensor(hot[:, k, :, :], bcast(iota[:, 0:E], 1, TT), bcast(picked[:, k, :], 2, E), ALU.is_equal)
            chain(last)
            chain(dve.tensor_tensor(both[:, :, :], hot[:, 0, :, :], hot[:, 1, :, :], ALU.add))
            dve.sem_inc(hot_ready, 1)
            chain(dve.tensor_tensor(gexp[:, :, :], logits[:, :, 0:GROUPS], bcast(top[:, :, 0], 2, GROUPS), ALU.subtract))
            chain(dve.tensor_tensor(m.pair_w[:, 1, :], top_e[:, :, 1], top_e[:, :, 0], ALU.subtract))
            dve.sem_inc(gx_ready, 1)
            dve.wait_ge(gx_done, 2)
            chain(dve.tensor_reduce(gsum[:, :], gexp[:, :, :], AX.X, ALU.add))
            chain(dve.tensor_scalar(m.pair_w[:, 0, :], m.pair_w[:, 1, :], 1.0, None, ALU.add))
            chain(dve.tensor_tensor(gsum[:, :], gsum[:, :], m.pair_w[:, 0, :], ALU.mult))
            chain(dve.reciprocal(m.pair_w[:, 0, :], gsum[:, :]))
            chain(dve.tensor_tensor(m.pair_w[:, 1, :], m.pair_w[:, 1, :], m.pair_w[:, 0, :], ALU.mult))
            dve.wait_ge(ranked, 1)
            chain(dve.tensor_copy(rank[:, :, :], m.bank[1][:, 0:TT * E].rearrange("p (t e) -> p t e", e=E)))
            chain(dve.tensor_copy(count[:, :], m.bank[2][:, 0:E]))
            chain(dve.tensor_scalar(over[:, :], count[:, :], float(SLOTS), None, ALU.is_gt))
            for b in range(2, T // SLOTS):
                chain(dve.scalar_tensor_tensor(out=over[:, :], in0=count[:, :], scalar=float(SLOTS * b), in1=over[:, :],
                                               op0=ALU.is_gt, op1=ALU.add))
            chain(dve.tensor_copy(scan[:, 0, :], over[:, :]))
            a = 0
            step = 1
            while step < E:
                chain(dve.tensor_copy(scan[:, 1 - a, 0:step], scan[:, a, 0:step]))
                chain(dve.tensor_tensor(scan[:, 1 - a, step:E], scan[:, a, step:E], scan[:, a, 0:E - step], ALU.add))
                a = 1 - a
                step *= 2
            ends = scan[:, a, :]
            chain(dve.tensor_tensor(whose_t[:, :, :], bcast(ends, 1, 8), bcast(iota[:, 0:8], 2, E), ALU.is_le))
            chain(dve.tensor_reduce(whose[:, 0, :], whose_t[:, :, :], AX.X, ALU.add))
            chain(dve.tensor_copy(m.steer[:, 0:OVER], whose[:, 0, 0:OVER]))
            chain(dve.tensor_copy(m.steer[:, OVER:OVER + 1], ends[:, E - 1:E]))
            starts = scan[:, 1 - a, :]
            chain(dve.tensor_tensor(starts, ends, over[:, :], ALU.subtract))
            for k in range(2):
                chain(dve.tensor_tensor(tmp[:, :, :], rank[:, :, :], hot[:, k, :, :], ALU.mult))
                chain(dve.tensor_reduce(r[:, k, :], tmp[:, :, :], AX.X, ALU.add))
                chain(dve.tensor_tensor(tmp[:, :, :], bcast(starts, 1, TT), hot[:, k, :, :], ALU.mult))
                chain(dve.tensor_reduce(ov[:, k, :], tmp[:, :, :], AX.X, ALU.add))
            chain(dve.tensor_scalar(q[:, :, :], r[:, :, :], float(SLOTS), None, ALU.is_ge))
            chain(dve.tensor_scalar(ov[:, :, :], ov[:, :, :], float(E - 1), None, ALU.add))
            chain(dve.tensor_tensor(ov[:, :, :], ov[:, :, :], picked[:, :, :], ALU.subtract))
            chain(dve.tensor_tensor(ov[:, :, :], ov[:, :, :], q[:, :, :], ALU.mult))
            for b in range(2, T // SLOTS):
                chain(dve.scalar_tensor_tensor(out=q[:, :, :], in0=r[:, :, :], scalar=float(SLOTS * b), in1=q[:, :, :],
                                               op0=ALU.is_ge, op1=ALU.add))
            chain(dve.tensor_tensor(ov[:, :, :], ov[:, :, :], picked[:, :, :], ALU.add))
            chain(dve.tensor_tensor(ov[:, :, :], ov[:, :, :], q[:, :, :], ALU.add))
            chain(dve.scalar_tensor_tensor(out=one[:, :, :], in0=q[:, :, :], scalar=-float(SLOTS), in1=r[:, :, :],
                                           op0=ALU.mult, op1=ALU.add))
            chain(dve.scalar_tensor_tensor(out=dest[:, :, :], in0=ov[:, :, :], scalar=float(SLOTS), in1=one[:, :, :],
                                           op0=ALU.mult, op1=ALU.add))
            chain(dve.tensor_copy(m.pair_row[:, :, :], dest[:, :, :]))
            chain(dve.scalar_tensor_tensor(out=dest[:, :, :], in0=one[:, :, :], scalar=float(BLOCKS), in1=ov[:, :, :],
                                           op0=ALU.mult, op1=ALU.add))
            chain(dve.tensor_copy(dest_t[:, :, :], dest[:, :, :]))
            chain(dve.tensor_copy(ids[:, :], m.const[:, C_TOKEN:C_TOKEN + TT]))
            dve.sem_inc(dest_ready, 1)

        @block.gpsimd
        def _(pool):
            own_wait = m.sem("rt_zero_sb")
            pool.memset(zeros[:, :], 0).then_inc(own_wait, 1)
            pool.wait_ge(own_wait, 1)
            pool.dma_start(d.slot_token.rearrange("(p b) o -> p (b o)", b=BLOCKS), zeros[:, :]).then_inc(zeroed, 16)
            pool.memset(blank[:, :], 0.0).then_inc(own_wait, 1)
            pool.wait_ge(own_wait, 2)
            for b in range(EXPERTS, BLOCKS):
                pool.dma_start(d.y_rows[b * SLOTS:(b + 1) * SLOTS, :], blank[:, :]).then_inc(zeroed, 16)
            pool.wait_ge(zeroed, 16 * (1 + BLOCKS - EXPERTS))
            pool.wait_ge(dest_ready, 1)
            for k in range(2):
                for t in range(TT):
                    pool.indirect_dma_start(
                        out=d.slot_token, out_offset=bass.IndirectOffsetOnAxis(ap=dest_t[:, k, t:t + 1], axis=0),
                        in_=ids[:, t:t + 1], in_offset=None).then_inc(scattered, 16)
            pool.wait_ge(scattered, 16 * 2 * TT)
            pool.dma_start(m.tokens[:, :], d.slot_token.rearrange("(p b) o -> p (b o)", b=BLOCKS)).then_inc(table, 16)
            pool.wait_ge(table, 16)


def stage_experts(nc, m):
    F = 512
    turns = EXPERTS // 4
    with ExitStack() as own:
        sb = lambda name, shape: own.enter_context(nc.sbuf_tensor("moe_" + name, shape, F32))
        x = sb("x", [P, 2, D])
        xT = sb("xT", [P, 2, D])
        gate = sb("gate", [P, F])
        hid = sb("hid", [P, F])
        hidT = sb("hidT", [P, F])
        y = sb("y", [P, 2, D])
        x_in = [m.sem(f"moe_x{i}") for i in range(2)]
        y_out = [m.sem(f"moe_y{i}") for i in range(2)]
        xt_mm, xt_sb, gated, hid_ready, hidt_mm, hidt_sb, y_sb = (
            m.sem(f"moe_{v}") for v in ("xt_mm", "xt_sb", "gated", "hid", "hidt_mm", "hidt_sb", "y_sb"))
        block = own.enter_context(nc.Block(no_gpsimd_drain=True))
        d = m.dram
        FIRST = 4 * S_MOE

        @block.sync
        def _(sp):
            load_slabs(m, sp, S_IN2 + RING)

        @block.gpsimd
        def _(pool):
            def store(e):
                pool.wait_ge(y_sb, 2 * e + 2)
                pool.dma_start(d.y_rows[e * SLOTS:(e + 1) * SLOTS, :], y[:, e % 2, :]).then_inc(y_out[e % 2], 16)

            for e in range(EXPERTS):
                if e >= 2:
                    pool.wait_ge(xt_mm, 2 * (e - 1))
                pool.indirect_dma_start(
                    out=x[:, e % 2, :], out_offset=None, in_=d.h_rows,
                    in_offset=bass.IndirectOffsetOnAxis(ap=m.tokens[:, e:e + 1], axis=0)).then_inc(x_in[e % 2], 16)
                if e >= 2:
                    store(e - 2)
            store(EXPERTS - 2)
            store(EXPERTS - 1)
            for i in range(2):
                pool.wait_ge(y_out[i], 16 * EXPERTS // 2)

        def expert(pe, e, i, slot):
            def slab(w):
                return (S_MOE + 3 * i + w) % RING

            def arrived(w):
                head = (S_MOE + 3 * i + w) // RING
                pe.wait_ge(m.slab_loaded[slab(w)], turn_slabs(e, i) + 16 * (head + 1))

            arrived(0)
            pe.wait_ge(xt_sb, 2 * e + 2)
            for w in range(2):
                if w == 1:
                    arrived(1)
                for k in range(DC):
                    mm = pe.matmul(m.bank[w][:, :], xT[:, slot, k * P:(k + 1) * P],
                                   m.ring[:, slab(w), k * F:(k + 1) * F], start=(k == 0), stop=(k == DC - 1))
                mm.then_inc(m.products, 4)

        def turn_slabs(e, i):
            return 16 * (3 * (e - i) // RING) if isinstance(e, int) else (e - i) * 12

        @block.tensor
        def _(pe):
            def turn_x(e, slot):
                pe.wait_ge(x_in[slot], 8 * e + 16 - 8 * slot)
                if not isinstance(e, int) or e >= 1:
                    pe.wait_ge(xt_sb, 2 * e)
                for k in range(DC):
                    mm = pe.transpose(m.bank[4 + k // 4][:, (k % 4) * P:(k % 4 + 1) * P],
                                      x[:, slot, k * P:(k + 1) * P], m.ident)
                    if k % 4 == 3:
                        mm.then_inc(xt_mm, 1)

            def second(e, i):
                pe.wait_ge(hid_ready, e + 1)
                for k in range(4):
                    mm = pe.transpose(m.bank[6][:, k * P:(k + 1) * P], hid[:, k * P:(k + 1) * P], m.ident)
                mm.then_inc(hidt_mm, 1)
                w, s = 2, (S_MOE + 3 * i + 2)
                pe.wait_ge(m.slab_loaded[s % RING], turn_slabs(e, i) + 16 * (s // RING + 1))
                pe.wait_ge(hidt_sb, e + 1)
                if not isinstance(e, int) or e >= 1:
                    pe.wait_ge(y_sb, 2 * e)
                for half in range(2):
                    for k in range(4):
                        mm = pe.matmul(m.bank[2 + half][:, :], hidT[:, k * P:(k + 1) * P],
                                       m.ring[:, s % RING, k * D + half * F:k * D + (half + 1) * F],
                                       start=(k == 0), stop=(k == 3))
                    mm.then_inc(m.products, 2)

            turn_x(0, 0)
            for i in range(4):
                expert(pe, i, i, i % 2)
                turn_x(i + 1, (i + 1) % 2)
                second(i, i)
            with pe.Fori(1, turns - 1) as turn:
                for i in range(4):
                    e = turn * 4 + i
                    expert(pe, e, i, i % 2)
                    turn_x(e + 1, (i + 1) % 2)
                    second(e, i)
            for i in range(4):
                e = 4 * (turns - 1) + i
                expert(pe, e, i, i % 2)
                if e + 1 < EXPERTS:
                    turn_x(e + 1, (i + 1) % 2)
                second(e, i)

        @block.scalar
        def _(act):
            def turned(e, slot, guarded):
                for i in range(2):
                    act.wait_ge(xt_mm, 2 * e + i + 1)
                    if i == 0 and guarded:
                        act.wait_ge(m.products, 12 * e + (FIRST - 16))
                    act.activation(xT[:, slot, i * F:(i + 1) * F], m.bank[4 + i][:, :], ACT.Copy).then_inc(xt_sb, 1)

            def middle(e, guarded):
                act.wait_ge(m.products, 12 * e + (FIRST + 4))
                if guarded:
                    act.wait_ge(hid_ready, e)
                act.activation(gate[:, :], m.bank[0][:, :], ACT.Silu).then_inc(gated, 1)

            def hidden(e):
                act.wait_ge(hidt_mm, e + 1)
                act.activation(hidT[:, :], m.bank[6][:, :], ACT.Copy).then_inc(hidt_sb, 1)

            turned(0, 0, False)
            for i in range(4):
                middle(i, i >= 1)
                turned(i + 1, (i + 1) % 2, i >= 1)
                hidden(i)
            with act.Fori(1, turns - 1) as turn:
                for i in range(4):
                    e = turn * 4 + i
                    middle(e, True)
                    turned(e + 1, (i + 1) % 2, True)
                    hidden(e)
            for i in range(4):
                e = 4 * (turns - 1) + i
                middle(e, True)
                if e + 1 < EXPERTS:
                    turned(e + 1, (i + 1) % 2, True)
                hidden(e)

        @block.vector
        def _(dve):
            def one(e, slot, guarded, guard_y):
                dve.wait_ge(gated, e + 1)
                dve.wait_ge(m.products, 12 * e + (FIRST + 8))
                if guarded:
                    dve.wait_ge(hidt_mm, e)
                dve.tensor_tensor(hid[:, :], gate[:, :], m.bank[1][:, :], ALU.mult).then_inc(hid_ready, 1)
                if guard_y:
                    dve.wait_ge(y_out[slot], 8 * e - 8 * slot)
                for half in range(2):
                    dve.wait_ge(m.products, 12 * e + (FIRST + 10 + 2 * half))
                    dve.tensor_copy(y[:, slot, half * F:(half + 1) * F], m.bank[2 + half][:, :]).then_inc(y_sb, 1)

            one(0, 0, False, False)
            one(1, 1, True, False)
            one(2, 0, True, True)
            one(3, 1, True, True)
            with dve.Fori(1, turns) as turn:
                for i in range(4):
                    one(turn * 4 + i, i % 2, True, True)


def stage_combine(nc, m, xT):
    with ExitStack() as own:
        rows = own.enter_context(nc.sbuf_tensor("cmb_rows", [P, 2, 2, D], F32))
        arrived = [m.sem(f"cmb_in{i}") for i in range(2)]
        mixed, turned, added = (m.sem(f"cmb_{v}") for v in ("mixed", "turned", "added"))
        block = own.enter_context(nc.Block(no_gpsimd_drain=True))

        @block.gpsimd
        def _(pool):
            for t in range(TT):
                if t >= 2:
                    pool.wait_ge(turned, 2 * (t - 1))
                for k in range(2):
                    pool.indirect_dma_start(
                        out=rows[:, t % 2, k, :], out_offset=None, in_=m.dram.y_rows,
                        in_offset=bass.IndirectOffsetOnAxis(ap=m.pair_row[:, k, t:t + 1], axis=0)
                    ).then_inc(arrived[t % 2], 16)

        @block.vector
        def _(dve):
            chain = lambda instruction: m.chain(dve, instruction)

            def mix(t):
                dve.wait_ge(arrived[t % 2], 32 * (t // 2 + 1))
                y0, y1 = rows[:, t % 2, 0, :], rows[:, t % 2, 1, :]
                chain(dve.tensor_scalar(y0, y0, m.pair_w[:, 0, t:t + 1], None, ALU.mult))
                dve.scalar_tensor_tensor(out=y0, in0=y1, scalar=m.pair_w[:, 1, t:t + 1], in1=y0,
                                         op0=ALU.mult, op1=ALU.add).then_inc(mixed, 1)

            mix(0)
            for t in range(TT):
                if t + 1 < TT:
                    mix(t + 1)
                for k in range(DC):
                    dve.wait_ge(turned, 2 * t + k // 4 + 1)
                    out = xT[:, k, t * P:(t + 1) * P]
                    dve.scalar_tensor_tensor(out=out, in0=m.bank[2 * (t % 2) + k // 4][:, (k % 4) * P:(k % 4 + 1) * P],
                                             scalar=m.mod[:, 40 + k:41 + k], in1=out, op0=ALU.mult,
                                             op1=ALU.add).then_inc(added, 1)

        @block.tensor
        def _(pe):
            for t in range(TT):
                pe.wait_ge(mixed, t + 1)
                if t >= 2:
                    pe.wait_ge(added, DC * (t - 1))
                for k in range(DC):
                    mm = pe.transpose(m.bank[2 * (t % 2) + k // 4][:, (k % 4) * P:(k % 4 + 1) * P],
                                      rows[:, t % 2, 0, k * P:(k + 1) * P], m.ident)
                    if k % 4 == 3:
                        mm.then_inc(turned, 1)


def stage_in2(nc, m, hT, qT, kT, vals, poolT, d_pool):
    m.begin(S_IN2)
    with ExitStack() as own:
        sb = lambda name, shape: own.enter_context(nc.sbuf_tensor("in2_" + name, shape, F32))
        squares = sb("sq", [P, 2, T])
        std = sb("std", [P, 2, T])
        run = sb("run", [P, 2, T])
        tail = sb("tail", [P, 16])
        sq_ready, total, root, normed = (m.sem(f"in2_{v}") for v in ("sq", "total", "root", "normed"))
        block = own.enter_context(nc.Block(no_gpsimd_drain=True))
        heads = [(S_IN2, j) for j in range(4)] + [(S_IN2 + 2, 0)]

        @block.sync
        def _(sp):
            load_slabs(m, sp, S_IN2 + 3 + RING)

        @block.tensor
        def _(pe):
            def norm(n):
                pe.wait_ge(sq_ready, n + 1)
                if n >= 2:
                    pe.wait_ge(root, n - 1)
                pe.matmul(m.bank[4 + n % 2][:, :], m.halves, squares[:, n % 2, :], start=True, stop=True).then_inc(total, 1)

            pe_features(m, pe, S_IN2, hT)
            for n in range(4):
                norm(n)
            pe_features(m, pe, S_IN2 + 1, hT)
            pe_features(m, pe, S_IN2 + 2, hT, tiles=1)
            norm(4)
            slot = (S_IN2 + 2) % RING
            m.wait_bank(pe, S_IN2 + 2, 1)
            for t in range(TT):
                for k in range(DC):
                    mm = pe.matmul(m.bank[1][:, t * P:(t + 1) * P], hT[:, k, t * P:(t + 1) * P],
                                   m.ring[:, slot, D + k * P:D + (k + 1) * P], start=(k == 0), stop=(k == DC - 1))
            mm.then_inc(m.products, 3)

        @block.scalar
        def _(act):
            for n, (s, j) in enumerate(heads):
                m.wait_product(act, s, j)
                if n >= 2:
                    act.wait_ge(total, n - 1)
                act.activation(squares[:, n % 2, :], m.bank[j][:, :], ACT.Square).then_inc(sq_ready, 1)
                act.wait_ge(total, n + 1)
                if n >= 2:
                    act.wait_ge(normed, n - 1)
                act.activation(std[:, n % 2, :], m.bank[4 + n % 2][:, :], ACT.Sqrt, bias=m.eps[:, :],
                               scale=1.0 / HD).then_inc(root, 1)
            act.wait_ge(m.products, 4 * (S_IN2 + 3))
            act.activation(vals[:, :, :], m.bank[1][:, :].rearrange("p (t n) -> p t n", n=P), ACT.Copy)

        @block.vector
        def _(dve):
            chain = lambda instruction: m.chain(dve, instruction)

            def head(n, dst, gain):
                s, j = heads[n]
                dve.wait_ge(root, n + 1)
                chain(dve.reciprocal(std[:, n % 2, :], std[:, n % 2, :]))
                chain(dve.scalar_tensor_tensor(out=dst, in0=m.bank[j][:, :], scalar=gain, in1=std[:, n % 2, :],
                                               op0=ALU.mult, op1=ALU.mult))
                dve.sem_inc(normed, 1)
                dve.sem_inc(m.emptied, 1)

            chain(dve.tensor_scalar(m.small[:, 0:1], m.small[:, 0:1], float(HD) ** -0.5, None, ALU.mult))
            for n in range(4):
                head(n, qT[:, n, :], m.small[:, 0:1])
            for g in range(4):
                m.wait_product(dve, S_IN2 + 1, g)
                chain(dve.tensor_copy(poolT[:, g, :], m.bank[g][:, :]))
                dve.sem_inc(m.emptied, 1)
            head(4, kT[:, :], m.small[:, 1:2])
            for g in range(4):
                window = 2 << g
                src = poolT[:, g, :]
                step = 1
                a = 0
                while step < window:
                    chain(dve.tensor_copy(run[:, a, 0:step], src[:, 0:step]))
                    chain(dve.tensor_tensor(run[:, a, step:T], src[:, step:T], src[:, 0:T - step], ALU.add))
                    src = run[:, a, :]
                    a = 1 - a
                    step *= 2
                chain(dve.scalar_tensor_tensor(out=d_pool[:, g, :], in0=src, scalar=1.0 / window, in1=poolT[:, g, :],
                                               op0=ALU.mult, op1=ALU.subtract))
                chain(dve.tensor_tensor(tail[:, :], src[:, 0:16], m.const[:, C_COUNT + 16 * g:C_COUNT + 16 * (g + 1)], ALU.mult))
                chain(dve.tensor_tensor(d_pool[:, g, 0:16], tail[:, :], poolT[:, g, 0:16], ALU.subtract))
    m.end(9)


def stage_window(nc, m, qT, kT, vals, d_pool, cat):
    with ExitStack() as own:
        sb = lambda name, shape: own.enter_context(nc.sbuf_tensor("swa_" + name, shape, F32))
        H = SWA_HEADS
        bias = sb("bias", [P, H, BAND])
        sc = sb("sc", [P, H, BAND])
        pT = sb("pT", [P, 2 * H, P])
        mx = sb("mx", [P, H])
        es = sb("es", [P, H])
        den = sb("den", [P, H])
        pool_w = sb("pool_w", [P, 4, P])
        loads, scores, shifted, exped, probs, turned, turned_sb, out_ready, out_sb, sinks_e, pooled, scored = (
            m.sem(f"swa_{v}") for v in ("loads", "scores", "shifted", "exped", "probs", "turned", "turned_sb", "out",
                                        "out_sb", "sinks", "pooled", "scored"))
        block = own.enter_context(nc.Block(no_gpsimd_drain=True))
        d = m.dram

        @block.sync
        def _(sp):
            for h in range(H):
                sp.dma_start(bias[:, h, :], d.bias_band[h]).then_inc(loads, 16)
            sp.dma_start(pool_w[:, :, :], d.pool_w).then_inc(loads, 16)
            sp.wait_ge(loads, 16 * (H + 1))

        def first_key(t):
            return P if t == 0 else 0

        @block.tensor
        def _(pe):
            pe.wait_ge(loads, 16 * (H + 1))
            for g in range(4):
                mm = pe.matmul(m.bank[g][:, :], pool_w[:, g, :], d_pool[:, g, :], start=True, stop=True)
            mm.then_inc(pooled, 1)
            pe.wait_ge(out_sb, 1)
            for t in range(TT):
                lo = first_key(t)
                if t >= 1:
                    pe.wait_ge(scored, t)
                    pe.wait_ge(out_sb, t + 1)
                for h in range(H):
                    r = HD * (h // 4)
                    mm = pe.matmul(m.bank[h // 2][:, (h % 2) * BAND + lo:(h % 2 + 1) * BAND],
                                   qT[r:r + HD, h % 4, t * P:(t + 1) * P],
                                   kT[r:r + HD, (t - 1) * P + lo:(t + 1) * P], start=True, stop=True)
                mm.then_inc(scores, 1)
                pe.wait_ge(probs, t + 1)
                if t >= 1:
                    pe.wait_ge(turned_sb, t)
                for h in range(H):
                    for b in range(lo // P, 2):
                        i = 2 * h + b
                        mm = pe.transpose(m.bank[4 + i // 4][:, (i % 4) * P:(i % 4 + 1) * P],
                                          sc[:, h, b * P:(b + 1) * P], m.ident)
                mm.then_inc(turned, 1)
                pe.wait_ge(turned_sb, t + 1)
                for h in range(H):
                    r = HD * (h // 4)
                    for b in range(lo // P, 2):
                        mm = pe.matmul(m.bank[0][r:r + HD, (h % 4) * P:(h % 4 + 1) * P],
                                       vals[:, t - 1 + b, r:r + HD], pT[:, 2 * h + b, :],
                                       start=(b == lo // P), stop=(b == 1))
                mm.then_inc(out_ready, 1)

        @block.scalar
        def _(act):
            for t in range(TT):
                lo = first_key(t)
                act.wait_ge(shifted, t + 1)
                act.activation(sc[:, :, lo:], sc[:, :, lo:], ACT.Exp).then_inc(exped, 1)
                act.activation(es[:, :], es[:, :], ACT.Exp).then_inc(exped, 1)
                act.wait_ge(turned, t + 1)
                if t >= 1:
                    act.wait_ge(out_ready, t)
                act.activation(pT[:, :, :].rearrange("p (h b) q -> p h b q", b=2)[:, :, lo // P:, :],
                               m.psum[:, 4:8, :].rearrange("p k (h b q) -> p (k h) b q", b=2, q=P)[:, :, lo // P:, :],
                               ACT.Copy).then_inc(turned_sb, 1)

        @block.vector
        def _(dve):
            chain = lambda instruction: m.chain(dve, instruction)
            dve.wait_ge(pooled, 1)
            for g in range(4):
                last = dve.tensor_scalar(cat[:, 4 + g, :], m.bank[g][:, :], m.small[:, 2 + g:3 + g], None, ALU.mult)
            last.then_inc(out_sb, 1)
            dve.wait_ge(loads, 16 * (H + 1))
            chain(dve.tensor_tensor(bias[:, :, :], bias[:, :, :],
                                    bcast(m.const[:, C_MASK:C_MASK + BAND], 1, H), ALU.add))
            for t in range(TT):
                lo = first_key(t)
                w = BAND - lo
                dve.wait_ge(scores, t + 1)
                if t >= 1:
                    dve.wait_ge(turned, t)
                chain(dve.tensor_tensor(sc[:, :, lo:],
                                        m.psum[:, 0:4, :].rearrange("p k (h j) -> p (k h) j", j=BAND)[:, :, lo:],
                                        bias[:, :, lo:], ALU.add))
                dve.sem_inc(scored, 1)
                chain(dve.tensor_reduce(mx[:, :], sc[:, :, lo:], AX.X, ALU.max))
                chain(dve.tensor_tensor(mx[:, :], mx[:, :], m.sinks[:, :], ALU.max))
                dve.tensor_tensor(sc[:, :, lo:], sc[:, :, lo:], bcast(mx[:, :], 2, w), ALU.subtract)
                dve.tensor_tensor(es[:, :], m.sinks[:, :], mx[:, :], ALU.subtract).then_inc(shifted, 1)
                dve.wait_ge(exped, 2 * (t + 1))
                chain(dve.tensor_reduce(den[:, :], sc[:, :, lo:], AX.X, ALU.add))
                chain(dve.tensor_tensor(den[:, :], den[:, :], es[:, :], ALU.add))
                chain(dve.reciprocal(den[:, :], den[:, :]))
                dve.tensor_tensor(sc[:, :, lo:], sc[:, :, lo:], bcast(den[:, :], 2, w), ALU.mult).then_inc(probs, 1)
                dve.wait_ge(out_ready, t + 1)
                dve.tensor_copy(cat[:, 0:4, t * P:(t + 1) * P],
                                m.bank[0][:, :].rearrange("p (h q) -> p h q", q=P)).then_inc(out_sb, 1)


def stage_peer_u(nc, m, hT):
    H, K = PH, TOPK
    HALF = PK // 8
    NB = 64
    with ExitStack() as own:
        sb = lambda name, shape, dt=F32: own.enter_context(nc.sbuf_tensor("pu_" + name, shape, dt))
        gl = sb("gl", [P, 2, 4, T])
        e_turned = sb("e_turned", [P, 3, T])
        iota = m.const[:, C_IOTA:C_IOTA + P]
        loads, scored, score_sb, picked, turned, turned_sb, act_ready, act_out = (
            m.sem(f"pu_{v}") for v in ("loads", "scored", "score_sb", "picked", "turned", "turned_sb", "act", "act_out"))
        gl_out = [m.sem(f"pu_gl{i}") for i in range(2)]
        d = m.dram
        first = 4 * S_U

        with ExitStack() as half:
            hb = lambda name, shape, dt=F32: half.enter_context(nc.sbuf_tensor("pk_" + name, shape, dt))
            qT = hb("q", [P, 2 * H, T])
            stage_linear(nc, m, "wq", [(S_WQ + i, hT, 0, "copy", (qT, 4 * i)) for i in range(4)])
            subkeys = hb("subkeys", [P, 2 * H, PK])
            sc = hb("sc", [P, 2 * H, PK])
            sc2 = hb("sc2", [P, 2 * H, PK])
            val = hb("val", [P, 2 * H, K])
            idx = hb("idx", [P, 2 * H, K], U32)
            idf = hb("idf", [P, 2 * H, K])
            best = hb("best", [P, H, K])
            pos = hb("pos", [P, H, K], U32)
            part = hb("part", [P, H, K], U32)
            partf = hb("partf", [P, 2, H, K])
            res = hb("res", [P, 3, H, K])
            gs = hb("gs", [P, H])
            exp_ready, exp_done = m.sem("pk_exp_ready"), m.sem("pk_exp_done")
            block = half.enter_context(nc.Block(no_gpsimd_drain=True))

            @block.sync
            def _(sp):
                sp.dma_start(subkeys[:, :, :], d.subkeys).then_inc(loads, 16)
                load_slabs(m, sp, S_U + HALF + RING)

            @block.tensor
            def _(pe):
                pe.wait_ge(loads, 16)

                def scores(t):
                    if t >= 1:
                        pe.wait_ge(score_sb, t)
                    for n in range(2 * H):
                        mm = pe.matmul(m.bank[2 + n // 4][:, (n % 4) * PK:(n % 4 + 1) * PK], qT[:, n, t * P:(t + 1) * P],
                                       subkeys[:, n, :], start=True, stop=True)
                    mm.then_inc(scored, 1)

                def turn(t):
                    pe.wait_ge(picked, t + 1)
                    if t >= 1:
                        pe.wait_ge(turned_sb, t)
                    for i in range(3):
                        mm = pe.transpose(m.bank[6][:, i * P:(i + 1) * P], res[:, i, :, :].rearrange("p h k -> p (h k)"), m.ident)
                    mm.then_inc(turned, 1)

                def u_slab(s, chunk):
                    wait_slab(m, pe, s)
                    for j in range(4):
                        if chunk + j >= 2:
                            pe.wait_ge(act_ready, chunk + j - 1)
                        for k in range(DC):
                            mm = pe.matmul(m.bank[j % 2][:, :], m.ring[:, s % RING, (j * DC + k) * P:(j * DC + k + 1) * P],
                                           hT[:, k, :], start=(k == 0), stop=(k == DC - 1))
                        mm.then_inc(m.products, 1)

                scores(0)
                for n in range(HALF):
                    u_slab(S_U + n, n * 4)
                    if n % 4 == 3 and n < HALF - 1 and n // 4 + 1 < TT:
                        turn(n // 4)
                        scores(n // 4 + 1)
                turn(TT - 1)

            def gelu_slab(act, n, slot, guarded):
                if guarded:
                    act.wait_ge(gl_out[slot], 8 * n - 8 * slot)
                for j in range(4):
                    act.wait_ge(m.products, 4 * n + (first + j + 1))
                    act.activation(gl[:, slot, j, :], m.bank[j % 2][:, :], ACT.Gelu).then_inc(act_ready, 1)
                act.wait_ge(act_ready, 4 * n + 4)
                dst = d.gelu[n] if isinstance(n, int) else d.gelu[bass.ds(n, 1)].rearrange("o p c t -> (o p) c t")
                act.dma_start(dst, gl[:, slot, :, :]).then_inc(gl_out[slot], 16)

            @block.scalar
            def _(act):
                for n in range(HALF):
                    if n % 4 == 0:
                        t = n // 4
                        act.wait_ge(scored, t + 1)
                        if t >= 1:
                            act.wait_ge(picked, t)
                        act.activation(sc[:, :, :], m.psum[:, 2:6, :].rearrange("p b (n k) -> p (b n) k", k=PK),
                                       ACT.Copy).then_inc(score_sb, 1)
                    gelu_slab(act, n, n % 2, n >= 2)
                    if n % 4 == 2:
                        t = n // 4
                        act.wait_ge(exp_ready, t + 1)
                        act.activation(best[:, :, :], best[:, :, :], ACT.Exp).then_inc(exp_done, 1)
                    if n % 4 == 3:
                        t = n // 4
                        act.wait_ge(turned, t + 1)
                        act.activation(e_turned[:, :, t * P:(t + 1) * P],
                                       m.bank[6][:, 0:3 * P].rearrange("p (i q) -> p i q", q=P), ACT.Copy).then_inc(turned_sb, 1)

            @block.vector
            def _(dve):
                chain = lambda instruction: m.chain(dve, instruction)

                def top16(n, source, spare, values, places):
                    for i in range(n):
                        last = dve.max(out=values[:, i, 0:8], in_=source(i))
                    chain(last)
                    for i in range(n):
                        dve.max_index(places[:, i, 0:8], values[:, i, 0:8], source(i))
                        last = dve.match_replace(out=spare(i), in_to_replace=values[:, i, 0:8], in_values=source(i),
                                                 imm_value=LOWEST)
                    chain(last)
                    for i in range(n):
                        last = dve.max(out=values[:, i, 8:16], in_=spare(i))
                    chain(last)
                    for i in range(n):
                        last = dve.max_index(places[:, i, 8:16], values[:, i, 8:16], spare(i))
                    chain(last)

                for t in range(TT):
                    dve.wait_ge(score_sb, t + 1)
                    top16(2 * H, lambda i: sc[:, i, :], lambda i: sc2[:, i, :], val, idx)
                    chain(dve.tensor_copy(idf[:, :, :], idx[:, :, :]))
                    cand = sc[:, :, :].rearrange("p (h a) k -> p h (a k)", a=2)
                    cand2 = sc2[:, :, :].rearrange("p (h a) k -> p h (a k)", a=2)
                    for h in range(H):
                        last = dve.tensor_tensor(cand[:, h, :].rearrange("p (i j) -> p i j", j=K),
                                                 bcast(val[:, 2 * h, :], 2, K), bcast(val[:, 2 * h + 1, :], 1, K), ALU.add)
                    chain(last)
                    top16(H, lambda i: cand[:, i, :], lambda i: cand2[:, i, :], best, pos)
                    chain(dve.tensor_scalar(part[:, :, :], pos[:, :, :], 4, None, ALU.logical_shift_right))
                    chain(dve.tensor_copy(partf[:, 0, :, :], part[:, :, :]))
                    chain(dve.tensor_scalar(part[:, :, :], pos[:, :, :], 15, None, ALU.bitwise_and))
                    chain(dve.tensor_copy(partf[:, 1, :, :], part[:, :, :]))
                    pick = sc[:, :, :].rearrange("p (h a) k -> p h (a k)", a=2)
                    for which in range(2):
                        for h in range(H):
                            last = dve.tensor_tensor(pick[:, h, :].rearrange("p (i j) -> p i j", j=K),
                                                     bcast(partf[:, which, h, :], 2, K), bcast(iota[:, 0:K], 1, K), ALU.is_equal)
                        chain(last)
                        for h in range(H):
                            one = pick[:, h, :].rearrange("p (i j) -> p i j", j=K)
                            last = dve.tensor_tensor(one, one, bcast(idf[:, 2 * h + which, :], 1, K), ALU.mult)
                        chain(last)
                        if which == 0 and t >= 1:
                            dve.wait_ge(turned, t)
                        chain(dve.tensor_reduce(res[:, which, :, :], pick[:, :, :].rearrange("p h (i j) -> p h i j", j=K),
                                                AX.X, ALU.add))
                    chain(dve.tensor_copy(gs[:, :], best[:, :, 0]))
                    chain(dve.tensor_tensor(best[:, :, :], best[:, :, :], bcast(gs[:, :], 2, K), ALU.subtract))
                    dve.sem_inc(exp_ready, 1)
                    dve.wait_ge(exp_done, t + 1)
                    chain(dve.tensor_reduce(gs[:, :], best[:, :, :], AX.X, ALU.add))
                    chain(dve.reciprocal(gs[:, :], gs[:, :]))
                    dve.tensor_tensor(res[:, 2, :, :], best[:, :, :], bcast(gs[:, :], 2, K), ALU.mult).then_inc(picked, 1)

        with ExitStack() as half:
            hb = lambda name, shape, dt=F32: half.enter_context(nc.sbuf_tensor("pg_" + name, shape, dt))
            hot1 = hb("hot1", [P, 8, PK])
            hot2 = hb("hot2", [P, 8, PK])
            table = hb("table", [P, 2, PK, NB])
            hot_ready, gates_mm, gates_sb = (m.sem(f"pg_{v}") for v in ("hot", "mm", "sb"))
            table_out = [m.sem(f"pg_out{i}") for i in range(2)]
            block = half.enter_context(nc.Block(no_gpsimd_drain=True))
            QUADS = T // 4
            STEPS = QUADS // (4 * HALF)
            assert STEPS * 4 * HALF == QUADS and NB % 32 == 0
            turns = HALF // 4

            @block.sync
            def _(sp):
                load_slabs(m, sp, S_V + RING)

            @block.tensor
            def _(pe):
                with pe.Fori(0, turns) as turn:
                    for i in range(4):
                        s = S_U + HALF + i
                        n = turn * 4 + (HALF + i)
                        pe.wait_ge(m.slab_loaded[s % RING], turn * 16 + 16 * (s // RING + 1))
                        for j in range(4):
                            pe.wait_ge(act_ready, n * 4 + (j - 1))
                            for k in range(DC):
                                mm = pe.matmul(m.bank[j % 2][:, :], m.ring[:, s % RING, (j * DC + k) * P:(j * DC + k + 1) * P],
                                               hT[:, k, :], start=(k == 0), stop=(k == DC - 1))
                            mm.then_inc(m.products, 1)
                            for b in range(STEPS):
                                at = (4 * i + j) * STEPS + b
                                quad = turn * (16 * STEPS) + at
                                pe.wait_ge(hot_ready, quad + 1)
                                pe.wait_ge(gates_sb, quad + 1)
                                for c in range(4):
                                    mm = pe.matmul(m.bank[4 + at % 4][:, c * PK:(c + 1) * PK], hot2[:, 4 * (at % 2) + c, :],
                                                   hot1[:, 4 * (at % 2) + c, :], start=True, stop=True)
                                mm.then_inc(gates_mm, 1)

            @block.vector
            def _(dve):
                dve.sem_inc(gates_mm, 2)
                dve.sem_inc(gates_sb, 4)
                with dve.Fori(0, turns) as turn:
                    for at in range(16 * STEPS):
                        quad = turn * (16 * STEPS) + at
                        dve.wait_ge(gates_mm, quad + 1)
                        for c in range(4):
                            token = turn * (64 * STEPS) + (4 * at + c)
                            dve.tensor_scalar(hot2[:, 4 * (at % 2) + c, :], iota, e_turned[:, 1, bass.ds(token, 1)],
                                              None, ALU.is_equal)
                            last = dve.tensor_scalar(hot1[:, 4 * (at % 2) + c, :], iota, e_turned[:, 0, bass.ds(token, 1)],
                                                     e_turned[:, 2, bass.ds(token, 1)], ALU.is_equal, ALU.mult)
                        last.then_inc(hot_ready, 1)

            @block.scalar
            def _(act):
                parts = 16 * STEPS // (NB // 4)
                with act.Fori(0, turns) as turn:
                    for i in range(4):
                        n = turn * 4 + (HALF + i)
                        act.wait_ge(gl_out[i % 2], 8 * n - 8 * (i % 2))
                        for j in range(4):
                            act.wait_ge(m.products, 4 * n + (first + j + 1))
                            act.activation(gl[:, i % 2, j, :], m.bank[j % 2][:, :], ACT.Gelu).then_inc(act_ready, 1)
                            for b in range(STEPS):
                                at = (4 * i + j) * STEPS + b
                                quad = turn * (16 * STEPS) + at
                                part = at // (NB // 4)
                                q = at % (NB // 4)
                                if q == 0:
                                    act.wait_ge(table_out[part % 2], (turn * parts + (part - part % 2)) * 8 + 16)
                                act.wait_ge(gates_mm, quad + 3)
                                act.activation(table[:, part % 2, :, 4 * q:4 * q + 4].rearrange("p e c -> p c e"),
                                               m.bank[4 + at % 4][:, :].rearrange("p (c e) -> p c e", e=PK),
                                               ACT.Copy).then_inc(gates_sb, 1)
                                if q == NB // 4 - 1:
                                    act.wait_ge(gates_sb, quad + 5)
                                    t0 = (turn * parts + part) * NB
                                    act.dma_start(d.gates[:, :, bass.ds(t0, NB)], table[:, part % 2, :, :]).then_inc(table_out[part % 2], 16)
                        act.wait_ge(act_ready, 4 * n + 4)
                        act.dma_start(d.gelu[bass.ds(n, 1)].rearrange("o p c t -> (o p) c t"),
                                      gl[:, i % 2, :, :]).then_inc(gl_out[i % 2], 16)
                for i in range(2):
                    act.wait_ge(gl_out[i], 16 * HALF)
                    act.wait_ge(table_out[i], 16 + 16 * turns * parts // 2)

            @block.gpsimd
            def _(pool):
                for i in range(2):
                    pool.sem_inc(table_out[i], 16)


def stage_peer_v(nc, m, xT):
    with ExitStack() as own:
        sb = lambda name, shape: own.enter_context(nc.sbuf_tensor("pv_" + name, shape, F32))
        gl = sb("gl", [P, 2, 4, T])
        gt = sb("gt", [P, 2, 4, T])
        coef = sb("coef", [P, 2, 4, T])
        zero = sb("zero", [P, T])
        gl_in = [m.sem(f"pv_gl{i}") for i in range(2)]
        gt_in = [m.sem(f"pv_gt{i}") for i in range(2)]
        zeroed, coef_ready, out_ready, done, stored = (
            m.sem(f"pv_{v}") for v in ("zeroed", "coef", "out", "done", "stored"))
        block = own.enter_context(nc.Block(no_gpsimd_drain=True))
        N = PK // 4
        turns = N // RING
        d = m.dram

        @block.sync
        def _(sp):
            load_slabs(m, sp, S_END)
            for k in range(DC):
                sp.wait_ge(done, k + 1)
                sp.dma_start(d.out[:, k, :], xT[:, k, :]).then_inc(stored, 16)
            sp.wait_ge(stored, 16 * DC)

        @block.scalar
        def _(act):
            with act.Fori(0, turns) as turn:
                for i in range(RING):
                    n = turn * RING + i
                    act.wait_ge(coef_ready, 4 * n + 4)
                    act.dma_start(gl[:, i % 2, :, :], d.gelu[bass.ds(n, 1)].rearrange("o p c t -> (o p) c t")).then_inc(gl_in[i % 2], 16)
                    act.dma_start(gt[:, i % 2, :, :], d.gates[:, bass.ds(n * 4, 4), :]).then_inc(gt_in[i % 2], 16)

        @block.vector
        def _(dve):
            dve.memset(zero[:, :], 0.0).then_inc(zeroed, 1)
            dve.sem_inc(coef_ready, 8)
            with dve.Fori(0, turns) as turn:
                for i in range(RING):
                    n = turn * RING + i
                    dve.wait_ge(gl_in[i % 2], turn * 32 + 16 * (i // 2 + 1))
                    dve.wait_ge(gt_in[i % 2], turn * 32 + 16 * (i // 2 + 1))
                    dve.wait_ge(m.products, 4 * n + (4 * S_V - 4))
                    for j in range(4):
                        dve.tensor_tensor(coef[:, i % 2, j, :], gl[:, i % 2, j, :], gt[:, i % 2, j, :],
                                          ALU.mult).then_inc(coef_ready, 1)
            for k in range(DC):
                dve.wait_ge(out_ready, k + 1)
                dve.tensor_tensor(xT[:, k, :], m.bank[k][:, :], xT[:, k, :], ALU.add).then_inc(done, 1)

        @block.tensor
        def _(pe):
            pe.wait_ge(zeroed, 1)
            for k in range(DC):
                pe.matmul(m.bank[k][:, :], zero[:, 0:P], zero[:, :], start=True, stop=False)
            with pe.Fori(0, turns) as turn:
                for i in range(RING):
                    s = S_V + i
                    n = turn * RING + i
                    pe.wait_ge(m.slab_loaded[s % RING], turn * 16 + 16 * (s // RING + 1))
                    for j in range(4):
                        pe.wait_ge(coef_ready, 4 * n + (j + 9))
                        for k in range(DC):
                            mm = pe.matmul(m.bank[k][:, :], m.ring[:, s % RING, j * D + k * P:j * D + (k + 1) * P],
                                           coef[:, i % 2, j, :], start=False, stop=False)
                        mm.then_inc(m.products, 1)
            for k in range(DC):
                pe.matmul(m.bank[k][:, :], zero[:, 0:P], zero[:, :], start=False, stop=True).then_inc(out_ready, 1)


def stage_overflow(nc, m):
    F = 512
    with ExitStack() as own:
        sb = lambda name, shape, dt=F32: own.enter_context(nc.sbuf_tensor("ov_" + name, shape, dt))
        w = sb("w", [P, 3, SLAB])
        x = sb("x", [P, D])
        xT = sb("xT", [P, D])
        gate = sb("gate", [P, F])
        hid = sb("hid", [P, F])
        hidT = sb("hidT", [P, F])
        y = sb("y", [P, D])
        ids = sb("ids", [P, 1], I32)
        w_in, ids_ready, x_in, xt_mm, xt_sb, gu, gated, hid_ready, hidt_mm, hidt_sb, y_mm, y_sb, y_out = (
            m.sem(f"ov_{v}") for v in ("w", "ids", "x", "xt_mm", "xt_sb", "gu", "gated", "hid", "hidt_mm", "hidt_sb",
                                       "y_mm", "y_sb", "y_out"))
        carrier = m.sem("ov_carrier")
        block = own.enter_context(nc.Block(no_gpsimd_drain=True))
        d = m.dram

        def each(engine, body):
            number = engine.value_load(m.steer[0:1, OVER:OVER + 1], min_val=0, max_val=OVER)
            with engine.Fori(0, OVER) as b:
                with engine.If(b < number):
                    body(b)

        @block.sync
        def _(sp):
            sp.sem_inc(y_out, 16)

            def body(b):
                e = sp.value_load(m.steer[0:1, bass.ds(b, 1)], min_val=0, max_val=EXPERTS - 1)
                for i in range(3):
                    sp.dma_start(w[:, i, :], m.weights[bass.ds(e * 3 + (S_MOE + i), 1)].rearrange("a p n -> (a p) n")
                                 ).then_inc(w_in, 16)
                sp.wait_ge(y_sb, b * 2 + 2)
                sp.dma_start(d.y_rows[bass.ds(b * SLOTS + EXPERTS * SLOTS, SLOTS), :], y[:, :]).then_inc(y_out, 16)
                sp.wait_ge(y_out, b * 16 + 32)
                sp.sem_inc(carrier, 1)
            each(sp, body)

        @block.gpsimd
        def _(pool):
            def body(b):
                pool.wait_ge(ids_ready, b + 1)
                pool.sem_inc(carrier, 1)
                pool.indirect_dma_start(out=x[:, :], out_offset=None, in_=d.h_rows,
                                        in_offset=bass.IndirectOffsetOnAxis(ap=ids[:, 0:1], axis=0)).then_inc(x_in, 16)
                pool.wait_ge(y_sb, b * 2 + 2)
            each(pool, body)

        @block.tensor
        def _(pe):
            def body(b):
                pe.wait_ge(x_in, b * 16 + 16)
                for k in range(DC):
                    mm = pe.transpose(m.bank[4 + k // 4][:, (k % 4) * P:(k % 4 + 1) * P], x[:, k * P:(k + 1) * P], m.ident)
                mm.then_inc(xt_mm, 1)
                pe.wait_ge(xt_sb, b * 2 + 2)
                pe.wait_ge(w_in, b * 48 + 48)
                for i in range(2):
                    for k in range(DC):
                        mm = pe.matmul(m.bank[i][:, :], xT[:, k * P:(k + 1) * P], w[:, i, k * F:(k + 1) * F],
                                       start=(k == 0), stop=(k == DC - 1))
                mm.then_inc(gu, 1)
                pe.wait_ge(hid_ready, b + 1)
                for k in range(4):
                    mm = pe.transpose(m.bank[6][:, k * P:(k + 1) * P], hid[:, k * P:(k + 1) * P], m.ident)
                mm.then_inc(hidt_mm, 1)
                pe.wait_ge(hidt_sb, b + 1)
                for half in range(2):
                    for k in range(4):
                        mm = pe.matmul(m.bank[2 + half][:, :], hidT[:, k * P:(k + 1) * P],
                                       w[:, 2, k * D + half * F:k * D + (half + 1) * F], start=(k == 0), stop=(k == 3))
                mm.then_inc(y_mm, 1)
                pe.wait_ge(y_sb, b * 2 + 2)
            each(pe, body)

        @block.scalar
        def _(act):
            def body(b):
                act.wait_ge(xt_mm, b + 1)
                for i in range(2):
                    act.activation(xT[:, i * F:(i + 1) * F], m.bank[4 + i][:, :], ACT.Copy).then_inc(xt_sb, 1)
                act.wait_ge(gu, b + 1)
                act.activation(gate[:, :], m.bank[0][:, :], ACT.Silu).then_inc(gated, 1)
                act.wait_ge(hidt_mm, b + 1)
                act.activation(hidT[:, :], m.bank[6][:, :], ACT.Copy).then_inc(hidt_sb, 1)
            each(act, body)

        @block.vector
        def _(dve):
            def body(b):
                dve.tensor_copy(ids[:, :], m.tokens[:, bass.ds(b + EXPERTS, 1)]).then_inc(ids_ready, 1)
                dve.wait_ge(gated, b + 1)
                dve.tensor_tensor(hid[:, :], gate[:, :], m.bank[1][:, :], ALU.mult).then_inc(hid_ready, 1)
                dve.wait_ge(y_mm, b + 1)
                dve.wait_ge(y_out, b * 16 + 16)
                for half in range(2):
                    dve.tensor_copy(y[:, half * F:(half + 1) * F], m.bank[2 + half][:, :]).then_inc(y_sb, 1)
            each(dve, body)


def program(nc, d):
    with ExitStack() as ctx:
        m = Names()
        m.dram = d
        m.weights = d.weights
        m.issued = 0
        m.sem = lambda name: ctx.enter_context(nc.semaphore(name))
        keep = lambda name, shape, dt=F32: ctx.enter_context(nc.sbuf_tensor(name, shape, dt))
        m.psum = ctx.enter_context(nc.psum_tensor("psum", [P, 8, 512], F32))
        m.bank = [m.psum[:, i, :] for i in range(8)]
        m.ring = keep("ring", [P, RING, SLAB])
        m.slab_loaded = [m.sem(f"slab_loaded{i}") for i in range(RING)]
        m.products = m.sem("products")
        m.chain = Chain(m.sem("vector_order"))
        m.emptied, m.emptied_after = m.sem("banks_emptied"), 0
        m.gate_ready, m.gate_used, m.gates = m.sem("gate_ready"), m.sem("gate_used"), 0
        m.norm_sems, m.norms = [m.sem(f"norm_{x}") for x in ("squares", "total", "root", "scaled")], 0
        m.const = keep("const", [P, C_END])
        m.ident = m.const[:, C_IDENT:C_IDENT + P]
        m.ones = m.const[:, C_ONES:C_ONES + P]
        m.halves = m.const[:, C_HALVES:C_HALVES + P]
        m.causal = m.const[:, C_CAUSAL:C_CAUSAL + P]
        m.before = m.const[:, C_BEFORE:C_BEFORE + P]
        m.vec = keep("vec", [P, 5, DC])
        m.small = keep("small", [P, 6])
        m.sinks = keep("sinks", [P, SWA_HEADS])
        m.dn = keep("dn", [P, 2])
        m.mod = keep("mod", [P, 48])
        m.scale = keep("scale", [P, 2, DC])
        m.eps = keep("eps", [P, 1])
        m.neg_lam = keep("neg_lam", [P, 1])
        m.tokens = keep("tokens", [P, BLOCKS], I32)
        m.pair_row = keep("pair_row", [P, 2, TT], I32)
        m.pair_w = keep("pair_w", [P, 2, TT])
        m.steer = keep("steer", [P, 8], I32)
        m.xT = keep("xT", [P, DC, T])
        m.hT = keep("hT", [P, DC, T])
        xT, hT = m.xT, m.hT

        with ExitStack() as first:
            fb = lambda name, shape: first.enter_context(nc.sbuf_tensor(name, shape, F32))
            m.rot_cos = fb("rot_cos", [P, T])
            m.rot_sin = fb("rot_sin", [P, T])
            stage_modulation(nc, m)
            stage_norm(nc, m, "norm_mix", xT, hT, m.scale[:, 0, :], m.mod[:, 0:8])
            merged = fb("merged", [P, DC, T])
            roT = fb("roT", [P, DC, T])
            with ExitStack() as qkv:
                qb = lambda name, shape: qkv.enter_context(nc.sbuf_tensor(name, shape, F32))
                qT, kT, vals = qb("ret_q", [P, 4, T]), qb("ret_k", [P, 4, T]), qb("ret_v", [P, TT, D])
                stage_project(nc, m, "retp", [(S_RQ, qT, 0), (S_RK, kT, 0)], [(S_RV, 0), (S_RV + 1, 512)], hT, vals)
                stage_retention(nc, m, qT, kT, vals, roT)
            stage_linear(nc, m, "ret_out", [
                (S_RG, hT, 0, "times_silu", (roT, 0)), (S_RG + 1, hT, 0, "times_silu", (roT, 4)),
                (S_RO, roT, 2, "copy", (merged, 0)), (S_RO + 1, roT, 2, "copy", (merged, 4)),
                (S_GR, hT, 0, "times_sigmoid", (merged, 0)), (S_GR + 1, hT, 0, "times_sigmoid", (merged, 4))])
            with ExitStack() as qkv:
                qb = lambda name, shape: qkv.enter_context(nc.sbuf_tensor(name, shape, F32))
                qT, kT, vals = qb("diff_q", [P, DC, T]), qb("diff_k", [P, DC, T]), qb("diff_v", [P, TT, D])
                stage_project(nc, m, "diffp", [(S_DQ, qT, 0), (S_DQ + 1, qT, 4), (S_DK, kT, 0), (S_DK + 1, kT, 4)],
                              [(S_DV, 0), (S_DV + 1, 512)], hT, vals)
                stage_diff(nc, m, qT, kT, vals, roT)
            other = fb("diff_out", [P, DC, T])
            stage_linear(nc, m, "mix_out", [
                (S_DO, roT, 0, "copy", (other, 0)), (S_DO + 1, roT, 0, "copy", (other, 4)),
                (S_GD, hT, 0, "add_sigmoid_times", (merged, 0, other)),
                (S_GD + 1, hT, 0, "add_sigmoid_times", (merged, 4, other)),
                (S_OUT, merged, 4, "add_scaled", (xT, 0, m.mod[:, 16:24])),
                (S_OUT + 1, merged, 4, "add_scaled", (xT, 4, m.mod[:, 16:24]))])
        stage_norm(nc, m, "norm_ffn", xT, hT, m.scale[:, 1, :], m.mod[:, 24:32])
        stage_route(nc, m, hT)
        stage_experts(nc, m)
        stage_overflow(nc, m)
        stage_combine(nc, m, xT)
        stage_norm(nc, m, "norm_final", xT, hT, m.vec[:, 2, :])
        xT, hT = hT, xT
        stage_norm(nc, m, "norm1", xT, hT, m.vec[:, 3, :])
        with ExitStack() as second:
            wb = lambda name, shape: second.enter_context(nc.sbuf_tensor(name, shape, F32))
            cat = wb("cat", [P, DC, T])
            qT, kT, vals = wb("swa_q", [P, 4, T]), wb("swa_k", [P, T]), wb("swa_v", [P, TT, P])
            d_pool = wb("d_pool", [P, 4, T])
            with ExitStack() as pool:
                poolT = pool.enter_context(nc.sbuf_tensor("pooled", [P, 4, T], F32))
                stage_in2(nc, m, hT, qT, kT, vals, poolT, d_pool)
            stage_window(nc, m, qT, kT, vals, d_pool, cat)
            stage_linear(nc, m, "out2", [(S_OUT2, cat, 0, "add", (xT, 0)), (S_OUT2 + 1, cat, 0, "add", (xT, 4))])
        stage_norm(nc, m, "norm2", xT, hT, m.vec[:, 4, :])
        stage_peer_u(nc, m, hT)
        stage_peer_v(nc, m, xT)


def kernel(**inputs):
    import numpy as np
    import concourse.bacc as bacc
    from concourse.bass_utils import run_bass_kernel_spmd

    a = {k: np.asarray(v) for k, v in inputs.items()}

    def rows_of(w, tiles=4):
        return w.reshape(DC, P, tiles, P).transpose(1, 2, 0, 3).reshape(P, -1)

    def wide(w):
        return w.reshape(-1, P, w.shape[1]).transpose(1, 0, 2).reshape(P, -1)

    def cut(w):
        return [w[:, i:i + 512] for i in range(0, w.shape[1], 512)]

    w_in, w_in2 = a["w_in"][0], a["w_in_2"][0]
    col = cut(w_in)
    slabs = [rows_of(c) for c in col[0:2]] + [wide(c) for c in col[2:4]] + [rows_of(c) for c in col[4:6]]
    slabs += [rows_of(c) for c in cut(a["w_ret_o"][0])] + [rows_of(c) for c in col[12:14]]
    slabs += [rows_of(c) for c in col[6:10]] + [wide(c) for c in col[10:12]]
    slabs += [rows_of(c) for c in cut(a["w_diff_o"][0])] + [rows_of(c) for c in col[14:16]]
    slabs += [rows_of(c) for c in cut(a["w_out"][0])]
    for e in range(EXPERTS):
        slabs += [wide(a["w_exp_gate"][0, e]), wide(a["w_exp_up"][0, e]), wide(a["w_exp_down"][0, e])]
    order = np.concatenate([np.arange(HD) + HD * h for j in range(4) for h in (j, j + 4)])
    slabs.append(rows_of(w_in2[:, order]))
    slabs.append(rows_of(w_in2[:, 768:1280]))
    kv = np.zeros((P, SLAB), np.float32)
    kv[:, 0:D] = rows_of(w_in2[:, 512:640], 1)
    kv[:, D:2 * D] = wide(w_in2[:, 640:768])
    slabs.append(kv)
    w_out2 = a["w_out_2"][0]
    w_out2 = np.concatenate([w_out2[order], w_out2[512:]], axis=0)
    slabs += [rows_of(c) for c in cut(w_out2)] + [rows_of(c) for c in cut(a["peer_wq_2"][0])]
    u_t = a["peer_u_2"][0].T
    slabs += [rows_of(c) for c in cut(u_t)]
    v = a["peer_v_2"][0].reshape(PK // 4, 4, P, D).transpose(0, 2, 1, 3).reshape(PK // 4, P, SLAB)
    weights = np.concatenate([np.stack(slabs), v])

    def cols(v):
        return np.ascontiguousarray(v.reshape(-1, P).T)

    r = np.arange(P)
    const = np.zeros((P, C_END), np.float32)
    const[:, C_IDENT:C_IDENT + P] = np.eye(P)
    const[:, C_ONES:C_ONES + P] = 1.0
    const[:, C_HALVES:C_HALVES + P] = (r[:, None] // HD) == (r[None, :] // HD)
    const[:, C_CAUSAL:C_CAUSAL + P] = np.where(r[None, :] <= r[:, None], 0.0, NEG)
    const[:, C_BEFORE:C_BEFORE + P] = r[:, None] < r[None, :]
    const[:, C_IOTA:C_IOTA + P] = r[None, :]
    inv = np.float32(10000.0) ** (-np.arange(0, P, 2, dtype=np.float32) / np.float32(P))
    const[:, C_INV] = np.tile(inv, 2)
    const[:, C_SIGN] = np.where(r < P // 2, 1.0, -1.0)
    const[:, C_TOKEN:C_TOKEN + TT] = r[:, None] + P * np.arange(TT)[None, :]
    for g in range(4):
        const[:, C_COUNT + 16 * g:C_COUNT + 16 * (g + 1)] = 1.0 / np.minimum(np.arange(16) + 1, 2 << g)
    j = np.arange(BAND)[None, :]
    chunk = r[:, None] // 64
    const[:, C_MASK:C_MASK + BAND] = np.where((j // 64 >= chunk) & (j // 64 <= chunk + 2), 0.0, NEG)
    gamma = 1.0 - 2.0 ** (-5.0 - np.arange(HEADS))
    rel = np.arange(T)[None, :] - r[:, None]
    decay = np.where(rel[None] >= 0, np.exp(np.log(gamma)[:, None, None] * np.maximum(rel, 0)[None]), 0.0) * ATT_SCALE
    decay = decay.transpose(1, 0, 2).astype(np.float32)
    dist = np.arange(VEC) - 255
    n = np.abs(dist)
    large = 8 + np.searchsorted(8.0 * 2.0 ** (np.arange(1, 8) / 2.0), n, side="right")
    bucket = np.where(dist > 0, 16, 0) + np.where(n < 8, n, np.minimum(large, 15))
    buckets = (np.arange(32)[:, None] == bucket[None, :]).astype(np.float32)

    arrays = {
        "weights": weights,
        "x": a["x"][0].T.reshape(DC, P, T).transpose(1, 0, 2),
        "c": a["c"],
        "positions": a["positions"],
        "w_ada": a["w_ada"][0].T.reshape(12, 4, P, D).transpose(0, 2, 1, 3).reshape(12, P, SLAB),
        "b_ada": cols(a["b_ada"][0]),
        "const": const,
        "decay": decay,
        "buckets": buckets,
        "vec": np.stack([cols(a[k].reshape(-1)) for k in ("norm_mix", "norm_ffn", "norm_final", "norm1_g_2", "norm2_g_2")], axis=1),
        "diff_norm": cols(a["diff_norm"][0]),
        "rel_bias": a["rel_bias_2"],
        "lam_q1": a["lam_q1"], "lam_k1": a["lam_k1"], "lam_q2": a["lam_q2"], "lam_k2": a["lam_k2"],
        "small": np.concatenate([np.tile(a["q_norm_g_2"][0], 2)[:, None], np.tile(a["k_norm_g_2"][0], 2)[:, None],
                                 cols(a["pool_scale_2"][0])], axis=1),
        "sinks": a["attn_sinks_2"],
        "pool_w": a["pool_w_2"][0].transpose(1, 0, 2),
        "w_router": np.concatenate([a["w_router_group"][0], a["w_router_expert"][0]], axis=1).reshape(DC, P, 36).transpose(1, 0, 2),
        "b_router": np.concatenate([a["b_router_group"], a["b_router_expert"]], axis=1),
        "subkeys": a["peer_subkeys_2"][0].reshape(2 * PH, PK, P).transpose(2, 0, 1),
    }
    arrays = {k: np.ascontiguousarray(v) for k, v in arrays.items()}

    nc = bacc.Bacc("TRN2", target_bir_lowering=False, num_devices=1)
    d = Names()
    for name, v in arrays.items():
        d.__dict__[name] = nc.dram_tensor("in_" + name, v.shape, mybir.dt.from_np(v.dtype), kind="ExternalInput").ap()
    d.lams = [d.lam_q1, d.lam_k1, d.lam_q2, d.lam_k2]
    scratch = lambda name, shape, dt=F32: nc.dram_tensor(name, shape, dt, kind="Internal").ap()
    d.by_distance = scratch("by_distance_rows", (SWA_HEADS, P, VEC))
    d.bias_band = [bass.AP(d.by_distance.tensor, h * P * VEC + P - 1, [[VEC - 1, P], [1, BAND]]) for h in range(SWA_HEADS)]
    d.h_rows = scratch("h_rows", (T, D))
    d.y_rows = scratch("y_rows", (BLOCKS * SLOTS, D))
    d.slot_token = scratch("slot_token", (BLOCKS * SLOTS, 1), I32)
    d.gelu = scratch("gelu_rows", (PK // 4, P, 4, T))
    d.gates = scratch("gates_rows", (P, PK, T))
    out = nc.dram_tensor("y", (P, DC, T), F32, kind="ExternalOutput").ap()
    d.out = out
    program(nc, d)
    result = run_bass_kernel_spmd(nc, [{"in_" + k: v for k, v in arrays.items()}], core_ids=[0])
    y = result.results[0]["y"]
    return y.transpose(1, 0, 2).reshape(D, T).T.reshape(1, T, D)
```

```python
from contextlib import ExitStack

import concourse.bass as bass
from concourse import mybir

F32 = mybir.dt.float32
F32R = mybir.dt.float32r
I32 = mybir.dt.int32
U32 = mybir.dt.uint32
ACT = mybir.ActivationFunctionType
ALU = mybir.AluOpType
AX = mybir.AxisListType

P = 128
T = 512
TT = T // P
D = 1024
DC = D // P
HEADS = 4
DV = 256
EPS = 1e-6
LAMBDA_INIT = 0.2
ATT_SCALE = float(P) ** -0.5
RING = 4
SLAB = 4096
EXPERTS = 32
GROUPS = 4
SLOTS = 128
OVER = 7
BLOCKS = EXPERTS + OVER + 1
ROWS = 2 * T
SWA_HEADS = 8
HD = 64
BAND = 256
VEC = 384
PH = 8
TOPK = 16
PK = 128
NEG = -1.0e30
LOWEST = -3.0e38

(S_RQ, S_RK, S_RV, S_RG, S_RO, S_GR, S_DQ, S_DK, S_DV, S_DO, S_GD, S_OUT) = (
    0, 1, 2, 4, 6, 8, 10, 12, 14, 16, 18, 20)
S_MOE = 22
S_IN2 = S_MOE + 3 * EXPERTS
S_OUT2 = S_IN2 + 3
S_WQ = S_OUT2 + 2
S_U = S_WQ + 4
S_V = S_U + PK // 4
S_END = S_V + PK // 4

C_IDENT, C_ONES, C_HALVES, C_CAUSAL, C_BEFORE, C_IOTA = 0, 128, 256, 384, 512, 640
C_INV, C_SIGN, C_TOKEN, C_COUNT, C_MASK = 768, 769, 770, 774, 774 + 64
C_END = C_MASK + BAND


class Chain:

    def __init__(self, sem):
        self.sem, self.n = sem, 0

    def __call__(self, engine, instruction):
        instruction.then_inc(self.sem, 1)
        self.n += 1
        engine.wait_ge(self.sem, self.n)


class Names:

    def begin(self, first_slab):
        self.first_slab = first_slab
        self.emptied_before = self.emptied_after

    def tile(self, s, j):
        return 4 * (s - self.first_slab) + j

    def wait_product(self, engine, s, j):
        engine.wait_ge(self.products, 4 * s + j + 1)

    def wait_bank(self, engine, s, j):
        if self.tile(s, j) >= 4:
            self.wait_emptied(engine, self.tile(s, j) - 3)

    def wait_emptied(self, engine, n):
        engine.wait_ge(self.emptied, self.emptied_before + n)

    def end(self, tiles):
        self.emptied_after = self.emptied_before + tiles


def bcast(ap, where, n):
    dims = list(ap.shape)
    return ap.unsqueeze(where).to_broadcast(dims[:where] + [n] + dims[where:])


def load_slabs(m, sp, until):
    def one(s, slot):
        if isinstance(s, int):
            if s >= RING:
                sp.wait_ge(m.products, 4 * (s - RING + 1))
            src = m.weights[s]
        else:
            sp.wait_ge(m.products, 4 * s - 4 * (RING - 1))
            src = m.weights[bass.ds(s, 1)].rearrange("a p n -> (a p) n")
        sp.dma_start(m.ring[:, slot, :], src).then_inc(m.slab_loaded[slot], 16)

    while m.issued < until and (m.issued % RING or m.issued < RING):
        one(m.issued, m.issued % RING)
        m.issued += 1
    turns = (until - m.issued) // RING
    if turns >= 2:
        first = m.issued
        with sp.Fori(0, turns) as turn:
            for slot in range(RING):
                one(turn * RING + (first + slot), slot)
        m.issued += turns * RING
    while m.issued < until:
        one(m.issued, m.issued % RING)
        m.issued += 1


def wait_slab(m, engine, s):
    engine.wait_ge(m.slab_loaded[s % RING], 16 * (s // RING + 1))


def pe_features(m, pe, s, acts, tiles=4):
    wait_slab(m, pe, s)
    for j in range(tiles):
        m.wait_bank(pe, s, j)
        for k in range(DC):
            mm = pe.matmul(m.bank[j][:, :], m.ring[:, s % RING, (j * DC + k) * P:(j * DC + k + 1) * P],
                           acts[:, k, :], start=(k == 0), stop=(k == DC - 1))
        mm.then_inc(m.products, 1)


def pe_tokens(m, pe, s, acts):
    wait_slab(m, pe, s)
    for j in range(TT):
        m.wait_bank(pe, s, j)
        for k in range(DC):
            mm = pe.matmul(m.bank[j][:, :], acts[:, k, j * P:(j + 1) * P],
                           m.ring[:, s % RING, k * 512:(k + 1) * 512], start=(k == 0), stop=(k == DC - 1))
        mm.then_inc(m.products, 1)


def split_number(s):
    return 4 * s - 4 * S_IN2


def load_halves(m, sp, first, until):
    def one(s, half):
        if not isinstance(s, int) or s > S_IN2:
            sp.wait_ge(m.lows, split_number(s) + (2 * half - 2))
        src = m.weights[s] if isinstance(s, int) else m.weights[bass.ds(s, 1)].rearrange("a p n -> (a p) n")
        sp.dma_start(m.half_slab[:, half, :], src[:, half * SLAB // 2:(half + 1) * SLAB // 2]
                     ).then_inc(m.half_loaded[half], 16)

    if until - first <= 4:
        for s in range(first, until):
            one(s, 0)
            one(s, 1)
    else:
        with sp.Fori(first, until) as s:
            one(s, 0)
            one(s, 1)


def act_high(m, act, s, j, slot):
    if j % 2 == 0:
        act.wait_ge(m.half_loaded[j // 2], s * 16 - (16 * S_IN2 - 16))
    if j == 0 and (not isinstance(s, int) or s >= S_IN2 + 2):
        act.wait_ge(m.products, 4 * s - 4)
    w = SLAB // 4
    act.activation(m.high[:, slot, j * w:(j + 1) * w], m.half_slab[:, j // 2, (j % 2) * w:(j % 2 + 1) * w],
                   ACT.Copy).then_inc(m.highs, 1)


def pool_low(m, pool, s, slot):
    w = SLAB // 4
    for j in range(4):
        pool.wait_ge(m.highs, split_number(s) + (j + 1))
        pool.tensor_tensor(m.low[:, slot, j * w:(j + 1) * w], m.half_slab[:, j // 2, (j % 2) * w:(j % 2 + 1) * w],
                           m.high[:, slot, j * w:(j + 1) * w].bitcast(F32), ALU.subtract).then_inc(m.lows, 1)


def three_passes(pe, out, w, x, start, stop):
    pe.matmul(out, w[0], x[0], start=start, stop=False)
    pe.matmul(out, w[0], x[1], start=False, stop=False)
    return pe.matmul(out, w[1], x[0], start=False, stop=stop)


def pe_features_split(m, pe, s, acts, tiles=4):
    for j in range(tiles):
        pe.wait_ge(m.lows, split_number(s) + j + 1)
        m.wait_bank(pe, s, j)
        for k in range(DC):
            at = slice((j * DC + k) * P, (j * DC + k + 1) * P)
            mm = three_passes(pe, m.bank[j][:, :], [m.high[:, s % 2, at], m.low[:, s % 2, at]],
                              [acts[0][:, k, :], acts[1][:, k, :]], k == 0, k == DC - 1)
        mm.then_inc(m.products, 1)


def stage_linear_split(nc, m, name, jobs, source=None):
    m.begin(jobs[0][0])
    with ExitStack() as own:
        acts_high, acts_low = m.sem(name + "_high"), m.sem(name + "_low")
        block = own.enter_context(nc.Block(no_gpsimd_drain=True))
        first, last = jobs[0][0], jobs[-1][0]

        @block.sync
        def _(sp):
            load_halves(m, sp, first + 2, last + 3)

        @block.gpsimd
        def _(pool):
            for s in range(first + 1, last + 2):
                pool_low(m, pool, s, s % 2)

        @block.tensor
        def _(pe):
            if source is not None:
                pe.wait_ge(acts_low, DC)
            for s, acts, _, _, _ in jobs:
                pe_features_split(m, pe, s, acts)

        @block.scalar
        def _(act):
            if source is not None:
                for k in range(DC):
                    act.activation(jobs[0][1][0][:, k, :], source[:, k, :], ACT.Copy).then_inc(acts_high, 1)
            for s in range(first, last + 1):
                for j in range(4):
                    act_high(m, act, s + 1, j, (s + 1) % 2)

        @block.vector
        def _(dve):
            chain = lambda instruction: m.chain(dve, instruction)
            if source is not None:
                high, low = jobs[0][1]
                for k in range(DC):
                    dve.wait_ge(acts_high, k + 1)
                    dve.tensor_tensor(low[:, k, :], source[:, k, :], high[:, k, :].bitcast(F32), ALU.subtract).then_inc(acts_low, 1)
            for s, _, kind, dst, chunk in jobs:
                for j in range(4):
                    out = dst[:, chunk + j, :]
                    m.wait_product(dve, s, j)
                    if kind == "copy":
                        chain(dve.tensor_copy(out, m.bank[j][:, :]))
                    else:
                        chain(dve.tensor_tensor(out, m.bank[j][:, :], out, ALU.add))
                    dve.sem_inc(m.emptied, 1)
    m.end(4 * len(jobs))


def stage_modulation(nc, m):
    with ExitStack() as own:
        sb = lambda name, shape, dt=F32: own.enter_context(nc.sbuf_tensor(name, shape, dt))
        ada = sb("ada_w", [P, 3, SLAB])
        c_row = sb("c_row", [P, D])
        c_act = sb("c_act", [P, D])
        junk = sb("ada_junk", [P, D])
        b_ada = sb("b_ada", [P, 48])
        raw = sb("mod_raw", [P, 48])
        pos = sb("pos", [P, T], I32)
        ang = sb("ang", [P, T])
        turn = sb("turn", [P, T])
        mag = sb("mag", [P, T])
        halfpi = sb("halfpi", [P, 1])
        lam_in = sb("lam_in", [P, 4, P])
        lam_p = sb("lam_p", [P, P])
        lam_s = sb("lam_s", [P, 2])
        lam_e = sb("lam_e", [P, 2])
        rel = sb("rel", [32, SWA_HEADS])
        rel_wide = sb("rel_wide", [32, SWA_HEADS, P])
        buckets = sb("buckets", [32, VEC])
        by_distance = sb("by_distance", [P, 2, VEC])

        small = m.sem("mod_small")
        xin = m.sem("mod_x")
        ada_loaded = [m.sem(f"ada_loaded{i}") for i in range(3)]
        ada_used = m.sem("ada_used")
        c_ready = m.sem("c_ready")
        ang_ready = m.sem("ang_ready")
        sin_ready = m.sem("sin_ready")
        lam_ready = m.sem("lam_ready")
        lam_exp = m.sem("lam_exp")
        wide_ready = m.sem("wide_ready")
        dist_mm = m.sem("dist_mm")
        dist_sb = m.sem("dist_sb")
        dist_out = [m.sem(f"dist_out{i}") for i in range(2)]
        block = own.enter_context(nc.Block(no_gpsimd_drain=True))
        d = m.dram
        loads = [(c_row[:, :], d.c.to_broadcast([P, D])), (b_ada[:, :], d.b_ada),
                 (pos[:, :], d.positions.to_broadcast([P, T])), (m.const[:, :], d.const),
                 (m.vec[:, :, :], d.vec), (m.dn[:, :], d.diff_norm), (m.small[:, :], d.small),
                 (m.sinks[:, :], d.sinks.to_broadcast([P, SWA_HEADS])), (rel[:, :], d.rel_bias),
                 (buckets[:, :], d.buckets)]
        loads += [(lam_in[:, i, :], a.to_broadcast([P, P])) for i, a in enumerate(d.lams)]

        @block.sync
        def _(sp):
            sp.dma_start(m.xT[:, :, :], d.x).then_inc(xin, 16)
            for s in range(12):
                if s >= 3:
                    sp.wait_ge(ada_used, s - 2)
                sp.dma_start(ada[:, s % 3, :], d.w_ada[s]).then_inc(ada_loaded[s % 3], 16)
            load_slabs(m, sp, RING)
            sp.wait_ge(xin, 16)

        @block.scalar
        def _(act):
            for dst, src in loads:
                act.dma_start(dst, src).then_inc(small, 16)
            act.wait_ge(small, 16 * len(loads))
            act.activation(c_act[:, :], c_row[:, :], ACT.Silu).then_inc(c_ready, 1)
            act.wait_ge(ang_ready, 1)
            act.activation(m.rot_sin[:, :], ang[:, :], ACT.Sin).then_inc(sin_ready, 1)
            act.wait_ge(ang_ready, 2)
            act.activation(m.rot_cos[:, :], mag[:, :], ACT.Sin, bias=halfpi[:, :], scale=-1.0).then_inc(sin_ready, 1)
            act.wait_ge(lam_ready, 1)
            act.activation(lam_e[:, :], lam_s[:, :], ACT.Exp).then_inc(lam_exp, 1)
            for h in range(SWA_HEADS):
                act.wait_ge(dist_mm, h + 1)
                if h >= 2:
                    act.wait_ge(dist_out[h % 2], 16 * (h // 2))
                act.activation(by_distance[:, h % 2, :], m.bank[h % 4][:, 0:VEC], ACT.Copy).then_inc(dist_sb, 1)
                act.wait_ge(dist_sb, h + 1)
                act.dma_start(d.by_distance[h], by_distance[:, h % 2, :]).then_inc(dist_out[h % 2], 16)
            for i in range(2):
                act.wait_ge(dist_out[i], 16 * SWA_HEADS // 2)

        @block.tensor
        def _(pe):
            pe.wait_ge(wide_ready, 1)
            pe.wait_ge(small, 16 * len(loads))
            for h in range(SWA_HEADS):
                if h >= 4:
                    pe.wait_ge(dist_sb, h - 3)
                pe.matmul(m.bank[h % 4][:, 0:VEC], rel_wide[:, h, :], buckets[:, :],
                          start=True, stop=True).then_inc(dist_mm, 1)

        @block.vector
        def _(dve):
            chain = lambda instruction: m.chain(dve, instruction)
            dve.memset(m.eps[:, :], EPS)
            dve.memset(halfpi[:, :], 1.5707963267948966)
            dve.wait_ge(small, 16 * len(loads))
            chain(dve.tensor_copy(turn[:, :], pos[:, :]))
            chain(dve.tensor_scalar(ang[:, :], turn[:, :], m.const[:, C_INV:C_INV + 1], None, ALU.mult))
            chain(dve.tensor_scalar(turn[:, :], ang[:, :], 0.15915494309189535, 12582912.0, ALU.mult, ALU.add))
            chain(dve.tensor_scalar(turn[:, :], turn[:, :], 12582912.0, None, ALU.subtract))
            for part in (-6.28125, -0.0019340515136718750, -1.2556659146019e-06):
                chain(dve.scalar_tensor_tensor(out=ang[:, :], in0=turn[:, :], scalar=part, in1=ang[:, :],
                                               op0=ALU.mult, op1=ALU.add))
            chain(dve.tensor_scalar(ang[:, :], ang[:, :], 3.1415925, -3.1415925, ALU.min, ALU.max))
            dve.scalar_tensor_tensor(out=mag[:, :], in0=ang[:, :], scalar=-1.0, in1=ang[:, :], op0=ALU.mult,
                                     op1=ALU.max).then_inc(ang_ready, 2)
            chain(dve.tensor_copy(rel_wide[:, :, :], bcast(rel[:, :], 2, P)))
            dve.sem_inc(wide_ready, 1)
            for i in range(2):
                chain(dve.tensor_tensor(lam_p[:, :], lam_in[:, 2 * i, :], lam_in[:, 2 * i + 1, :], ALU.mult))
                chain(dve.tensor_reduce(lam_s[:, i:i + 1], lam_p[:, :], AX.X, ALU.add))
            dve.sem_inc(lam_ready, 1)
            dve.wait_ge(sin_ready, 2)
            chain(dve.tensor_scalar(m.rot_sin[:, :], m.rot_sin[:, :], m.const[:, C_SIGN:C_SIGN + 1], None, ALU.mult))
            dve.wait_ge(lam_exp, 1)
            chain(dve.tensor_tensor(m.neg_lam[:, :], lam_e[:, 1:2], lam_e[:, 0:1], ALU.subtract))
            chain(dve.tensor_scalar(m.neg_lam[:, :], m.neg_lam[:, :], LAMBDA_INIT, None, ALU.subtract))
            dve.tensor_scalar(m.dn[:, :], m.dn[:, :], 1.0 - LAMBDA_INIT, None, ALU.mult)
            dve.wait_ge(c_ready, 1)
            for s in range(12):
                dve.wait_ge(ada_loaded[s % 3], 16 * (s // 3 + 1))
                for j in range(4):
                    n = 4 * s + j
                    chain(dve.tensor_tensor_reduce(
                        out=junk[:, :], in0=ada[:, s % 3, j * D:(j + 1) * D], in1=c_act[:, :], scale=1.0,
                        scalar=0.0, op0=ALU.mult, op1=ALU.add, accum_out=raw[:, n:n + 1]))
                dve.sem_inc(ada_used, 1)
            chain(dve.tensor_tensor(m.mod[:, :], raw[:, :], b_ada[:, :], ALU.add))
            for v, at in ((0, 8), (1, 32)):
                chain(dve.tensor_scalar(raw[:, 0:8], m.mod[:, at:at + 8], 1.0, None, ALU.add))
                chain(dve.tensor_tensor(m.scale[:, v, :], raw[:, 0:8], m.vec[:, v, :], ALU.mult))


def stage_norm(nc, m, name, src, dst, scale, shift=None, work=None):
    work = dst if work is None else work
    squares, total, root, scaled = m.norm_sems
    n = m.norms
    m.norms += 1
    with ExitStack() as own:
        rstd = own.enter_context(nc.sbuf_tensor(name + "_rstd", [P, T], F32))
        block = own.enter_context(nc.Block(no_gpsimd_drain=True))

        @block.scalar
        def _(act):
            for k in range(DC):
                act.activation(work[:, k, :], src[:, k, :], ACT.Square).then_inc(squares, 1)
            act.wait_ge(total, n + 1)
            act.activation(rstd[:, :], m.bank[4][:, :], ACT.Sqrt, bias=m.eps[:, :], scale=1.0 / D).then_inc(root, 1)
            if shift is not None:
                for k in range(DC):
                    act.wait_ge(scaled, n * DC + k + 1)
                    act.activation(dst[:, k, :], dst[:, k, :], ACT.Identity, bias=shift[:, k:k + 1])

        @block.tensor
        def _(pe):
            for k in range(DC):
                pe.wait_ge(squares, n * DC + k + 1)
                mm = pe.matmul(m.bank[4][:, :], m.ones, work[:, k, :], start=(k == 0), stop=(k == DC - 1))
            mm.then_inc(total, 1)

        @block.vector
        def _(dve):
            dve.wait_ge(root, n + 1)
            m.chain(dve, dve.reciprocal(rstd[:, :], rstd[:, :]))
            for k in range(DC):
                dve.scalar_tensor_tensor(out=dst[:, k, :], in0=src[:, k, :], scalar=scale[:, k:k + 1],
                                         in1=rstd[:, :], op0=ALU.mult, op1=ALU.mult).then_inc(scaled, 1)


def stage_norm_split(nc, m, name, src, dst, scale, first=False):
    squares, total, root, scaled = m.norm_sems
    n = m.norms
    m.norms += 1
    high, low = dst
    with ExitStack() as own:
        rstd = own.enter_context(nc.sbuf_tensor(name + "_rstd", [P, T], F32))
        work = own.enter_context(nc.sbuf_tensor(name + "_work", [P, DC, T], F32))
        rounded = m.sem(name + "_rounded")
        block = own.enter_context(nc.Block(no_gpsimd_drain=True))

        @block.sync
        def _(sp):
            if first:
                load_halves(m, sp, S_IN2, S_IN2 + 2)

        @block.gpsimd
        def _(pool):
            if first:
                pool_low(m, pool, S_IN2, S_IN2 % 2)

        @block.scalar
        def _(act):
            for k in range(DC):
                act.activation(work[:, k, :], src[:, k, :], ACT.Square).then_inc(squares, 1)
            if first:
                for j in range(4):
                    act_high(m, act, S_IN2, j, S_IN2 % 2)
            act.wait_ge(total, n + 1)
            act.activation(rstd[:, :], m.bank[4][:, :], ACT.Sqrt, bias=m.eps[:, :], scale=1.0 / D).then_inc(root, 1)
            for k in range(DC):
                act.wait_ge(scaled, n * DC + k + 1)
                act.activation(high[:, k, :], work[:, k, :], ACT.Copy).then_inc(rounded, 1)

        @block.tensor
        def _(pe):
            for k in range(DC):
                pe.wait_ge(squares, n * DC + k + 1)
                mm = pe.matmul(m.bank[4][:, :], m.ones, work[:, k, :], start=(k == 0), stop=(k == DC - 1))
            mm.then_inc(total, 1)

        @block.vector
        def _(dve):
            dve.wait_ge(root, n + 1)
            m.chain(dve, dve.reciprocal(rstd[:, :], rstd[:, :]))
            for k in range(DC):
                dve.scalar_tensor_tensor(out=work[:, k, :], in0=src[:, k, :], scalar=scale[:, k:k + 1],
                                         in1=rstd[:, :], op0=ALU.mult, op1=ALU.mult).then_inc(scaled, 1)
            for k in range(DC):
                dve.wait_ge(rounded, k + 1)
                dve.tensor_tensor(low[:, k, :], work[:, k, :], high[:, k, :].bitcast(F32), ALU.subtract)


def stage_project(nc, m, name, rotated, values, acts, vals):
    m.begin(rotated[0][0])
    with ExitStack() as own:
        straight = own.enter_context(nc.sbuf_tensor(name + "_straight", [P, T], F32))
        crossed = own.enter_context(nc.sbuf_tensor(name + "_crossed", [P, T], F32))
        block = own.enter_context(nc.Block(no_gpsimd_drain=True))
        half = P // 2

        @block.sync
        def _(sp):
            load_slabs(m, sp, values[-1][0] + 1 + RING)

        @block.tensor
        def _(pe):
            for s, _, _ in rotated:
                pe_features(m, pe, s, acts)
            for s, _ in values:
                pe_tokens(m, pe, s, acts)

        @block.vector
        def _(dve):
            chain = lambda instruction: m.chain(dve, instruction)
            for s, dst, chunk in rotated:
                for j in range(4):
                    m.wait_product(dve, s, j)
                    acc = m.bank[j]
                    dve.tensor_tensor(straight[:, :], acc[:, :], m.rot_cos[:, :], ALU.mult)
                    dve.tensor_tensor(crossed[0:half, :], acc[half:P, :], m.rot_sin[half:P, :], ALU.mult)
                    chain(dve.tensor_tensor(crossed[half:P, :], acc[0:half, :], m.rot_sin[0:half, :], ALU.mult))
                    chain(dve.tensor_tensor(dst[:, chunk + j, :], straight[:, :], crossed[:, :], ALU.add))
                    dve.sem_inc(m.emptied, 1)

        @block.scalar
        def _(act):
            m.wait_emptied(act, 4 * len(rotated))
            for s, column in values:
                for j in range(TT):
                    m.wait_product(act, s, j)
                    act.activation(vals[:, j, column:column + 512], m.bank[j][:, :], ACT.Copy).then_inc(m.emptied, 1)
    m.end(4 * (len(rotated) + len(values)))


def head_norm_act(m, act, o_banks, ss_bank, squares, std, h, s):
    act.wait_ge(s.out_ready, h + 1)
    if h >= 1:
        act.wait_ge(s.total, h)
    for c in range(2):
        act.activation(squares[:, c, :], o_banks[c][:, :], ACT.Square).then_inc(s.squares, 1)
    act.wait_ge(s.total, h + 1)
    if h >= 1:
        act.wait_ge(s.normed, h)
    act.activation(std[:, :], ss_bank[:, :], ACT.Sqrt, bias=m.eps[:, :], scale=1.0 / DV).then_inc(s.root, 1)


def stage_retention(nc, m, qT, kT, vals, roT):
    with ExitStack() as own:
        sb = lambda name, shape: own.enter_context(nc.sbuf_tensor(name, shape, F32))
        decay = sb("decay", [P, HEADS, T])
        probs = sb("ret_probs", [P, 2, TT, T])
        squares = sb("ret_sq", [P, 2, T])
        std = sb("ret_std", [P, T])
        s = Names()
        s.decay, s.scores, s.weighted, s.out_ready, s.squares, s.total, s.root, s.normed = (
            m.sem(f"ret_{x}") for x in ("decay", "scores", "weighted", "out", "squares", "total", "root", "normed"))
        block = own.enter_context(nc.Block(no_gpsimd_drain=True))
        score_bank = [m.bank[i] for i in (0, 1, 4, 5)]
        o_bank = [m.bank[6], m.bank[7]]
        ss_bank = m.bank[2]

        @block.sync
        def _(sp):
            sp.dma_start(decay[:, :, :], m.dram.decay).then_inc(s.decay, 16)
            sp.wait_ge(s.decay, 16)

        @block.tensor
        def _(pe):
            def scores(h):
                if h >= 1:
                    pe.wait_ge(s.weighted, TT * h)
                for j in range(TT):
                    pe.matmul(score_bank[j][:, 0:T - j * P], kT[:, h, j * P:(j + 1) * P], qT[:, h, j * P:T],
                              start=True, stop=True).then_inc(s.scores, 1)

            scores(0)
            for h in range(HEADS):
                if h + 1 < HEADS:
                    scores(h + 1)
                pe.wait_ge(s.weighted, TT * (h + 1))
                if h >= 1:
                    pe.wait_ge(s.normed, h)
                for c in range(2):
                    for j in range(TT):
                        mm = pe.matmul(o_bank[c][:, j * P:T], vals[:, j, h * DV + c * P:h * DV + (c + 1) * P],
                                       probs[:, h % 2, j, j * P:T], start=(j == 0), stop=(j == TT - 1))
                mm.then_inc(s.out_ready, 1)
                pe.wait_ge(s.squares, 2 * (h + 1))
                if h >= 1:
                    pe.wait_ge(s.root, h)
                for c in range(2):
                    mm = pe.matmul(ss_bank[:, :], m.ones, squares[:, c, :], start=(c == 0), stop=(c == 1))
                mm.then_inc(s.total, 1)

        @block.scalar
        def _(act):
            for h in range(HEADS):
                head_norm_act(m, act, o_bank, ss_bank, squares, std, h, s)

        @block.vector
        def _(dve):
            chain = lambda instruction: m.chain(dve, instruction)
            dve.wait_ge(s.decay, 16)

            def weigh(h):
                if h >= 2:
                    dve.wait_ge(s.out_ready, h - 1)
                for j in range(TT):
                    dve.wait_ge(s.scores, TT * h + j + 1)
                    dve.tensor_tensor(probs[:, h % 2, j, j * P:T], score_bank[j][:, 0:T - j * P],
                                      decay[:, h, 0:T - j * P], ALU.mult).then_inc(s.weighted, 1)

            weigh(0)
            for h in range(HEADS):
                if h + 1 < HEADS:
                    weigh(h + 1)
                dve.wait_ge(s.root, h + 1)
                chain(dve.reciprocal(std[:, :], std[:, :]))
                for c in range(2):
                    last = dve.tensor_tensor(roT[:, 2 * h + c, :], o_bank[c][:, :], std[:, :], ALU.mult)
                last.then_inc(s.normed, 1)


def stage_linear(nc, m, name, jobs):
    m.begin(jobs[0][0])
    gates = {"times_silu": ACT.Silu, "times_sigmoid": ACT.Sigmoid, "add_sigmoid_times": ACT.Sigmoid}
    with ExitStack() as own:
        gate = own.enter_context(nc.sbuf_tensor(name + "_gate", [P, 2, T], F32))
        gate_ready, gate_used, g0 = m.gate_ready, m.gate_used, m.gates
        block = own.enter_context(nc.Block(no_gpsimd_drain=True))
        tiles = [(job, j) for job in jobs for j in range(4)]

        @block.sync
        def _(sp):
            load_slabs(m, sp, min(jobs[-1][0] + 1 + RING, S_END))

        @block.tensor
        def _(pe):
            for s, acts, before, _, _ in jobs:
                if before:
                    m.wait_emptied(pe, 4 * before)
                pe_features(m, pe, s, acts)

        @block.scalar
        def _(act):
            g = 0
            for (s, _, _, kind, _), j in tiles:
                if kind in gates:
                    m.wait_product(act, s, j)
                    if g >= 2:
                        act.wait_ge(gate_used, g0 + g - 1)
                    act.activation(gate[:, g % 2, :], m.bank[j][:, :], gates[kind]).then_inc(gate_ready, 1)
                    g += 1

        @block.vector
        def _(dve):
            chain = lambda instruction: m.chain(dve, instruction)
            g = 0
            for (s, _, _, kind, ops), j in tiles:
                dst, at = ops[0], ops[1] + j
                out = dst[:, at, :]
                m.wait_product(dve, s, j)
                if kind in gates:
                    dve.wait_ge(gate_ready, g0 + g + 1)
                    gated = out if kind != "add_sigmoid_times" else ops[2][:, at, :]
                    chain(dve.tensor_tensor(gated, gated, gate[:, g % 2, :], ALU.mult))
                    dve.sem_inc(gate_used, 1)
                    if kind == "add_sigmoid_times":
                        chain(dve.tensor_tensor(out, out, gated, ALU.add))
                    g += 1
                elif kind == "copy":
                    chain(dve.tensor_copy(out, m.bank[j][:, :]))
                elif kind == "add":
                    chain(dve.tensor_tensor(out, m.bank[j][:, :], out, ALU.add))
                elif kind == "add_scaled":
                    chain(dve.scalar_tensor_tensor(out=out, in0=m.bank[j][:, :], scalar=ops[2][:, at:at + 1],
                                                   in1=out, op0=ALU.mult, op1=ALU.add))
                dve.sem_inc(m.emptied, 1)
    m.gates += sum(4 for job in jobs if job[3] in gates)
    m.end(len(tiles))


def stage_diff(nc, m, qT, kT, vals, doT):
    units = [(h, t) for h in range(HEADS) for t in range(TT)]
    with ExitStack() as own:
        sb = lambda name, shape: own.enter_context(nc.sbuf_tensor(name, shape, F32))
        p = sb("diff_p", [P, 2, 2, T])
        aT = sb("diff_aT", [P, TT, T])
        st = sb("diff_st", [P, 2, 8])
        squares = sb("diff_sq", [P, 2, T])
        std = sb("diff_std", [P, T])
        s = Names()
        (s.scores, s.maxed, s.probs, s.mixed, s.turned, s.turned_sb, s.out_ready, s.squares, s.total, s.root,
         s.normed) = (m.sem(f"diff_{x}") for x in ("scores", "maxed", "probs", "mixed", "turned", "turned_sb", "out",
                                                    "squares", "total", "root", "normed"))
        block = own.enter_context(nc.Block(no_gpsimd_drain=True))
        s_bank = lambda u, c: m.bank[2 * (u % 2) + c]
        t_bank, ss_bank = m.bank[4], m.bank[5]
        o_bank = [m.bank[6], m.bank[7]]

        @block.tensor
        def _(pe):
            def scores(u):
                h, t = units[u]
                if u >= 2:
                    pe.wait_ge(s.probs, 2 * (u - 1))
                for c in range(2):
                    mm = pe.matmul(s_bank(u, c)[:, 0:(t + 1) * P], qT[:, 2 * h + c, t * P:(t + 1) * P],
                                   kT[:, 2 * h + c, 0:(t + 1) * P], start=True, stop=True)
                mm.then_inc(s.scores, 1)

            def turn(u):
                h, t = units[u]
                pe.wait_ge(s.mixed, u + 1)
                if u >= 1:
                    pe.wait_ge(s.turned_sb, u)
                for j in range(t + 1):
                    mm = pe.transpose(t_bank[:, j * P:(j + 1) * P], p[:, u % 2, 0, j * P:(j + 1) * P], m.ident)
                mm.then_inc(s.turned, 1)

            def output(h):
                pe.wait_ge(s.turned_sb, TT * (h + 1))
                if h >= 1:
                    pe.wait_ge(s.normed, h)
                for c in range(2):
                    for j in range(TT):
                        mm = pe.matmul(o_bank[c][:, j * P:T], vals[:, j, h * DV + c * P:h * DV + (c + 1) * P],
                                       aT[:, j, j * P:T], start=(j == 0), stop=(j == TT - 1))
                mm.then_inc(s.out_ready, 1)

            def total(h):
                pe.wait_ge(s.squares, 2 * (h + 1))
                if h >= 1:
                    pe.wait_ge(s.root, h)
                for c in range(2):
                    mm = pe.matmul(ss_bank[:, :], m.ones, squares[:, c, :], start=(c == 0), stop=(c == 1))
                mm.then_inc(s.total, 1)

            scores(0)
            for u, (h, t) in enumerate(units):
                if u + 1 < len(units):
                    scores(u + 1)
                if t == 0 and h >= 1:
                    output(h - 1)
                turn(u)
                if t == 1 and h >= 1:
                    total(h - 1)
            output(HEADS - 1)
            total(HEADS - 1)

        @block.scalar
        def _(act):
            def squares_of(h):
                act.wait_ge(s.out_ready, h + 1)
                if h >= 1:
                    act.wait_ge(s.total, h)
                for c in range(2):
                    act.activation(squares[:, c, :], o_bank[c][:, :], ACT.Square).then_inc(s.squares, 1)

            def root_of(h):
                act.wait_ge(s.total, h + 1)
                if h >= 1:
                    act.wait_ge(s.normed, h)
                act.activation(std[:, :], ss_bank[:, :], ACT.Sqrt, bias=m.eps[:, :], scale=1.0 / DV).then_inc(s.root, 1)

            for u, (h, t) in enumerate(units):
                act.wait_ge(s.maxed, u + 1)
                if u >= 2:
                    act.wait_ge(s.mixed, u - 1)
                for c in range(2):
                    act.activation(p[:, u % 2, c, 0:(t + 1) * P], s_bank(u, c)[:, 0:(t + 1) * P], ACT.Exp,
                                   bias=st[:, u % 2, 2 + c:3 + c], scale=ATT_SCALE,
                                   accum_out=st[:, u % 2, 4 + c:5 + c]).then_inc(s.probs, 1)
                act.wait_ge(s.turned, u + 1)
                if t == 0 and h >= 1:
                    act.wait_ge(s.out_ready, h)
                act.activation(aT[:, 0:t + 1, t * P:(t + 1) * P],
                               t_bank[:, 0:(t + 1) * P].rearrange("p (j q) -> p j q", q=P), ACT.Copy).then_inc(s.turned_sb, 1)
                if t == 0 and h >= 1:
                    squares_of(h - 1)
                if t == 2 and h >= 1:
                    root_of(h - 1)
            squares_of(HEADS - 1)
            root_of(HEADS - 1)

        @block.vector
        def _(dve):
            chain = lambda instruction: m.chain(dve, instruction)

            def normed(h):
                dve.wait_ge(s.root, h + 1)
                chain(dve.reciprocal(std[:, :], std[:, :]))
                for c in range(2):
                    last = dve.scalar_tensor_tensor(out=doT[:, 2 * h + c, :], in0=o_bank[c][:, :],
                                                    scalar=m.dn[:, c:c + 1], in1=std[:, :], op0=ALU.mult, op1=ALU.mult)
                last.then_inc(s.normed, 1)

            def softmax_max(u):
                h, t = units[u]
                dve.wait_ge(s.scores, u + 1)
                if u >= 2:
                    dve.wait_ge(s.probs, 2 * (u - 1))
                for c in range(2):
                    bank = s_bank(u, c)
                    link = dve.tensor_tensor(bank[:, t * P:(t + 1) * P], bank[:, t * P:(t + 1) * P], m.causal, ALU.add)
                    if c:
                        chain(link)
                for c in range(2):
                    link = dve.tensor_reduce(st[:, u % 2, c:c + 1], s_bank(u, c)[:, 0:(t + 1) * P], AX.X, ALU.max)
                    if c:
                        chain(link)
                dve.tensor_scalar(st[:, u % 2, 2:4], st[:, u % 2, 0:2], -ATT_SCALE, None, ALU.mult).then_inc(s.maxed, 1)

            softmax_max(0)
            for u, (h, t) in enumerate(units):
                if u + 1 < len(units):
                    softmax_max(u + 1)
                w = (t + 1) * P
                dve.wait_ge(s.probs, 2 * (u + 1))
                chain(dve.reciprocal(st[:, u % 2, 6:8], st[:, u % 2, 4:6]))
                mixed = p[:, u % 2, 0, 0:w]
                dve.tensor_scalar(mixed, mixed, st[:, u % 2, 6:7], None, ALU.mult)
                chain(dve.tensor_scalar(st[:, u % 2, 7:8], st[:, u % 2, 7:8], m.neg_lam[:, :], None, ALU.mult))
                dve.scalar_tensor_tensor(out=mixed, in0=p[:, u % 2, 1, 0:w], scalar=st[:, u % 2, 7:8], in1=mixed,
                                         op0=ALU.mult, op1=ALU.add).then_inc(s.mixed, 1)
                if t == 3 and h >= 1:
                    normed(h - 1)
            normed(HEADS - 1)


def stage_route(nc, m, hT):
    E = EXPERTS
    with ExitStack() as own:
        sb = lambda name, shape, dt=F32: own.enter_context(nc.sbuf_tensor("rt_" + name, shape, dt))
        w_r = sb("w", [P, DC, 36])
        b_r = sb("b", [P, 36])
        logits = sb("logits", [P, TT, 36])
        group = sb("group", [P, TT, 8])
        top = sb("top", [P, TT, 8])
        top_e = sb("top_e", [P, TT, 8])
        where = sb("where", [P, TT, 8], U32)
        where_e = sb("where_e", [P, TT, 8], U32)
        gidx = sb("gidx", [P, TT])
        gexp = sb("gexp", [P, TT, GROUPS])
        gsum = sb("gsum", [P, TT])
        gmask = sb("gmask", [P, TT, GROUPS])
        e_in = sb("e_in", [P, TT, E])
        picked = sb("picked", [P, 2, TT])
        hot = sb("hot", [P, 2, TT, E])
        both = sb("both", [P, TT, E])
        rank = sb("rank", [P, TT, E])
        count = sb("count", [P, E])
        over = sb("over", [P, E])
        scan = sb("scan", [P, 2, E])
        tmp = sb("tmp", [P, TT, E])
        r = sb("r", [P, 2, TT])
        q = sb("q", [P, 2, TT])
        ov = sb("ov", [P, 2, TT])
        one = sb("one", [P, 2, TT])
        dest = sb("dest", [P, 2, TT])
        dest_t = sb("dest_t", [P, 2, TT], U32)
        ids = sb("ids", [P, TT], I32)
        zeros = sb("zeros", [P, BLOCKS], I32)
        whose = sb("whose", [P, 2, 8])
        whose_t = sb("whose_t", [P, 8, E])
        rows = sb("rows", [P, 2, D])
        blank = sb("blank", [P, D])

        loads, lg, bias_done, gx_ready, gx_done, hot_ready, ranked, dest_ready, zeroed, scattered, table = (
            m.sem(f"rt_{x}") for x in ("loads", "lg", "bias", "gx_ready", "gx_done", "hot", "ranked", "dest", "zeroed",
                                       "scattered", "table"))
        turned, rows_ready = m.sem("rt_turned"), m.sem("rt_rows")
        rows_out = [m.sem(f"rt_rows_out{i}") for i in range(2)]
        block = own.enter_context(nc.Block(no_gpsimd_drain=True))
        d = m.dram
        iota = m.const[:, C_IOTA:C_IOTA + P]

        @block.sync
        def _(sp):
            sp.dma_start(w_r[:, :, :], d.w_router).then_inc(loads, 16)
            sp.dma_start(b_r[:, :], d.b_router.to_broadcast([P, 36])).then_inc(loads, 16)
            for t in range(TT):
                sp.wait_ge(rows_ready, 2 * (t + 1))
                sp.dma_start(d.h_rows[t * P:(t + 1) * P, :], rows[:, t % 2, :]).then_inc(rows_out[t % 2], 16)
            for i in range(2):
                sp.wait_ge(rows_out[i], 16 * TT // 2)

        @block.tensor
        def _(pe):
            pe.wait_ge(loads, 32)
            for t in range(TT):
                for k in range(DC):
                    mm = pe.matmul(m.bank[0][:, t * 36:t * 36 + 36], hT[:, k, t * P:(t + 1) * P], w_r[:, k, :],
                                   start=(k == 0), stop=(k == DC - 1))
            mm.then_inc(lg, 1)
            for t in range(TT):
                if t >= 1:
                    pe.wait_ge(rows_ready, 2 * t)
                for k in range(DC):
                    mm = pe.transpose(m.bank[4 + k // 4][:, (k % 4) * P:(k % 4 + 1) * P], hT[:, k, t * P:(t + 1) * P],
                                      m.ident)
                    if k % 4 == 3:
                        mm.then_inc(turned, 1)
            pe.wait_ge(hot_ready, 1)
            for t in range(TT):
                for u in range(t + 1):
                    mm = pe.matmul(m.bank[1][:, t * E:(t + 1) * E], m.before if u == t else m.ones, both[:, u, :],
                                   start=(u == 0), stop=(u == t))
            for u in range(TT):
                mm = pe.matmul(m.bank[2][:, 0:E], m.ones, both[:, u, :], start=(u == 0), stop=(u == TT - 1))
            mm.then_inc(ranked, 1)

        @block.scalar
        def _(act):
            for t in range(TT):
                if t >= 2:
                    act.wait_ge(rows_out[t % 2], 16 * (t // 2))
                for i in range(2):
                    act.wait_ge(turned, 2 * t + i + 1)
                    act.activation(rows[:, t % 2, i * 512:(i + 1) * 512], m.bank[4 + i][:, :], ACT.Copy).then_inc(rows_ready, 1)
            act.wait_ge(gx_ready, 1)
            act.activation(gexp[:, :, :], gexp[:, :, :], ACT.Exp).then_inc(gx_done, 1)
            act.activation(m.pair_w[:, 1, :], m.pair_w[:, 1, :], ACT.Exp).then_inc(gx_done, 1)

        @block.vector
        def _(dve):
            chain = lambda instruction: m.chain(dve, instruction)
            chain(dve.memset(group[:, :, :], LOWEST))
            dve.wait_ge(lg, 1)
            dve.wait_ge(loads, 32)
            chain(dve.tensor_tensor(logits[:, :, :], m.bank[0][:, 0:4 * 36].rearrange("p (t e) -> p t e", e=36),
                                    bcast(b_r[:, :], 1, TT), ALU.add))
            chain(dve.tensor_copy(group[:, :, 0:GROUPS], logits[:, :, 0:GROUPS]))
            for t in range(TT):
                last = dve.max(out=top[:, t, :], in_=group[:, t, :])
            chain(last)
            for t in range(TT):
                last = dve.max_index(where[:, t, :], top[:, t, :], group[:, t, :])
            chain(last)
            chain(dve.tensor_copy(gidx[:, :], where[:, :, 0]))
            chain(dve.tensor_tensor(gmask[:, :, :], bcast(iota[:, 0:GROUPS], 1, TT), bcast(gidx[:, :], 2, GROUPS), ALU.is_equal))
            chain(dve.tensor_scalar(gmask[:, :, :], gmask[:, :, :], 1.0, 1.0e30, ALU.subtract, ALU.mult))
            for t in range(TT):
                last = dve.tensor_tensor(e_in[:, t, :].rearrange("p (g e) -> p g e", g=GROUPS),
                                         logits[:, t, GROUPS:36].rearrange("p (g e) -> p g e", g=GROUPS),
                                         bcast(gmask[:, t, :], 2, E // GROUPS), ALU.add)
            chain(last)
            for t in range(TT):
                last = dve.max(out=top_e[:, t, :], in_=e_in[:, t, :])
            chain(last)
            for t in range(TT):
                last = dve.max_index(where_e[:, t, :], top_e[:, t, :], e_in[:, t, :])
            chain(last)
            chain(dve.tensor_copy(picked[:, :, :], where_e[:, :, 0:2].rearrange("p t k -> p k t")))
            for k in range(2):
                last = dve.tensor_tensor(hot[:, k, :, :], bcast(iota[:, 0:E], 1, TT), bcast(picked[:, k, :], 2, E), ALU.is_equal)
            chain(last)
            chain(dve.tensor_tensor(both[:, :, :], hot[:, 0, :, :], hot[:, 1, :, :], ALU.add))
            dve.sem_inc(hot_ready, 1)
            chain(dve.tensor_tensor(gexp[:, :, :], logits[:, :, 0:GROUPS], bcast(top[:, :, 0], 2, GROUPS), ALU.subtract))
            chain(dve.tensor_tensor(m.pair_w[:, 1, :], top_e[:, :, 1], top_e[:, :, 0], ALU.subtract))
            dve.sem_inc(gx_ready, 1)
            dve.wait_ge(gx_done, 2)
            chain(dve.tensor_reduce(gsum[:, :], gexp[:, :, :], AX.X, ALU.add))
            chain(dve.tensor_scalar(m.pair_w[:, 0, :], m.pair_w[:, 1, :], 1.0, None, ALU.add))
            chain(dve.tensor_tensor(gsum[:, :], gsum[:, :], m.pair_w[:, 0, :], ALU.mult))
            chain(dve.reciprocal(m.pair_w[:, 0, :], gsum[:, :]))
            chain(dve.tensor_tensor(m.pair_w[:, 1, :], m.pair_w[:, 1, :], m.pair_w[:, 0, :], ALU.mult))
            dve.wait_ge(ranked, 1)
            chain(dve.tensor_copy(rank[:, :, :], m.bank[1][:, 0:TT * E].rearrange("p (t e) -> p t e", e=E)))
            chain(dve.tensor_copy(count[:, :], m.bank[2][:, 0:E]))
            chain(dve.tensor_scalar(over[:, :], count[:, :], float(SLOTS), None, ALU.is_gt))
            for b in range(2, T // SLOTS):
                chain(dve.scalar_tensor_tensor(out=over[:, :], in0=count[:, :], scalar=float(SLOTS * b), in1=over[:, :],
                                               op0=ALU.is_gt, op1=ALU.add))
            chain(dve.tensor_copy(scan[:, 0, :], over[:, :]))
            a = 0
            step = 1
            while step < E:
                chain(dve.tensor_copy(scan[:, 1 - a, 0:step], scan[:, a, 0:step]))
                chain(dve.tensor_tensor(scan[:, 1 - a, step:E], scan[:, a, step:E], scan[:, a, 0:E - step], ALU.add))
                a = 1 - a
                step *= 2
            ends = scan[:, a, :]
            chain(dve.tensor_tensor(whose_t[:, :, :], bcast(ends, 1, 8), bcast(iota[:, 0:8], 2, E), ALU.is_le))
            chain(dve.tensor_reduce(whose[:, 0, :], whose_t[:, :, :], AX.X, ALU.add))
            chain(dve.tensor_copy(m.steer[:, 0:OVER], whose[:, 0, 0:OVER]))
            chain(dve.tensor_copy(m.steer[:, OVER:OVER + 1], ends[:, E - 1:E]))
            starts = scan[:, 1 - a, :]
            chain(dve.tensor_tensor(starts, ends, over[:, :], ALU.subtract))
            for k in range(2):
                chain(dve.tensor_tensor(tmp[:, :, :], rank[:, :, :], hot[:, k, :, :], ALU.mult))
                chain(dve.tensor_reduce(r[:, k, :], tmp[:, :, :], AX.X, ALU.add))
                chain(dve.tensor_tensor(tmp[:, :, :], bcast(starts, 1, TT), hot[:, k, :, :], ALU.mult))
                chain(dve.tensor_reduce(ov[:, k, :], tmp[:, :, :], AX.X, ALU.add))
            chain(dve.tensor_scalar(q[:, :, :], r[:, :, :], float(SLOTS), None, ALU.is_ge))
            chain(dve.tensor_scalar(ov[:, :, :], ov[:, :, :], float(E - 1), None, ALU.add))
            chain(dve.tensor_tensor(ov[:, :, :], ov[:, :, :], picked[:, :, :], ALU.subtract))
            chain(dve.tensor_tensor(ov[:, :, :], ov[:, :, :], q[:, :, :], ALU.mult))
            for b in range(2, T // SLOTS):
                chain(dve.scalar_tensor_tensor(out=q[:, :, :], in0=r[:, :, :], scalar=float(SLOTS * b), in1=q[:, :, :],
                                               op0=ALU.is_ge, op1=ALU.add))
            chain(dve.tensor_tensor(ov[:, :, :], ov[:, :, :], picked[:, :, :], ALU.add))
            chain(dve.tensor_tensor(ov[:, :, :], ov[:, :, :], q[:, :, :], ALU.add))
            chain(dve.scalar_tensor_tensor(out=one[:, :, :], in0=q[:, :, :], scalar=-float(SLOTS), in1=r[:, :, :],
                                           op0=ALU.mult, op1=ALU.add))
            chain(dve.scalar_tensor_tensor(out=dest[:, :, :], in0=ov[:, :, :], scalar=float(SLOTS), in1=one[:, :, :],
                                           op0=ALU.mult, op1=ALU.add))
            chain(dve.tensor_copy(m.pair_row[:, :, :], dest[:, :, :]))
            chain(dve.scalar_tensor_tensor(out=dest[:, :, :], in0=one[:, :, :], scalar=float(BLOCKS), in1=ov[:, :, :],
                                           op0=ALU.mult, op1=ALU.add))
            chain(dve.tensor_copy(dest_t[:, :, :], dest[:, :, :]))
            chain(dve.tensor_copy(ids[:, :], m.const[:, C_TOKEN:C_TOKEN + TT]))
            dve.sem_inc(dest_ready, 1)

        @block.gpsimd
        def _(pool):
            own_wait = m.sem("rt_zero_sb")
            pool.memset(zeros[:, :], 0).then_inc(own_wait, 1)
            pool.wait_ge(own_wait, 1)
            pool.dma_start(d.slot_token.rearrange("(p b) o -> p (b o)", b=BLOCKS), zeros[:, :]).then_inc(zeroed, 16)
            pool.memset(blank[:, :], 0.0).then_inc(own_wait, 1)
            pool.wait_ge(own_wait, 2)
            for b in range(EXPERTS, BLOCKS):
                pool.dma_start(d.y_rows[b * SLOTS:(b + 1) * SLOTS, :], blank[:, :]).then_inc(zeroed, 16)
            pool.wait_ge(zeroed, 16 * (1 + BLOCKS - EXPERTS))
            pool.wait_ge(dest_ready, 1)
            for k in range(2):
                for t in range(TT):
                    pool.indirect_dma_start(
                        out=d.slot_token, out_offset=bass.IndirectOffsetOnAxis(ap=dest_t[:, k, t:t + 1], axis=0),
                        in_=ids[:, t:t + 1], in_offset=None).then_inc(scattered, 16)
            pool.wait_ge(scattered, 16 * 2 * TT)
            pool.dma_start(m.tokens[:, :], d.slot_token.rearrange("(p b) o -> p (b o)", b=BLOCKS)).then_inc(table, 16)
            pool.wait_ge(table, 16)


def stage_experts(nc, m):
    F = 512
    turns = EXPERTS // 4
    with ExitStack() as own:
        sb = lambda name, shape: own.enter_context(nc.sbuf_tensor("moe_" + name, shape, F32))
        x = sb("x", [P, 2, D])
        xT = sb("xT", [P, 2, D])
        gate = sb("gate", [P, F])
        hid = sb("hid", [P, F])
        hidT = sb("hidT", [P, F])
        y = sb("y", [P, 2, D])
        x_in = [m.sem(f"moe_x{i}") for i in range(2)]
        y_out = [m.sem(f"moe_y{i}") for i in range(2)]
        xt_mm, xt_sb, gated, hid_ready, hidt_mm, hidt_sb, y_sb = (
            m.sem(f"moe_{v}") for v in ("xt_mm", "xt_sb", "gated", "hid", "hidt_mm", "hidt_sb", "y_sb"))
        block = own.enter_context(nc.Block(no_gpsimd_drain=True))
        d = m.dram
        FIRST = 4 * S_MOE

        @block.sync
        def _(sp):
            load_slabs(m, sp, S_IN2)

        @block.gpsimd
        def _(pool):
            def store(e):
                pool.wait_ge(y_sb, 2 * e + 2)
                pool.dma_start(d.y_rows[e * SLOTS:(e + 1) * SLOTS, :], y[:, e % 2, :]).then_inc(y_out[e % 2], 16)

            for e in range(EXPERTS):
                if e >= 2:
                    pool.wait_ge(xt_mm, 2 * (e - 1))
                pool.indirect_dma_start(
                    out=x[:, e % 2, :], out_offset=None, in_=d.h_rows,
                    in_offset=bass.IndirectOffsetOnAxis(ap=m.tokens[:, e:e + 1], axis=0)).then_inc(x_in[e % 2], 16)
                if e >= 2:
                    store(e - 2)
            store(EXPERTS - 2)
            store(EXPERTS - 1)
            for i in range(2):
                pool.wait_ge(y_out[i], 16 * EXPERTS // 2)

        def expert(pe, e, i, slot):
            def slab(w):
                return (S_MOE + 3 * i + w) % RING

            def arrived(w):
                head = (S_MOE + 3 * i + w) // RING
                pe.wait_ge(m.slab_loaded[slab(w)], turn_slabs(e, i) + 16 * (head + 1))

            arrived(0)
            pe.wait_ge(xt_sb, 2 * e + 2)
            for w in range(2):
                if w == 1:
                    arrived(1)
                for k in range(DC):
                    mm = pe.matmul(m.bank[w][:, :], xT[:, slot, k * P:(k + 1) * P],
                                   m.ring[:, slab(w), k * F:(k + 1) * F], start=(k == 0), stop=(k == DC - 1))
                mm.then_inc(m.products, 4)

        def turn_slabs(e, i):
            return 16 * (3 * (e - i) // RING) if isinstance(e, int) else (e - i) * 12

        @block.tensor
        def _(pe):
            def turn_x(e, slot):
                pe.wait_ge(x_in[slot], 8 * e + 16 - 8 * slot)
                if not isinstance(e, int) or e >= 1:
                    pe.wait_ge(xt_sb, 2 * e)
                for k in range(DC):
                    mm = pe.transpose(m.bank[4 + k // 4][:, (k % 4) * P:(k % 4 + 1) * P],
                                      x[:, slot, k * P:(k + 1) * P], m.ident)
                    if k % 4 == 3:
                        mm.then_inc(xt_mm, 1)

            def second(e, i):
                pe.wait_ge(hid_ready, e + 1)
                for k in range(4):
                    mm = pe.transpose(m.bank[6][:, k * P:(k + 1) * P], hid[:, k * P:(k + 1) * P], m.ident)
                mm.then_inc(hidt_mm, 1)
                w, s = 2, (S_MOE + 3 * i + 2)
                pe.wait_ge(m.slab_loaded[s % RING], turn_slabs(e, i) + 16 * (s // RING + 1))
                pe.wait_ge(hidt_sb, e + 1)
                if not isinstance(e, int) or e >= 1:
                    pe.wait_ge(y_sb, 2 * e)
                for half in range(2):
                    for k in range(4):
                        mm = pe.matmul(m.bank[2 + half][:, :], hidT[:, k * P:(k + 1) * P],
                                       m.ring[:, s % RING, k * D + half * F:k * D + (half + 1) * F],
                                       start=(k == 0), stop=(k == 3))
                    mm.then_inc(m.products, 2)

            turn_x(0, 0)
            for i in range(4):
                expert(pe, i, i, i % 2)
                turn_x(i + 1, (i + 1) % 2)
                second(i, i)
            with pe.Fori(1, turns - 1) as turn:
                for i in range(4):
                    e = turn * 4 + i
                    expert(pe, e, i, i % 2)
                    turn_x(e + 1, (i + 1) % 2)
                    second(e, i)
            for i in range(4):
                e = 4 * (turns - 1) + i
                expert(pe, e, i, i % 2)
                if e + 1 < EXPERTS:
                    turn_x(e + 1, (i + 1) % 2)
                second(e, i)

        @block.scalar
        def _(act):
            def turned(e, slot, guarded):
                for i in range(2):
                    act.wait_ge(xt_mm, 2 * e + i + 1)
                    if i == 0 and guarded:
                        act.wait_ge(m.products, 12 * e + (FIRST - 16))
                    act.activation(xT[:, slot, i * F:(i + 1) * F], m.bank[4 + i][:, :], ACT.Copy).then_inc(xt_sb, 1)

            def middle(e, guarded):
                act.wait_ge(m.products, 12 * e + (FIRST + 4))
                if guarded:
                    act.wait_ge(hid_ready, e)
                act.activation(gate[:, :], m.bank[0][:, :], ACT.Silu).then_inc(gated, 1)

            def hidden(e):
                act.wait_ge(hidt_mm, e + 1)
                act.activation(hidT[:, :], m.bank[6][:, :], ACT.Copy).then_inc(hidt_sb, 1)

            turned(0, 0, False)
            for i in range(4):
                middle(i, i >= 1)
                turned(i + 1, (i + 1) % 2, i >= 1)
                hidden(i)
            with act.Fori(1, turns - 1) as turn:
                for i in range(4):
                    e = turn * 4 + i
                    middle(e, True)
                    turned(e + 1, (i + 1) % 2, True)
                    hidden(e)
            for i in range(4):
                e = 4 * (turns - 1) + i
                middle(e, True)
                if e + 1 < EXPERTS:
                    turned(e + 1, (i + 1) % 2, True)
                hidden(e)

        @block.vector
        def _(dve):
            def one(e, slot, guarded, guard_y):
                dve.wait_ge(gated, e + 1)
                dve.wait_ge(m.products, 12 * e + (FIRST + 8))
                if guarded:
                    dve.wait_ge(hidt_mm, e)
                dve.tensor_tensor(hid[:, :], gate[:, :], m.bank[1][:, :], ALU.mult).then_inc(hid_ready, 1)
                if guard_y:
                    dve.wait_ge(y_out[slot], 8 * e - 8 * slot)
                for half in range(2):
                    dve.wait_ge(m.products, 12 * e + (FIRST + 10 + 2 * half))
                    dve.tensor_copy(y[:, slot, half * F:(half + 1) * F], m.bank[2 + half][:, :]).then_inc(y_sb, 1)

            one(0, 0, False, False)
            one(1, 1, True, False)
            one(2, 0, True, True)
            one(3, 1, True, True)
            with dve.Fori(1, turns) as turn:
                for i in range(4):
                    one(turn * 4 + i, i % 2, True, True)


def stage_combine(nc, m, xT):
    with ExitStack() as own:
        rows = own.enter_context(nc.sbuf_tensor("cmb_rows", [P, 2, 2, D], F32))
        arrived = [m.sem(f"cmb_in{i}") for i in range(2)]
        mixed, turned, added = (m.sem(f"cmb_{v}") for v in ("mixed", "turned", "added"))
        block = own.enter_context(nc.Block(no_gpsimd_drain=True))

        @block.gpsimd
        def _(pool):
            for t in range(TT):
                if t >= 2:
                    pool.wait_ge(turned, 2 * (t - 1))
                for k in range(2):
                    pool.indirect_dma_start(
                        out=rows[:, t % 2, k, :], out_offset=None, in_=m.dram.y_rows,
                        in_offset=bass.IndirectOffsetOnAxis(ap=m.pair_row[:, k, t:t + 1], axis=0)
                    ).then_inc(arrived[t % 2], 16)

        @block.vector
        def _(dve):
            chain = lambda instruction: m.chain(dve, instruction)

            def mix(t):
                dve.wait_ge(arrived[t % 2], 32 * (t // 2 + 1))
                y0, y1 = rows[:, t % 2, 0, :], rows[:, t % 2, 1, :]
                chain(dve.tensor_scalar(y0, y0, m.pair_w[:, 0, t:t + 1], None, ALU.mult))
                dve.scalar_tensor_tensor(out=y0, in0=y1, scalar=m.pair_w[:, 1, t:t + 1], in1=y0,
                                         op0=ALU.mult, op1=ALU.add).then_inc(mixed, 1)

            mix(0)
            for t in range(TT):
                if t + 1 < TT:
                    mix(t + 1)
                for k in range(DC):
                    dve.wait_ge(turned, 2 * t + k // 4 + 1)
                    out = xT[:, k, t * P:(t + 1) * P]
                    dve.scalar_tensor_tensor(out=out, in0=m.bank[2 * (t % 2) + k // 4][:, (k % 4) * P:(k % 4 + 1) * P],
                                             scalar=m.mod[:, 40 + k:41 + k], in1=out, op0=ALU.mult,
                                             op1=ALU.add).then_inc(added, 1)

        @block.tensor
        def _(pe):
            for t in range(TT):
                pe.wait_ge(mixed, t + 1)
                if t >= 2:
                    pe.wait_ge(added, DC * (t - 1))
                for k in range(DC):
                    mm = pe.transpose(m.bank[2 * (t % 2) + k // 4][:, (k % 4) * P:(k % 4 + 1) * P],
                                      rows[:, t % 2, 0, k * P:(k + 1) * P], m.ident)
                    if k % 4 == 3:
                        mm.then_inc(turned, 1)


def stage_in2(nc, m, hT, qT, kT, vals, poolT, d_pool):
    m.begin(S_IN2)
    with ExitStack() as own:
        sb = lambda name, shape: own.enter_context(nc.sbuf_tensor("in2_" + name, shape, F32))
        squares = sb("sq", [P, 2, T])
        std = sb("std", [P, 2, T])
        run = sb("run", [P, 2, T])
        tail = sb("tail", [P, 16])
        sq_ready, total, root, normed = (m.sem(f"in2_{v}") for v in ("sq", "total", "root", "normed"))
        block = own.enter_context(nc.Block(no_gpsimd_drain=True))
        heads = [(S_IN2, j) for j in range(4)] + [(S_IN2 + 2, 0)]

        @block.sync
        def _(sp):
            load_halves(m, sp, S_IN2 + 2, S_IN2 + 5)

        @block.gpsimd
        def _(pool):
            for s in range(S_IN2 + 1, S_IN2 + 4):
                pool_low(m, pool, s, s % 2)

        @block.tensor
        def _(pe):
            def norm(n):
                pe.wait_ge(sq_ready, n + 1)
                if n >= 2:
                    pe.wait_ge(root, n - 1)
                pe.matmul(m.bank[4 + n % 2][:, :], m.halves, squares[:, n % 2, :], start=True, stop=True).then_inc(total, 1)

            pe_features_split(m, pe, S_IN2, hT)
            for n in range(4):
                norm(n)
            pe_features_split(m, pe, S_IN2 + 1, hT)
            pe_features_split(m, pe, S_IN2 + 2, hT, tiles=1)
            norm(4)
            slot = (S_IN2 + 2) % 2
            pe.wait_ge(m.lows, split_number(S_IN2 + 3))
            m.wait_bank(pe, S_IN2 + 2, 1)
            for t in range(TT):
                for k in range(DC):
                    tok, at = slice(t * P, (t + 1) * P), slice(D + k * P, D + (k + 1) * P)
                    mm = three_passes(pe, m.bank[1][:, tok], [hT[0][:, k, tok], hT[1][:, k, tok]],
                                      [m.high[:, slot, at], m.low[:, slot, at]], k == 0, k == DC - 1)
            mm.then_inc(m.products, 3)

        @block.scalar
        def _(act):
            for n, (s, j) in enumerate(heads):
                if n == 4:
                    for s1 in (S_IN2 + 2, S_IN2 + 3):
                        for j1 in range(4):
                            act_high(m, act, s1, j1, s1 % 2)
                m.wait_product(act, s, j)
                if n >= 2:
                    act.wait_ge(total, n - 1)
                act.activation(squares[:, n % 2, :], m.bank[j][:, :], ACT.Square).then_inc(sq_ready, 1)
                if n < 4:
                    act_high(m, act, S_IN2 + 1, n, (S_IN2 + 1) % 2)
                act.wait_ge(total, n + 1)
                if n >= 2:
                    act.wait_ge(normed, n - 1)
                act.activation(std[:, n % 2, :], m.bank[4 + n % 2][:, :], ACT.Sqrt, bias=m.eps[:, :],
                               scale=1.0 / HD).then_inc(root, 1)
            act.wait_ge(m.products, 4 * (S_IN2 + 3))
            act.activation(vals[:, :, :], m.bank[1][:, :].rearrange("p (t n) -> p t n", n=P), ACT.Copy)

        @block.vector
        def _(dve):
            chain = lambda instruction: m.chain(dve, instruction)

            def head(n, dst, gain):
                s, j = heads[n]
                dve.wait_ge(root, n + 1)
                chain(dve.reciprocal(std[:, n % 2, :], std[:, n % 2, :]))
                chain(dve.scalar_tensor_tensor(out=dst, in0=m.bank[j][:, :], scalar=gain, in1=std[:, n % 2, :],
                                               op0=ALU.mult, op1=ALU.mult))
                dve.sem_inc(normed, 1)
                dve.sem_inc(m.emptied, 1)

            chain(dve.tensor_scalar(m.small[:, 0:1], m.small[:, 0:1], float(HD) ** -0.5, None, ALU.mult))
            for n in range(4):
                head(n, qT[:, n, :], m.small[:, 0:1])
            for g in range(4):
                m.wait_product(dve, S_IN2 + 1, g)
                chain(dve.tensor_copy(poolT[:, g, :], m.bank[g][:, :]))
                dve.sem_inc(m.emptied, 1)
            head(4, kT[:, :], m.small[:, 1:2])
            for g in range(4):
                window = 2 << g
                src = poolT[:, g, :]
                step = 1
                a = 0
                while step < window:
                    chain(dve.tensor_copy(run[:, a, 0:step], src[:, 0:step]))
                    chain(dve.tensor_tensor(run[:, a, step:T], src[:, step:T], src[:, 0:T - step], ALU.add))
                    src = run[:, a, :]
                    a = 1 - a
                    step *= 2
                chain(dve.scalar_tensor_tensor(out=d_pool[:, g, :], in0=src, scalar=1.0 / window, in1=poolT[:, g, :],
                                               op0=ALU.mult, op1=ALU.subtract))
                chain(dve.tensor_tensor(tail[:, :], src[:, 0:16], m.const[:, C_COUNT + 16 * g:C_COUNT + 16 * (g + 1)], ALU.mult))
                chain(dve.tensor_tensor(d_pool[:, g, 0:16], tail[:, :], poolT[:, g, 0:16], ALU.subtract))
    m.end(9)


def stage_window(nc, m, qT, kT, vals, d_pool, cat):
    with ExitStack() as own:
        sb = lambda name, shape: own.enter_context(nc.sbuf_tensor("swa_" + name, shape, F32))
        H = SWA_HEADS
        bias = sb("bias", [P, H, BAND])
        sc = sb("sc", [P, H, BAND])
        pT = sb("pT", [P, 2 * H, P])
        mx = sb("mx", [P, H])
        es = sb("es", [P, H])
        den = sb("den", [P, H])
        pool_w = sb("pool_w", [P, 4, P])
        loads, scores, shifted, exped, probs, turned, turned_sb, out_ready, out_sb, sinks_e, pooled, scored = (
            m.sem(f"swa_{v}") for v in ("loads", "scores", "shifted", "exped", "probs", "turned", "turned_sb", "out",
                                        "out_sb", "sinks", "pooled", "scored"))
        block = own.enter_context(nc.Block(no_gpsimd_drain=True))
        d = m.dram

        @block.sync
        def _(sp):
            for h in range(H):
                sp.dma_start(bias[:, h, :], d.bias_band[h]).then_inc(loads, 16)
            sp.dma_start(pool_w[:, :, :], d.pool_w).then_inc(loads, 16)
            sp.wait_ge(loads, 16 * (H + 1))

        def first_key(t):
            return P if t == 0 else 0

        @block.tensor
        def _(pe):
            pe.wait_ge(loads, 16 * (H + 1))
            for g in range(4):
                mm = pe.matmul(m.bank[g][:, :], pool_w[:, g, :], d_pool[:, g, :], start=True, stop=True)
            mm.then_inc(pooled, 1)
            pe.wait_ge(out_sb, 1)
            for t in range(TT):
                lo = first_key(t)
                if t >= 1:
                    pe.wait_ge(scored, t)
                    pe.wait_ge(out_sb, t + 1)
                for h in range(H):
                    r = HD * (h // 4)
                    mm = pe.matmul(m.bank[h // 2][:, (h % 2) * BAND + lo:(h % 2 + 1) * BAND],
                                   qT[r:r + HD, h % 4, t * P:(t + 1) * P],
                                   kT[r:r + HD, (t - 1) * P + lo:(t + 1) * P], start=True, stop=True)
                mm.then_inc(scores, 1)
                pe.wait_ge(probs, t + 1)
                if t >= 1:
                    pe.wait_ge(turned_sb, t)
                for h in range(H):
                    for b in range(lo // P, 2):
                        i = 2 * h + b
                        mm = pe.transpose(m.bank[4 + i // 4][:, (i % 4) * P:(i % 4 + 1) * P],
                                          sc[:, h, b * P:(b + 1) * P], m.ident)
                mm.then_inc(turned, 1)
                pe.wait_ge(turned_sb, t + 1)
                for h in range(H):
                    r = HD * (h // 4)
                    for b in range(lo // P, 2):
                        mm = pe.matmul(m.bank[0][r:r + HD, (h % 4) * P:(h % 4 + 1) * P],
                                       vals[:, t - 1 + b, r:r + HD], pT[:, 2 * h + b, :],
                                       start=(b == lo // P), stop=(b == 1))
                mm.then_inc(out_ready, 1)

        @block.scalar
        def _(act):
            for t in range(TT):
                lo = first_key(t)
                act.wait_ge(shifted, t + 1)
                act.activation(sc[:, :, lo:], sc[:, :, lo:], ACT.Exp).then_inc(exped, 1)
                act.activation(es[:, :], es[:, :], ACT.Exp).then_inc(exped, 1)
                act.wait_ge(turned, t + 1)
                if t >= 1:
                    act.wait_ge(out_ready, t)
                act.activation(pT[:, :, :].rearrange("p (h b) q -> p h b q", b=2)[:, :, lo // P:, :],
                               m.psum[:, 4:8, :].rearrange("p k (h b q) -> p (k h) b q", b=2, q=P)[:, :, lo // P:, :],
                               ACT.Copy).then_inc(turned_sb, 1)

        @block.vector
        def _(dve):
            chain = lambda instruction: m.chain(dve, instruction)
            dve.wait_ge(pooled, 1)
            for g in range(4):
                last = dve.tensor_scalar(cat[:, 4 + g, :], m.bank[g][:, :], m.small[:, 2 + g:3 + g], None, ALU.mult)
            last.then_inc(out_sb, 1)
            dve.wait_ge(loads, 16 * (H + 1))
            chain(dve.tensor_tensor(bias[:, :, :], bias[:, :, :],
                                    bcast(m.const[:, C_MASK:C_MASK + BAND], 1, H), ALU.add))
            for t in range(TT):
                lo = first_key(t)
                w = BAND - lo
                dve.wait_ge(scores, t + 1)
                if t >= 1:
                    dve.wait_ge(turned, t)
                chain(dve.tensor_tensor(sc[:, :, lo:],
                                        m.psum[:, 0:4, :].rearrange("p k (h j) -> p (k h) j", j=BAND)[:, :, lo:],
                                        bias[:, :, lo:], ALU.add))
                dve.sem_inc(scored, 1)
                chain(dve.tensor_reduce(mx[:, :], sc[:, :, lo:], AX.X, ALU.max))
                chain(dve.tensor_tensor(mx[:, :], mx[:, :], m.sinks[:, :], ALU.max))
                dve.tensor_tensor(sc[:, :, lo:], sc[:, :, lo:], bcast(mx[:, :], 2, w), ALU.subtract)
                dve.tensor_tensor(es[:, :], m.sinks[:, :], mx[:, :], ALU.subtract).then_inc(shifted, 1)
                dve.wait_ge(exped, 2 * (t + 1))
                chain(dve.tensor_reduce(den[:, :], sc[:, :, lo:], AX.X, ALU.add))
                chain(dve.tensor_tensor(den[:, :], den[:, :], es[:, :], ALU.add))
                chain(dve.reciprocal(den[:, :], den[:, :]))
                dve.tensor_tensor(sc[:, :, lo:], sc[:, :, lo:], bcast(den[:, :], 2, w), ALU.mult).then_inc(probs, 1)
                dve.wait_ge(out_ready, t + 1)
                dve.tensor_copy(cat[:, 0:4, t * P:(t + 1) * P],
                                m.bank[0][:, :].rearrange("p (h q) -> p h q", q=P)).then_inc(out_sb, 1)


def stage_peer_u(nc, m, hT, xT):
    H, K = PH, TOPK
    HALF = PK // 8
    NB = 64
    with ExitStack() as own:
        sb = lambda name, shape, dt=F32: own.enter_context(nc.sbuf_tensor("pu_" + name, shape, dt))
        gl = xT[:, 0:4, :].rearrange("p (a c) t -> p a c t", a=2)
        hot1 = xT[:, 4:6, :].rearrange("p a (c k) -> p (a c) k", k=PK)
        hot2 = xT[:, 6:8, :].rearrange("p a (c k) -> p (a c) k", k=PK)
        e_turned = sb("e_turned", [P, 3, T])
        iota = m.const[:, C_IOTA:C_IOTA + P]
        loads, scored, score_sb, picked, turned, turned_sb, act_ready, act_out = (
            m.sem(f"pu_{v}") for v in ("loads", "scored", "score_sb", "picked", "turned", "turned_sb", "act", "act_out"))
        gl_out = [m.sem(f"pu_gl{i}") for i in range(2)]
        x_out = m.sem("pu_x_out")
        d = m.dram
        first = 4 * S_U

        def u_chunk(pe, slot, j):
            for k in range(DC):
                at = slice((j * DC + k) * P, (j * DC + k + 1) * P)
                mm = three_passes(pe, m.bank[j % 2][:, :], [m.high[:, slot, at], m.low[:, slot, at]],
                                  [hT[0][:, k, :], hT[1][:, k, :]], k == 0, k == DC - 1)
            mm.then_inc(m.products, 1)

        with ExitStack() as half:
            hb = lambda name, shape, dt=F32: half.enter_context(nc.sbuf_tensor("pk_" + name, shape, dt))
            qT = hb("q", [P, 2 * H, T])
            stage_linear_split(nc, m, "wq", [(S_WQ + i, hT, "copy", qT, 4 * i) for i in range(4)])
            subkeys = hb("subkeys", [P, 2 * H, PK])
            sc = hb("sc", [P, 2 * H, PK])
            sc2 = hb("sc2", [P, 2 * H, PK])
            val = hb("val", [P, 2 * H, K])
            idx = hb("idx", [P, 2 * H, K], U32)
            idf = hb("idf", [P, 2 * H, K])
            best = hb("best", [P, H, K])
            pos = hb("pos", [P, H, K], U32)
            part = hb("part", [P, H, K], U32)
            partf = hb("partf", [P, 2, H, K])
            res = hb("res", [P, 3, H, K])
            gs = hb("gs", [P, H])
            exp_ready, exp_done = m.sem("pk_exp_ready"), m.sem("pk_exp_done")
            block = half.enter_context(nc.Block(no_gpsimd_drain=True))

            @block.sync
            def _(sp):
                sp.dma_start(d.x_rows, xT[:, :, :]).then_inc(x_out, 16)
                sp.dma_start(subkeys[:, :, :], d.subkeys).then_inc(loads, 16)
                load_halves(m, sp, S_U + 2, S_U + HALF + 2)
                sp.wait_ge(x_out, 16)

            @block.gpsimd
            def _(pool):
                with pool.Fori(S_U + 1, S_U + HALF + 1, 2) as s:
                    pool_low(m, pool, s, (S_U + 1) % 2)
                    pool_low(m, pool, s + 1, S_U % 2)

            @block.tensor
            def _(pe):
                pe.wait_ge(loads, 16)

                def scores(t):
                    if t >= 1:
                        pe.wait_ge(score_sb, t)
                    for n in range(2 * H):
                        mm = pe.matmul(m.bank[2 + n // 4][:, (n % 4) * PK:(n % 4 + 1) * PK], qT[:, n, t * P:(t + 1) * P],
                                       subkeys[:, n, :], start=True, stop=True)
                    mm.then_inc(scored, 1)

                def turn(t):
                    pe.wait_ge(picked, t + 1)
                    if t >= 1:
                        pe.wait_ge(turned_sb, t)
                    for i in range(3):
                        mm = pe.transpose(m.bank[6][:, i * P:(i + 1) * P], res[:, i, :, :].rearrange("p h k -> p (h k)"), m.ident)
                    mm.then_inc(turned, 1)

                def u_slab(s, chunk):
                    for j in range(4):
                        pe.wait_ge(m.lows, split_number(s) + j + 1)
                        if chunk + j >= 2:
                            pe.wait_ge(act_ready, chunk + j - 1)
                        u_chunk(pe, s % 2, j)

                scores(0)
                for n in range(HALF):
                    u_slab(S_U + n, n * 4)
                    if n % 4 == 3 and n < HALF - 1 and n // 4 + 1 < TT:
                        turn(n // 4)
                        scores(n // 4 + 1)
                turn(TT - 1)

            def gelu_slab(act, n):
                if n == 0:
                    act.wait_ge(x_out, 16)
                for j in range(4):
                    act_high(m, act, S_U + n + 1, j, (S_U + n + 1) % 2)
                    act.wait_ge(m.products, 4 * n + (first + j + 1))
                    if n >= 1 and j % 2 == 0:
                        act.wait_ge(gl_out[j // 2], 16 * n)
                    act.activation(gl[:, j // 2, j % 2, :], m.bank[j % 2][:, :], ACT.Gelu).then_inc(act_ready, 1)
                    if j % 2 == 1:
                        act.wait_ge(act_ready, 4 * n + j + 1)
                        act.dma_start(d.gelu[n][:, j - 1:j + 1, :], gl[:, j // 2, :, :]).then_inc(gl_out[j // 2], 16)

            @block.scalar
            def _(act):
                for n in range(HALF):
                    if n % 4 == 0:
                        t = n // 4
                        act.wait_ge(scored, t + 1)
                        if t >= 1:
                            act.wait_ge(picked, t)
                        act.activation(sc[:, :, :], m.psum[:, 2:6, :].rearrange("p b (n k) -> p (b n) k", k=PK),
                                       ACT.Copy).then_inc(score_sb, 1)
                    gelu_slab(act, n)
                    if n % 4 == 2:
                        t = n // 4
                        act.wait_ge(exp_ready, t + 1)
                        act.activation(best[:, :, :], best[:, :, :], ACT.Exp).then_inc(exp_done, 1)
                    if n % 4 == 3:
                        t = n // 4
                        act.wait_ge(turned, t + 1)
                        act.activation(e_turned[:, :, t * P:(t + 1) * P],
                                       m.bank[6][:, 0:3 * P].rearrange("p (i q) -> p i q", q=P), ACT.Copy).then_inc(turned_sb, 1)

            @block.vector
            def _(dve):
                chain = lambda instruction: m.chain(dve, instruction)

                def top16(n, source, spare, values, places):
                    for i in range(n):
                        last = dve.max(out=values[:, i, 0:8], in_=source(i))
                    chain(last)
                    for i in range(n):
                        dve.max_index(places[:, i, 0:8], values[:, i, 0:8], source(i))
                        last = dve.match_replace(out=spare(i), in_to_replace=values[:, i, 0:8], in_values=source(i),
                                                 imm_value=LOWEST)
                    chain(last)
                    for i in range(n):
                        last = dve.max(out=values[:, i, 8:16], in_=spare(i))
                    chain(last)
                    for i in range(n):
                        last = dve.max_index(places[:, i, 8:16], values[:, i, 8:16], spare(i))
                    chain(last)

                for t in range(TT):
                    dve.wait_ge(score_sb, t + 1)
                    top16(2 * H, lambda i: sc[:, i, :], lambda i: sc2[:, i, :], val, idx)
                    chain(dve.tensor_copy(idf[:, :, :], idx[:, :, :]))
                    cand = sc[:, :, :].rearrange("p (h a) k -> p h (a k)", a=2)
                    cand2 = sc2[:, :, :].rearrange("p (h a) k -> p h (a k)", a=2)
                    for h in range(H):
                        last = dve.tensor_tensor(cand[:, h, :].rearrange("p (i j) -> p i j", j=K),
                                                 bcast(val[:, 2 * h, :], 2, K), bcast(val[:, 2 * h + 1, :], 1, K), ALU.add)
                    chain(last)
                    top16(H, lambda i: cand[:, i, :], lambda i: cand2[:, i, :], best, pos)
                    chain(dve.tensor_scalar(part[:, :, :], pos[:, :, :], 4, None, ALU.logical_shift_right))
                    chain(dve.tensor_copy(partf[:, 0, :, :], part[:, :, :]))
                    chain(dve.tensor_scalar(part[:, :, :], pos[:, :, :], 15, None, ALU.bitwise_and))
                    chain(dve.tensor_copy(partf[:, 1, :, :], part[:, :, :]))
                    pick = sc[:, :, :].rearrange("p (h a) k -> p h (a k)", a=2)
                    for which in range(2):
                        for h in range(H):
                            last = dve.tensor_tensor(pick[:, h, :].rearrange("p (i j) -> p i j", j=K),
                                                     bcast(partf[:, which, h, :], 2, K), bcast(iota[:, 0:K], 1, K), ALU.is_equal)
                        chain(last)
                        for h in range(H):
                            one = pick[:, h, :].rearrange("p (i j) -> p i j", j=K)
                            last = dve.tensor_tensor(one, one, bcast(idf[:, 2 * h + which, :], 1, K), ALU.mult)
                        chain(last)
                        if which == 0 and t >= 1:
                            dve.wait_ge(turned, t)
                        chain(dve.tensor_reduce(res[:, which, :, :], pick[:, :, :].rearrange("p h (i j) -> p h i j", j=K),
                                                AX.X, ALU.add))
                    chain(dve.tensor_copy(gs[:, :], best[:, :, 0]))
                    chain(dve.tensor_tensor(best[:, :, :], best[:, :, :], bcast(gs[:, :], 2, K), ALU.subtract))
                    dve.sem_inc(exp_ready, 1)
                    dve.wait_ge(exp_done, t + 1)
                    chain(dve.tensor_reduce(gs[:, :], best[:, :, :], AX.X, ALU.add))
                    chain(dve.reciprocal(gs[:, :], gs[:, :]))
                    dve.tensor_tensor(res[:, 2, :, :], best[:, :, :], bcast(gs[:, :], 2, K), ALU.mult).then_inc(picked, 1)

        with ExitStack() as half:
            hb = lambda name, shape, dt=F32: half.enter_context(nc.sbuf_tensor("pg_" + name, shape, dt))
            table = hb("table", [P, 2, PK, NB])
            hot_ready, gates_mm, gates_sb = (m.sem(f"pg_{v}") for v in ("hot", "mm", "sb"))
            table_out = [m.sem(f"pg_out{i}") for i in range(2)]
            block = half.enter_context(nc.Block(no_gpsimd_drain=True))
            QUADS = T // 4
            STEPS = QUADS // (4 * HALF)
            assert STEPS * 4 * HALF == QUADS and NB % 32 == 0
            turns = HALF // 4

            @block.sync
            def _(sp):
                load_halves(m, sp, S_U + HALF + 2, S_V + 2)

            @block.gpsimd
            def _(pool):
                with pool.Fori(S_U + HALF + 1, S_V + 1, 2) as s:
                    pool_low(m, pool, s, (S_U + 1) % 2)
                    pool_low(m, pool, s + 1, S_U % 2)
                for i in range(2):
                    pool.wait_ge(gl_out[i], 16 * 2 * HALF)

            @block.tensor
            def _(pe):
                with pe.Fori(0, turns) as turn:
                    for i in range(4):
                        n = turn * 4 + (HALF + i)
                        for j in range(4):
                            pe.wait_ge(m.lows, n * 4 + (split_number(S_U) + j + 1))
                            pe.wait_ge(act_ready, n * 4 + (j - 1))
                            u_chunk(pe, (S_U + i) % 2, j)
                            for b in range(STEPS):
                                at = (4 * i + j) * STEPS + b
                                quad = turn * (16 * STEPS) + at
                                pe.wait_ge(hot_ready, quad + 1)
                                pe.wait_ge(gates_sb, quad + 1)
                                for c in range(4):
                                    mm = pe.matmul(m.bank[4 + at % 4][:, c * PK:(c + 1) * PK], hot2[:, 4 * (at % 2) + c, :],
                                                   hot1[:, 4 * (at % 2) + c, :], start=True, stop=True)
                                mm.then_inc(gates_mm, 1)

            @block.vector
            def _(dve):
                dve.sem_inc(gates_mm, 2)
                dve.sem_inc(gates_sb, 4)
                for i in range(2):
                    dve.sem_inc(table_out[i], 16)
                with dve.Fori(0, turns) as turn:
                    for at in range(16 * STEPS):
                        quad = turn * (16 * STEPS) + at
                        dve.wait_ge(gates_mm, quad + 1)
                        for c in range(4):
                            token = turn * (64 * STEPS) + (4 * at + c)
                            dve.tensor_scalar(hot2[:, 4 * (at % 2) + c, :], iota, e_turned[:, 1, bass.ds(token, 1)],
                                              None, ALU.is_equal)
                            last = dve.tensor_scalar(hot1[:, 4 * (at % 2) + c, :], iota, e_turned[:, 0, bass.ds(token, 1)],
                                                     e_turned[:, 2, bass.ds(token, 1)], ALU.is_equal, ALU.mult)
                        last.then_inc(hot_ready, 1)

            @block.scalar
            def _(act):
                parts = 16 * STEPS // (NB // 4)
                with act.Fori(0, turns) as turn:
                    for i in range(4):
                        n = turn * 4 + (HALF + i)
                        for j in range(4):
                            act_high(m, act, n + (S_U + 1), j, (S_U + i + 1) % 2)
                            act.wait_ge(m.products, 4 * n + (first + j + 1))
                            if j % 2 == 0:
                                act.wait_ge(gl_out[j // 2], 16 * n)
                            act.activation(gl[:, j // 2, j % 2, :], m.bank[j % 2][:, :], ACT.Gelu).then_inc(act_ready, 1)
                            if j % 2 == 1:
                                act.wait_ge(act_ready, 4 * n + (j + 1))
                                act.dma_start(d.gelu[bass.ds(n, 1)].rearrange("o p c t -> (o p) c t")[:, j - 1:j + 1, :],
                                              gl[:, j // 2, :, :]).then_inc(gl_out[j // 2], 16)
                            for b in range(STEPS):
                                at = (4 * i + j) * STEPS + b
                                quad = turn * (16 * STEPS) + at
                                part = at // (NB // 4)
                                q = at % (NB // 4)
                                if q == 0:
                                    act.wait_ge(table_out[part % 2], (turn * parts + (part - part % 2)) * 8 + 16)
                                act.wait_ge(gates_mm, quad + 3)
                                act.activation(table[:, part % 2, :, 4 * q:4 * q + 4].rearrange("p e c -> p c e"),
                                               m.bank[4 + at % 4][:, :].rearrange("p (c e) -> p c e", e=PK),
                                               ACT.Copy).then_inc(gates_sb, 1)
                                if q == NB // 4 - 1:
                                    act.wait_ge(gates_sb, quad + 5)
                                    t0 = (turn * parts + part) * NB
                                    act.dma_start(d.gates[:, :, bass.ds(t0, NB)], table[:, part % 2, :, :]).then_inc(table_out[part % 2], 16)
                for i in range(2):
                    act.wait_ge(table_out[i], 16 + 16 * turns * parts // 2)


def stage_peer_v(nc, m, h, xT):
    with ExitStack() as own:
        sb = lambda name, shape, dt=F32: own.enter_context(nc.sbuf_tensor("pv_" + name, shape, dt))
        gl = sb("gl", [P, 2, 4, T])
        gt = sb("gt", [P, 2, 4, T])
        coef = sb("coef", [P, 2, 4, T])
        coef_high, coef_low = (part[:, :, :].rearrange("p (a c) t -> p a c t", a=2) for part in h)
        zero = sb("zero", [P, T])
        gl_in = [m.sem(f"pv_gl{i}") for i in range(2)]
        gt_in = [m.sem(f"pv_gt{i}") for i in range(2)]
        x_in, zeroed, coef_ready, high_ready, low_ready, out_ready, done, stored = (
            m.sem(f"pv_{v}") for v in ("x_in", "zeroed", "coef", "high", "low", "out", "done", "stored"))
        block = own.enter_context(nc.Block(no_gpsimd_drain=True))
        N = PK // 4
        d = m.dram
        FIRST = 4 * S_V

        @block.sync
        def _(sp):
            sp.dma_start(xT[:, :, :], d.x_rows).then_inc(x_in, 16)
            load_halves(m, sp, S_V + 2, S_END)
            for k in range(DC):
                sp.wait_ge(done, k + 1)
                sp.dma_start(d.out[:, k, :], xT[:, k, :]).then_inc(stored, 16)
            sp.wait_ge(stored, 16 * DC)

        @block.gpsimd
        def _(pool):
            with pool.Fori(S_V + 1, S_END - 1, 2) as s:
                pool_low(m, pool, s, (S_V + 1) % 2)
                pool_low(m, pool, s + 1, S_V % 2)
            pool_low(m, pool, S_END - 1, (S_END - 1) % 2)

        @block.scalar
        def _(act):
            def one(n, i, ahead=True):
                act.wait_ge(coef_ready, 4 * n + 4)
                gl_src = d.gelu[n] if isinstance(n, int) else d.gelu[bass.ds(n, 1)].rearrange("o p c t -> (o p) c t")
                act.dma_start(gl[:, i, :, :], gl_src).then_inc(gl_in[i], 16)
                act.dma_start(gt[:, i, :, :], d.gates[:, bass.ds(n * 4, 4), :]).then_inc(gt_in[i], 16)

            def highs(n, i):
                for j in range(4):
                    act.wait_ge(coef_ready, 4 * n + (j + 9))
                    if j == 0 and (not isinstance(n, int) or n >= 2):
                        act.wait_ge(m.products, 4 * n + (FIRST - 4))
                    act.activation(coef_high[:, i, j, :], coef[:, i, j, :], ACT.Copy).then_inc(high_ready, 1)

            def slab(n, i):
                for j in range(4):
                    act_high(m, act, n + (S_V + 1), j, (S_V + i + 1) % 2)

            one(0, 0)
            one(1, 1)
            highs(0, 0)
            slab(0, 0)
            one(2, 0)
            highs(1, 1)
            slab(1, 1)
            with act.Fori(2, N - 2, 2) as n:
                one(n + 1, 1)
                highs(n, 0)
                slab(n, 0)
                one(n + 2, 0)
                highs(n + 1, 1)
                slab(n + 1, 1)
            one(N - 1, 1)
            highs(N - 2, 0)
            slab(N - 2, 0)
            highs(N - 1, 1)

        @block.vector
        def _(dve):
            dve.memset(zero[:, :], 0.0).then_inc(zeroed, 1)
            dve.sem_inc(coef_ready, 8)

            def product(n, i):
                dve.wait_ge(gl_in[i], n * 8 + (16 - 8 * i))
                dve.wait_ge(gt_in[i], n * 8 + (16 - 8 * i))
                for j in range(4):
                    if not isinstance(n, int) or n >= 2:
                        dve.wait_ge(low_ready, 4 * n + (j - 7))
                    dve.tensor_tensor(coef[:, i, j, :], gl[:, i, j, :], gt[:, i, j, :], ALU.mult).then_inc(coef_ready, 1)

            def lows(n, i):
                for j in range(4):
                    dve.wait_ge(high_ready, 4 * n + (j + 1))
                    dve.tensor_tensor(coef_low[:, i, j, :], coef[:, i, j, :], coef_high[:, i, j, :].bitcast(F32),
                                      ALU.subtract).then_inc(low_ready, 1)

            product(0, 0)
            product(1, 1)
            lows(0, 0)
            lows(1, 1)
            with dve.Fori(2, N, 2) as n:
                product(n, 0)
                product(n + 1, 1)
                lows(n, 0)
                lows(n + 1, 1)
            dve.wait_ge(x_in, 16)
            for k in range(DC):
                dve.wait_ge(out_ready, k + 1)
                dve.tensor_tensor(xT[:, k, :], m.bank[k][:, :], xT[:, k, :], ALU.add).then_inc(done, 1)

        @block.tensor
        def _(pe):
            pe.wait_ge(zeroed, 1)
            for k in range(DC):
                pe.matmul(m.bank[k][:, :], zero[:, 0:P], zero[:, :], start=True, stop=False)
            with pe.Fori(0, N, 2) as pair:
                for i in range(2):
                    n = pair + i
                    for j in range(4):
                        pe.wait_ge(m.lows, n * 4 + (split_number(S_V) + j + 1))
                        pe.wait_ge(low_ready, n * 4 + (j + 1))
                        for k in range(DC):
                            at = slice(j * D + k * P, j * D + (k + 1) * P)
                            mm = three_passes(pe, m.bank[k][:, :], [m.high[:, (S_V + i) % 2, at], m.low[:, (S_V + i) % 2, at]],
                                              [coef_high[:, i, j, :], coef_low[:, i, j, :]], False, False)
                        mm.then_inc(m.products, 1)
            for k in range(DC):
                pe.matmul(m.bank[k][:, :], zero[:, 0:P], zero[:, :], start=False, stop=True).then_inc(out_ready, 1)


def stage_overflow(nc, m):
    F = 512
    with ExitStack() as own:
        sb = lambda name, shape, dt=F32: own.enter_context(nc.sbuf_tensor("ov_" + name, shape, dt))
        w = sb("w", [P, 3, SLAB])
        x = sb("x", [P, D])
        xT = sb("xT", [P, D])
        gate = sb("gate", [P, F])
        hid = sb("hid", [P, F])
        hidT = sb("hidT", [P, F])
        y = sb("y", [P, D])
        ids = sb("ids", [P, 1], I32)
        w_in, ids_ready, x_in, xt_mm, xt_sb, gu, gated, hid_ready, hidt_mm, hidt_sb, y_mm, y_sb, y_out = (
            m.sem(f"ov_{v}") for v in ("w", "ids", "x", "xt_mm", "xt_sb", "gu", "gated", "hid", "hidt_mm", "hidt_sb",
                                       "y_mm", "y_sb", "y_out"))
        carrier = m.sem("ov_carrier")
        block = own.enter_context(nc.Block(no_gpsimd_drain=True))
        d = m.dram

        def each(engine, body):
            number = engine.value_load(m.steer[0:1, OVER:OVER + 1], min_val=0, max_val=OVER)
            with engine.Fori(0, OVER) as b:
                with engine.If(b < number):
                    body(b)

        @block.sync
        def _(sp):
            sp.sem_inc(y_out, 16)

            def body(b):
                e = sp.value_load(m.steer[0:1, bass.ds(b, 1)], min_val=0, max_val=EXPERTS - 1)
                for i in range(3):
                    sp.dma_start(w[:, i, :], m.weights[bass.ds(e * 3 + (S_MOE + i), 1)].rearrange("a p n -> (a p) n")
                                 ).then_inc(w_in, 16)
                sp.wait_ge(y_sb, b * 2 + 2)
                sp.dma_start(d.y_rows[bass.ds(b * SLOTS + EXPERTS * SLOTS, SLOTS), :], y[:, :]).then_inc(y_out, 16)
                sp.wait_ge(y_out, b * 16 + 32)
                sp.sem_inc(carrier, 1)
            each(sp, body)

        @block.gpsimd
        def _(pool):
            def body(b):
                pool.wait_ge(ids_ready, b + 1)
                pool.sem_inc(carrier, 1)
                pool.indirect_dma_start(out=x[:, :], out_offset=None, in_=d.h_rows,
                                        in_offset=bass.IndirectOffsetOnAxis(ap=ids[:, 0:1], axis=0)).then_inc(x_in, 16)
                pool.wait_ge(y_sb, b * 2 + 2)
            each(pool, body)

        @block.tensor
        def _(pe):
            def body(b):
                pe.wait_ge(x_in, b * 16 + 16)
                for k in range(DC):
                    mm = pe.transpose(m.bank[4 + k // 4][:, (k % 4) * P:(k % 4 + 1) * P], x[:, k * P:(k + 1) * P], m.ident)
                mm.then_inc(xt_mm, 1)
                pe.wait_ge(xt_sb, b * 2 + 2)
                pe.wait_ge(w_in, b * 48 + 48)
                for i in range(2):
                    for k in range(DC):
                        mm = pe.matmul(m.bank[i][:, :], xT[:, k * P:(k + 1) * P], w[:, i, k * F:(k + 1) * F],
                                       start=(k == 0), stop=(k == DC - 1))
                mm.then_inc(gu, 1)
                pe.wait_ge(hid_ready, b + 1)
                for k in range(4):
                    mm = pe.transpose(m.bank[6][:, k * P:(k + 1) * P], hid[:, k * P:(k + 1) * P], m.ident)
                mm.then_inc(hidt_mm, 1)
                pe.wait_ge(hidt_sb, b + 1)
                for half in range(2):
                    for k in range(4):
                        mm = pe.matmul(m.bank[2 + half][:, :], hidT[:, k * P:(k + 1) * P],
                                       w[:, 2, k * D + half * F:k * D + (half + 1) * F], start=(k == 0), stop=(k == 3))
                mm.then_inc(y_mm, 1)
                pe.wait_ge(y_sb, b * 2 + 2)
            each(pe, body)

        @block.scalar
        def _(act):
            def body(b):
                act.wait_ge(xt_mm, b + 1)
                for i in range(2):
                    act.activation(xT[:, i * F:(i + 1) * F], m.bank[4 + i][:, :], ACT.Copy).then_inc(xt_sb, 1)
                act.wait_ge(gu, b + 1)
                act.activation(gate[:, :], m.bank[0][:, :], ACT.Silu).then_inc(gated, 1)
                act.wait_ge(hidt_mm, b + 1)
                act.activation(hidT[:, :], m.bank[6][:, :], ACT.Copy).then_inc(hidt_sb, 1)
            each(act, body)

        @block.vector
        def _(dve):
            def body(b):
                dve.tensor_copy(ids[:, :], m.tokens[:, bass.ds(b + EXPERTS, 1)]).then_inc(ids_ready, 1)
                dve.wait_ge(gated, b + 1)
                dve.tensor_tensor(hid[:, :], gate[:, :], m.bank[1][:, :], ALU.mult).then_inc(hid_ready, 1)
                dve.wait_ge(y_mm, b + 1)
                dve.wait_ge(y_out, b * 16 + 16)
                for half in range(2):
                    dve.tensor_copy(y[:, half * F:(half + 1) * F], m.bank[2 + half][:, :]).then_inc(y_sb, 1)
            each(dve, body)


def program(nc, d):
    with ExitStack() as ctx:
        m = Names()
        m.dram = d
        m.weights = d.weights
        m.issued = 0
        m.sem = lambda name: ctx.enter_context(nc.semaphore(name))
        keep = lambda name, shape, dt=F32: ctx.enter_context(nc.sbuf_tensor(name, shape, dt))
        m.psum = ctx.enter_context(nc.psum_tensor("psum", [P, 8, 512], F32))
        m.bank = [m.psum[:, i, :] for i in range(8)]
        m.slab_loaded = [m.sem(f"slab_loaded{i}") for i in range(RING)]
        m.products = m.sem("products")
        m.chain = Chain(m.sem("vector_order"))
        m.emptied, m.emptied_after = m.sem("banks_emptied"), 0
        m.gate_ready, m.gate_used, m.gates = m.sem("gate_ready"), m.sem("gate_used"), 0
        m.norm_sems, m.norms = [m.sem(f"norm_{x}") for x in ("squares", "total", "root", "scaled")], 0
        m.const = keep("const", [P, C_END])
        m.ident = m.const[:, C_IDENT:C_IDENT + P]
        m.ones = m.const[:, C_ONES:C_ONES + P]
        m.halves = m.const[:, C_HALVES:C_HALVES + P]
        m.causal = m.const[:, C_CAUSAL:C_CAUSAL + P]
        m.before = m.const[:, C_BEFORE:C_BEFORE + P]
        m.vec = keep("vec", [P, 5, DC])
        m.small = keep("small", [P, 6])
        m.sinks = keep("sinks", [P, SWA_HEADS])
        m.dn = keep("dn", [P, 2])
        m.mod = keep("mod", [P, 48])
        m.scale = keep("scale", [P, 2, DC])
        m.eps = keep("eps", [P, 1])
        m.neg_lam = keep("neg_lam", [P, 1])
        m.tokens = keep("tokens", [P, BLOCKS], I32)
        m.pair_row = keep("pair_row", [P, 2, TT], I32)
        m.pair_w = keep("pair_w", [P, 2, TT])
        m.steer = keep("steer", [P, 8], I32)
        m.xT = keep("xT", [P, DC, T])
        block_one = ctx.enter_context(ExitStack())
        m.ring = block_one.enter_context(nc.sbuf_tensor("ring", [P, RING, SLAB], F32))
        hT = block_one.enter_context(nc.sbuf_tensor("hT", [P, DC, T], F32))
        xT = m.xT

        with ExitStack() as first:
            fb = lambda name, shape: first.enter_context(nc.sbuf_tensor(name, shape, F32))
            m.rot_cos = fb("rot_cos", [P, T])
            m.rot_sin = fb("rot_sin", [P, T])
            stage_modulation(nc, m)
            stage_norm(nc, m, "norm_mix", xT, hT, m.scale[:, 0, :], m.mod[:, 0:8])
            merged = fb("merged", [P, DC, T])
            roT = fb("roT", [P, DC, T])
            with ExitStack() as qkv:
                qb = lambda name, shape: qkv.enter_context(nc.sbuf_tensor(name, shape, F32))
                qT, kT, vals = qb("ret_q", [P, 4, T]), qb("ret_k", [P, 4, T]), qb("ret_v", [P, TT, D])
                stage_project(nc, m, "retp", [(S_RQ, qT, 0), (S_RK, kT, 0)], [(S_RV, 0), (S_RV + 1, 512)], hT, vals)
                stage_retention(nc, m, qT, kT, vals, roT)
            stage_linear(nc, m, "ret_out", [
                (S_RG, hT, 0, "times_silu", (roT, 0)), (S_RG + 1, hT, 0, "times_silu", (roT, 4)),
                (S_RO, roT, 2, "copy", (merged, 0)), (S_RO + 1, roT, 2, "copy", (merged, 4)),
                (S_GR, hT, 0, "times_sigmoid", (merged, 0)), (S_GR + 1, hT, 0, "times_sigmoid", (merged, 4))])
            with ExitStack() as qkv:
                qb = lambda name, shape: qkv.enter_context(nc.sbuf_tensor(name, shape, F32))
                qT, kT, vals = qb("diff_q", [P, DC, T]), qb("diff_k", [P, DC, T]), qb("diff_v", [P, TT, D])
                stage_project(nc, m, "diffp", [(S_DQ, qT, 0), (S_DQ + 1, qT, 4), (S_DK, kT, 0), (S_DK + 1, kT, 4)],
                              [(S_DV, 0), (S_DV + 1, 512)], hT, vals)
                stage_diff(nc, m, qT, kT, vals, roT)
            other = fb("diff_out", [P, DC, T])
            stage_linear(nc, m, "mix_out", [
                (S_DO, roT, 0, "copy", (other, 0)), (S_DO + 1, roT, 0, "copy", (other, 4)),
                (S_GD, hT, 0, "add_sigmoid_times", (merged, 0, other)),
                (S_GD + 1, hT, 0, "add_sigmoid_times", (merged, 4, other)),
                (S_OUT, merged, 4, "add_scaled", (xT, 0, m.mod[:, 16:24])),
                (S_OUT + 1, merged, 4, "add_scaled", (xT, 4, m.mod[:, 16:24]))])
        stage_norm(nc, m, "norm_ffn", xT, hT, m.scale[:, 1, :], m.mod[:, 24:32])
        stage_route(nc, m, hT)
        stage_experts(nc, m)
        stage_overflow(nc, m)
        stage_combine(nc, m, xT)
        stage_norm(nc, m, "norm_final", xT, xT, m.vec[:, 2, :], work=hT)
        block_one.close()

        m.half_slab = keep("half_slab", [P, 2, SLAB // 2])
        m.high = keep("slab_high", [P, 2, SLAB], F32R)
        m.low = keep("slab_low", [P, 2, SLAB], F32R)
        m.half_loaded = [m.sem(f"half_loaded{i}") for i in range(2)]
        m.highs, m.lows = m.sem("slab_highs"), m.sem("slab_lows")
        h = [keep("h_high", [P, DC, T], F32R), keep("h_low", [P, DC, T], F32R)]
        stage_norm_split(nc, m, "norm1", xT, h, m.vec[:, 3, :], first=True)
        with ExitStack() as second:
            wb = lambda name, shape: second.enter_context(nc.sbuf_tensor(name, shape, F32))
            cat = wb("cat", [P, DC, T])
            with ExitStack() as attention:
                ab = lambda name, shape: attention.enter_context(nc.sbuf_tensor(name, shape, F32))
                qT, kT, vals = ab("swa_q", [P, 4, T]), ab("swa_k", [P, T]), ab("swa_v", [P, TT, P])
                d_pool = ab("d_pool", [P, 4, T])
                with ExitStack() as pool:
                    poolT = pool.enter_context(nc.sbuf_tensor("pooled", [P, 4, T], F32))
                    stage_in2(nc, m, h, qT, kT, vals, poolT, d_pool)
                stage_window(nc, m, qT, kT, vals, d_pool, cat)
            stage_linear_split(nc, m, "out2", [(S_OUT2, h, "add", xT, 0), (S_OUT2 + 1, h, "add", xT, 4)], source=cat)
        stage_norm_split(nc, m, "norm2", xT, h, m.vec[:, 4, :])
        stage_peer_u(nc, m, h, xT)
        stage_peer_v(nc, m, h, xT)


def kernel(**inputs):
    import numpy as np
    import concourse.bacc as bacc
    from concourse.bass_utils import run_bass_kernel_spmd

    a = {k: np.asarray(v) for k, v in inputs.items()}

    def rows_of(w, tiles=4):
        return w.reshape(DC, P, tiles, P).transpose(1, 2, 0, 3).reshape(P, -1)

    def wide(w):
        return w.reshape(-1, P, w.shape[1]).transpose(1, 0, 2).reshape(P, -1)

    def cut(w):
        return [w[:, i:i + 512] for i in range(0, w.shape[1], 512)]

    w_in, w_in2 = a["w_in"][0], a["w_in_2"][0]
    col = cut(w_in)
    slabs = [rows_of(c) for c in col[0:2]] + [wide(c) for c in col[2:4]] + [rows_of(c) for c in col[4:6]]
    slabs += [rows_of(c) for c in cut(a["w_ret_o"][0])] + [rows_of(c) for c in col[12:14]]
    slabs += [rows_of(c) for c in col[6:10]] + [wide(c) for c in col[10:12]]
    slabs += [rows_of(c) for c in cut(a["w_diff_o"][0])] + [rows_of(c) for c in col[14:16]]
    slabs += [rows_of(c) for c in cut(a["w_out"][0])]
    for e in range(EXPERTS):
        slabs += [wide(a["w_exp_gate"][0, e]), wide(a["w_exp_up"][0, e]), wide(a["w_exp_down"][0, e])]
    order = np.concatenate([np.arange(HD) + HD * h for j in range(4) for h in (j, j + 4)])
    slabs.append(rows_of(w_in2[:, order]))
    slabs.append(rows_of(w_in2[:, 768:1280]))
    kv = np.zeros((P, SLAB), np.float32)
    kv[:, 0:D] = rows_of(w_in2[:, 512:640], 1)
    kv[:, D:2 * D] = wide(w_in2[:, 640:768])
    slabs.append(kv)
    w_out2 = a["w_out_2"][0]
    w_out2 = np.concatenate([w_out2[order], w_out2[512:]], axis=0)
    slabs += [rows_of(c) for c in cut(w_out2)] + [rows_of(c) for c in cut(a["peer_wq_2"][0])]
    u_t = a["peer_u_2"][0].T
    slabs += [rows_of(c) for c in cut(u_t)]
    v = a["peer_v_2"][0].reshape(PK // 4, 4, P, D).transpose(0, 2, 1, 3).reshape(PK // 4, P, SLAB)
    weights = np.concatenate([np.stack(slabs), v])

    def cols(v):
        return np.ascontiguousarray(v.reshape(-1, P).T)

    r = np.arange(P)
    const = np.zeros((P, C_END), np.float32)
    const[:, C_IDENT:C_IDENT + P] = np.eye(P)
    const[:, C_ONES:C_ONES + P] = 1.0
    const[:, C_HALVES:C_HALVES + P] = (r[:, None] // HD) == (r[None, :] // HD)
    const[:, C_CAUSAL:C_CAUSAL + P] = np.where(r[None, :] <= r[:, None], 0.0, NEG)
    const[:, C_BEFORE:C_BEFORE + P] = r[:, None] < r[None, :]
    const[:, C_IOTA:C_IOTA + P] = r[None, :]
    inv = np.float32(10000.0) ** (-np.arange(0, P, 2, dtype=np.float32) / np.float32(P))
    const[:, C_INV] = np.tile(inv, 2)
    const[:, C_SIGN] = np.where(r < P // 2, 1.0, -1.0)
    const[:, C_TOKEN:C_TOKEN + TT] = r[:, None] + P * np.arange(TT)[None, :]
    for g in range(4):
        const[:, C_COUNT + 16 * g:C_COUNT + 16 * (g + 1)] = 1.0 / np.minimum(np.arange(16) + 1, 2 << g)
    j = np.arange(BAND)[None, :]
    chunk = r[:, None] // 64
    const[:, C_MASK:C_MASK + BAND] = np.where((j // 64 >= chunk) & (j // 64 <= chunk + 2), 0.0, NEG)
    gamma = 1.0 - 2.0 ** (-5.0 - np.arange(HEADS))
    rel = np.arange(T)[None, :] - r[:, None]
    decay = np.where(rel[None] >= 0, np.exp(np.log(gamma)[:, None, None] * np.maximum(rel, 0)[None]), 0.0) * ATT_SCALE
    decay = decay.transpose(1, 0, 2).astype(np.float32)
    dist = np.arange(VEC) - 255
    n = np.abs(dist)
    large = 8 + np.searchsorted(8.0 * 2.0 ** (np.arange(1, 8) / 2.0), n, side="right")
    bucket = np.where(dist > 0, 16, 0) + np.where(n < 8, n, np.minimum(large, 15))
    buckets = (np.arange(32)[:, None] == bucket[None, :]).astype(np.float32)

    arrays = {
        "weights": weights,
        "x": a["x"][0].T.reshape(DC, P, T).transpose(1, 0, 2),
        "c": a["c"],
        "positions": a["positions"],
        "w_ada": a["w_ada"][0].T.reshape(12, 4, P, D).transpose(0, 2, 1, 3).reshape(12, P, SLAB),
        "b_ada": cols(a["b_ada"][0]),
        "const": const,
        "decay": decay,
        "buckets": buckets,
        "vec": np.stack([cols(a[k].reshape(-1)) for k in ("norm_mix", "norm_ffn", "norm_final", "norm1_g_2", "norm2_g_2")], axis=1),
        "diff_norm": cols(a["diff_norm"][0]),
        "rel_bias": a["rel_bias_2"],
        "lam_q1": a["lam_q1"], "lam_k1": a["lam_k1"], "lam_q2": a["lam_q2"], "lam_k2": a["lam_k2"],
        "small": np.concatenate([np.tile(a["q_norm_g_2"][0], 2)[:, None], np.tile(a["k_norm_g_2"][0], 2)[:, None],
                                 cols(a["pool_scale_2"][0])], axis=1),
        "sinks": a["attn_sinks_2"],
        "pool_w": a["pool_w_2"][0].transpose(1, 0, 2),
        "w_router": np.concatenate([a["w_router_group"][0], a["w_router_expert"][0]], axis=1).reshape(DC, P, 36).transpose(1, 0, 2),
        "b_router": np.concatenate([a["b_router_group"], a["b_router_expert"]], axis=1),
        "subkeys": a["peer_subkeys_2"][0].reshape(2 * PH, PK, P).transpose(2, 0, 1),
    }
    arrays = {k: np.ascontiguousarray(v) for k, v in arrays.items()}

    nc = bacc.Bacc("TRN2", target_bir_lowering=False, num_devices=1)
    d = Names()
    for name, v in arrays.items():
        d.__dict__[name] = nc.dram_tensor("in_" + name, v.shape, mybir.dt.from_np(v.dtype), kind="ExternalInput").ap()
    d.lams = [d.lam_q1, d.lam_k1, d.lam_q2, d.lam_k2]
    scratch = lambda name, shape, dt=F32: nc.dram_tensor(name, shape, dt, kind="Internal").ap()
    d.by_distance = scratch("by_distance_rows", (SWA_HEADS, P, VEC))
    d.bias_band = [bass.AP(d.by_distance.tensor, h * P * VEC + P - 1, [[VEC - 1, P], [1, BAND]]) for h in range(SWA_HEADS)]
    d.h_rows = scratch("h_rows", (T, D))
    d.y_rows = scratch("y_rows", (BLOCKS * SLOTS, D))
    d.slot_token = scratch("slot_token", (BLOCKS * SLOTS, 1), I32)
    d.x_rows = scratch("x_rows", (P, DC, T))
    d.gelu = scratch("gelu_rows", (PK // 4, P, 4, T))
    d.gates = scratch("gates_rows", (P, PK, T))
    out = nc.dram_tensor("y", (P, DC, T), F32, kind="ExternalOutput").ap()
    d.out = out
    program(nc, d)
    result = run_bass_kernel_spmd(nc, [{"in_" + k: v for k, v in arrays.items()}], core_ids=[0])
    y = result.results[0]["y"]
    return y.transpose(1, 0, 2).reshape(D, T).T.reshape(1, T, D)
```

```python
from contextlib import ExitStack

import concourse.bass as bass
from concourse import mybir

F32 = mybir.dt.float32
F32R = mybir.dt.float32r
I32 = mybir.dt.int32
U32 = mybir.dt.uint32
ACT = mybir.ActivationFunctionType
ALU = mybir.AluOpType
AX = mybir.AxisListType

P = 128
T = 512
TT = T // P
D = 1024
DC = D // P
HEADS = 4
DV = 256
EPS = 1e-6
LAMBDA_INIT = 0.2
ATT_SCALE = float(P) ** -0.5
SLAB = 4096
EXPERTS = 32
GROUPS = 4
SLOTS = 128
OVER = 7
BLOCKS = EXPERTS + OVER + 1
ROWS = 2 * T
SWA_HEADS = 8
HD = 64
BAND = 256
VEC = 384
PH = 8
TOPK = 16
PK = 128
NEG = -1.0e30
LOWEST = -3.0e38

(S_RQ, S_RK, S_RV, S_RG, S_GR, S_RO, S_DQ, S_DK, S_DV, S_GD, S_DO, S_OUT) = (
    0, 1, 2, 4, 6, 8, 10, 12, 14, 16, 18, 20)
S_MOE = 22
S_IN2 = S_MOE + 3 * EXPERTS
S_OUT2 = S_IN2 + 3
S_WQ = S_OUT2 + 2
S_U = S_WQ + 4
S_V = S_U + PK // 4
S_END = S_V + PK // 4

C_IDENT, C_ONES, C_HALVES, C_CAUSAL, C_BEFORE, C_IOTA = 0, 128, 256, 384, 512, 640
C_INV, C_SIGN, C_TOKEN, C_COUNT, C_MASK = 768, 769, 770, 774, 774 + 64
C_END = C_MASK + BAND


class Chain:

    def __init__(self, sem):
        self.sem, self.n = sem, 0

    def __call__(self, engine, instruction):
        instruction.then_inc(self.sem, 1)
        self.n += 1
        engine.wait_ge(self.sem, self.n)


class Names:

    def begin(self, first_slab):
        self.first_slab = first_slab
        self.emptied_before = self.emptied_after

    def tile(self, s, j):
        return 4 * (s - self.first_slab) + j

    def wait_product(self, engine, s, j):
        engine.wait_ge(self.products, 4 * s + j + 1)

    def wait_bank(self, engine, s, j):
        if self.tile(s, j) >= 4:
            self.wait_emptied(engine, self.tile(s, j) - 3)

    def wait_emptied(self, engine, n):
        engine.wait_ge(self.emptied, self.emptied_before + n)

    def end(self, tiles):
        self.emptied_after = self.emptied_before + tiles


def bcast(ap, where, n):
    dims = list(ap.shape)
    return ap.unsqueeze(where).to_broadcast(dims[:where] + [n] + dims[where:])


def load_expert_slabs(m, sp, first, until):
    def one(turn, slot):
        slab = S_MOE + slot + 2 * turn if isinstance(turn, int) else turn * 2 + (S_MOE + slot)
        for half in range(2):
            if not isinstance(turn, int) or turn >= 1:
                sp.wait_ge(m.lows, turn * 8 + (4 * (S_MOE + slot - 2) + 2 * half + 2))
            src = m.weights[slab] if isinstance(turn, int) else m.weights[bass.ds(slab, 1)].rearrange("a p n -> (a p) n")
            sp.dma_start(m.half_slab[:, 2 * slot + half, :], src[:, half * SLAB // 2:(half + 1) * SLAB // 2]
                         ).then_inc(m.half_loaded[2 * slot + half], 16)

    if until == 2:
        one(0, 0)
        one(0, 1)
    else:
        with sp.Fori(first // 2, until // 2) as turn:
            one(turn, 0)
            one(turn, 1)


def split_number(s):
    return 4 * s


def load_halves(m, sp, first, until):
    def one(s, half):
        if not isinstance(s, int) or s > 0:
            sp.wait_ge(m.lows, split_number(s) + (2 * half - 2))
        src = m.weights[s] if isinstance(s, int) else m.weights[bass.ds(s, 1)].rearrange("a p n -> (a p) n")
        sp.dma_start(m.half_slab[:, half, :], src[:, half * SLAB // 2:(half + 1) * SLAB // 2]
                     ).then_inc(m.half_loaded[half], 16)

    if until - first <= 6:
        for s in range(first, until):
            one(s, 0)
            one(s, 1)
    else:
        with sp.Fori(first, until) as s:
            one(s, 0)
            one(s, 1)


def act_high(m, act, s, j, slot):
    first_block = isinstance(s, int) and s < S_MOE
    if j % 2 == 0:
        act.wait_ge(m.half_loaded[j // 2], s * 16 + (16 if first_block else 16 - 16 * (S_IN2 - S_MOE) // 2))
    if first_block:
        if s >= 1:
            act.wait_ge(m.products, 4 * s + j - 3)
    elif j == 0 and (not isinstance(s, int) or s >= S_IN2 + 2):
        act.wait_ge(m.products, 4 * s - 4)
    w = SLAB // 4
    act.activation(m.high[:, slot, j * w:(j + 1) * w], m.half_slab[:, j // 2, (j % 2) * w:(j % 2 + 1) * w],
                   ACT.Copy).then_inc(m.highs, 1)


def pool_low(m, pool, s, slot):
    w = SLAB // 4
    for j in range(4):
        pool.wait_ge(m.highs, split_number(s) + (j + 1))
        pool.tensor_tensor(m.low[:, slot, j * w:(j + 1) * w], m.half_slab[:, j // 2, (j % 2) * w:(j % 2 + 1) * w],
                           m.high[:, slot, j * w:(j + 1) * w].bitcast(F32), ALU.subtract).then_inc(m.lows, 1)


def split_ahead(m, nc, block, first, last):
    @block.sync
    def _(sp):
        load_halves(m, sp, first + 2, min(last + 3, S_MOE))

    @block.gpsimd
    def _(pool):
        for s in range(first + 1, min(last + 2, S_MOE)):
            pool_low(m, pool, s, 0)


def three_passes(pe, out, w, x, start, stop):
    pe.matmul(out, w[0], x[0], start=start, stop=False)
    pe.matmul(out, w[0], x[1], start=False, stop=False)
    return pe.matmul(out, w[1], x[0], start=False, stop=stop)


def pe_features(m, pe, s, acts, tiles=4):
    slot = s % m.split_slots
    for j in range(tiles):
        pe.wait_ge(m.lows, split_number(s) + j + 1)
        m.wait_bank(pe, s, j)
        for k in range(DC):
            at = slice((j * DC + k) * P, (j * DC + k + 1) * P)
            mm = three_passes(pe, m.bank[j][:, :], [m.high[:, slot, at], m.low[:, slot, at]],
                              [acts[0][:, k, :], acts[1][:, k, :]], k == 0, k == DC - 1)
        mm.then_inc(m.products, 1)


def pe_tokens(m, pe, s, acts):
    slot = s % m.split_slots
    for q in range(4):
        pe.wait_ge(m.lows, split_number(s) + q + 1)
        for j in range(TT):
            if q == 0:
                m.wait_bank(pe, s, j)
            for k in (2 * q, 2 * q + 1):
                tok, at = slice(j * P, (j + 1) * P), slice(k * 512, (k + 1) * 512)
                mm = three_passes(pe, m.bank[j][:, :], [acts[0][:, k, tok], acts[1][:, k, tok]],
                                  [m.high[:, slot, at], m.low[:, slot, at]], k == 0, k == DC - 1)
        mm.then_inc(m.products, 1)


def split_acts(m, act, dve, source, high, low, counts, ahead=0):
    for k in range(DC):
        if act is not None:
            act.activation(high[:, k, :], source[:, k, :], ACT.Copy).then_inc(counts[0], 1)
        else:
            dve.wait_ge(counts[0], ahead + k + 1)
            dve.tensor_tensor(low[:, k, :], source[:, k, :], high[:, k, :].bitcast(F32), ALU.subtract).then_inc(counts[1], 1)


def stage_linear_split(nc, m, name, jobs, source=None):
    m.begin(jobs[0][0])
    with ExitStack() as own:
        acts_high, acts_low = m.sem(name + "_high"), m.sem(name + "_low")
        block = own.enter_context(nc.Block(no_gpsimd_drain=True))
        first, last = jobs[0][0], jobs[-1][0]

        @block.sync
        def _(sp):
            load_halves(m, sp, first + 2, last + 3)

        @block.gpsimd
        def _(pool):
            for s in range(first + 1, last + 2):
                pool_low(m, pool, s, s % 2)

        @block.tensor
        def _(pe):
            if source is not None:
                pe.wait_ge(acts_low, DC)
            for s, acts, _, _, _ in jobs:
                pe_features(m, pe, s, acts)

        @block.scalar
        def _(act):
            if source is not None:
                for k in range(DC):
                    act.activation(jobs[0][1][0][:, k, :], source[:, k, :], ACT.Copy).then_inc(acts_high, 1)
            for s in range(first, last + 1):
                for j in range(4):
                    act_high(m, act, s + 1, j, (s + 1) % 2)

        @block.vector
        def _(dve):
            chain = lambda instruction: m.chain(dve, instruction)
            if source is not None:
                high, low = jobs[0][1]
                for k in range(DC):
                    dve.wait_ge(acts_high, k + 1)
                    dve.tensor_tensor(low[:, k, :], source[:, k, :], high[:, k, :].bitcast(F32), ALU.subtract).then_inc(acts_low, 1)
            for s, _, kind, dst, chunk in jobs:
                for j in range(4):
                    out = dst[:, chunk + j, :]
                    m.wait_product(dve, s, j)
                    if kind == "copy":
                        chain(dve.tensor_copy(out, m.bank[j][:, :]))
                    else:
                        chain(dve.tensor_tensor(out, m.bank[j][:, :], out, ALU.add))
                    dve.sem_inc(m.emptied, 1)
    m.end(4 * len(jobs))


def stage_modulation(nc, m):
    with ExitStack() as own:
        sb = lambda name, shape, dt=F32: own.enter_context(nc.sbuf_tensor(name, shape, dt))
        ada = sb("ada_w", [P, 3, SLAB])
        c_row = sb("c_row", [P, D])
        c_act = sb("c_act", [P, D])
        junk = sb("ada_junk", [P, D])
        b_ada, raw = m.b_ada, m.raw
        pos = sb("pos", [P, T], I32)
        ang = sb("ang", [P, T])
        turn = sb("turn", [P, T])
        mag = sb("mag", [P, T])
        halfpi = sb("halfpi", [P, 1])
        lam_in = sb("lam_in", [P, 4, P])
        lam_p = sb("lam_p", [P, P])
        lam_s = sb("lam_s", [P, 2])
        lam_e = sb("lam_e", [P, 2])
        rel = sb("rel", [32, SWA_HEADS])
        rel_wide = sb("rel_wide", [32, SWA_HEADS, P])
        buckets = sb("buckets", [32, VEC])
        by_distance = sb("by_distance", [P, 2, VEC])

        small = m.sem("mod_small")
        xin = m.sem("mod_x")
        ada_loaded, c_ready = m.ada_loaded, m.c_ready
        ang_ready = m.sem("ang_ready")
        sin_ready = m.sem("sin_ready")
        lam_ready = m.sem("lam_ready")
        lam_exp = m.sem("lam_exp")
        wide_ready = m.sem("wide_ready")
        dist_mm = m.sem("dist_mm")
        dist_sb = m.sem("dist_sb")
        dist_out = [m.sem(f"dist_out{i}") for i in range(2)]
        block = own.enter_context(nc.Block(no_gpsimd_drain=True))
        d = m.dram
        loads = [(c_row[:, :], d.c.to_broadcast([P, D])), (b_ada[:, :], d.b_ada),
                 (pos[:, :], d.positions.to_broadcast([P, T])), (m.const[:, :], d.const),
                 (m.vec[:, :, :], d.vec), (m.dn[:, :], d.diff_norm), (m.small[:, :], d.small),
                 (m.sinks[:, :], d.sinks.to_broadcast([P, SWA_HEADS])), (rel[:, :], d.rel_bias),
                 (buckets[:, :], d.buckets)]
        loads += [(lam_in[:, i, :], a.to_broadcast([P, P])) for i, a in enumerate(d.lams)]

        @block.sync
        def _(sp):
            for s in range(4):
                if s >= 3:
                    sp.wait_ge(m.ada_used, s - 2)
                sp.dma_start(ada[:, s % 3, :], d.w_ada[s]).then_inc(ada_loaded[s % 3], 16)
            sp.dma_start(m.xT[:, :, :], d.x).then_inc(xin, 16)
            sp.wait_ge(xin, 16)

        @block.scalar
        def _(act):
            for dst, src in loads:
                act.dma_start(dst, src).then_inc(small, 16)
            act.wait_ge(small, 16 * len(loads))
            act.activation(c_act[:, :], c_row[:, :], ACT.Silu).then_inc(c_ready, 1)
            act.wait_ge(ang_ready, 1)
            act.activation(m.rot_sin[:, :], ang[:, :], ACT.Sin).then_inc(sin_ready, 1)
            act.wait_ge(ang_ready, 2)
            act.activation(m.rot_cos[:, :], mag[:, :], ACT.Sin, bias=halfpi[:, :], scale=-1.0).then_inc(sin_ready, 1)
            act.wait_ge(lam_ready, 1)
            act.activation(lam_e[:, :], lam_s[:, :], ACT.Exp).then_inc(lam_exp, 1)
            for h in range(SWA_HEADS):
                act.wait_ge(dist_mm, h + 1)
                if h >= 2:
                    act.wait_ge(dist_out[h % 2], 16 * (h // 2))
                act.activation(by_distance[:, h % 2, :], m.bank[h % 4][:, 0:VEC], ACT.Copy).then_inc(dist_sb, 1)
                act.wait_ge(dist_sb, h + 1)
                act.dma_start(d.by_distance[h], by_distance[:, h % 2, :]).then_inc(dist_out[h % 2], 16)
            for i in range(2):
                act.wait_ge(dist_out[i], 16 * SWA_HEADS // 2)

        @block.tensor
        def _(pe):
            pe.wait_ge(wide_ready, 1)
            pe.wait_ge(small, 16 * len(loads))
            for h in range(SWA_HEADS):
                if h >= 4:
                    pe.wait_ge(dist_sb, h - 3)
                pe.matmul(m.bank[h % 4][:, 0:VEC], rel_wide[:, h, :], buckets[:, :],
                          start=True, stop=True).then_inc(dist_mm, 1)

        @block.vector
        def _(dve):
            chain = lambda instruction: m.chain(dve, instruction)
            dve.memset(m.eps[:, :], EPS)
            dve.memset(halfpi[:, :], 1.5707963267948966)
            dve.wait_ge(small, 16 * len(loads))
            chain(dve.tensor_copy(turn[:, :], pos[:, :]))
            chain(dve.tensor_scalar(ang[:, :], turn[:, :], m.const[:, C_INV:C_INV + 1], None, ALU.mult))
            chain(dve.tensor_scalar(turn[:, :], ang[:, :], 0.15915494309189535, 12582912.0, ALU.mult, ALU.add))
            chain(dve.tensor_scalar(turn[:, :], turn[:, :], 12582912.0, None, ALU.subtract))
            for part in (-6.28125, -0.0019340515136718750, -1.2556659146019e-06):
                chain(dve.scalar_tensor_tensor(out=ang[:, :], in0=turn[:, :], scalar=part, in1=ang[:, :],
                                               op0=ALU.mult, op1=ALU.add))
            chain(dve.tensor_scalar(ang[:, :], ang[:, :], 3.1415925, -3.1415925, ALU.min, ALU.max))
            dve.scalar_tensor_tensor(out=mag[:, :], in0=ang[:, :], scalar=-1.0, in1=ang[:, :], op0=ALU.mult,
                                     op1=ALU.max).then_inc(ang_ready, 2)
            chain(dve.tensor_copy(rel_wide[:, :, :], bcast(rel[:, :], 2, P)))
            dve.sem_inc(wide_ready, 1)
            for i in range(2):
                chain(dve.tensor_tensor(lam_p[:, :], lam_in[:, 2 * i, :], lam_in[:, 2 * i + 1, :], ALU.mult))
                chain(dve.tensor_reduce(lam_s[:, i:i + 1], lam_p[:, :], AX.X, ALU.add))
            dve.sem_inc(lam_ready, 1)
            dve.wait_ge(sin_ready, 2)
            chain(dve.tensor_scalar(m.rot_sin[:, :], m.rot_sin[:, :], m.const[:, C_SIGN:C_SIGN + 1], None, ALU.mult))
            dve.wait_ge(lam_exp, 1)
            chain(dve.tensor_tensor(m.neg_lam[:, :], lam_e[:, 1:2], lam_e[:, 0:1], ALU.subtract))
            chain(dve.tensor_scalar(m.neg_lam[:, :], m.neg_lam[:, :], LAMBDA_INIT, None, ALU.subtract))
            dve.tensor_scalar(m.dn[:, :], m.dn[:, :], 1.0 - LAMBDA_INIT, None, ALU.mult)
            dve.wait_ge(c_ready, 1)
            for s in range(4):
                dve.wait_ge(ada_loaded[s % 3], 16 * (s // 3 + 1))
                for j in range(4):
                    n = 4 * s + j
                    chain(dve.tensor_tensor_reduce(
                        out=junk[:, :], in0=ada[:, s % 3, j * D:(j + 1) * D], in1=c_act[:, :], scale=1.0,
                        scalar=0.0, op0=ALU.mult, op1=ALU.add, accum_out=raw[:, n:n + 1]))
                dve.sem_inc(m.ada_used, 1)
            modulate(m, dve, 0, 16, 0, 8)


def modulate(m, dve, first, until, v, at):
    chain = lambda instruction: m.chain(dve, instruction)
    chain(dve.tensor_tensor(m.mod[:, first:until], m.raw[:, first:until], m.b_ada[:, first:until], ALU.add))
    chain(dve.tensor_scalar(m.raw[:, 0:8], m.mod[:, at:at + 8], 1.0, None, ALU.add))
    chain(dve.tensor_tensor(m.scale[:, v, :], m.raw[:, 0:8], m.vec[:, v, :], ALU.mult))


def stage_norm(nc, m, name, src, dst, scale, shift=None, work=None, prefetch=False):
    work = dst if work is None else work
    squares, total, root, scaled = m.norm_sems
    n = m.norms
    m.norms += 1
    with ExitStack() as own:
        rstd = own.enter_context(nc.sbuf_tensor(name + "_rstd", [P, T], F32))
        block = own.enter_context(nc.Block(no_gpsimd_drain=True))

        @block.sync
        def _(sp):
            if prefetch:
                load_expert_slabs(m, sp, 0, 2)

        @block.scalar
        def _(act):
            for k in range(DC):
                act.activation(work[:, k, :], src[:, k, :], ACT.Square).then_inc(squares, 1)
            act.wait_ge(total, n + 1)
            act.activation(rstd[:, :], m.bank[4][:, :], ACT.Sqrt, bias=m.eps[:, :], scale=1.0 / D).then_inc(root, 1)
            if shift is not None:
                for k in range(DC):
                    act.wait_ge(scaled, n * DC + k + 1)
                    act.activation(dst[:, k, :], dst[:, k, :], ACT.Identity, bias=shift[:, k:k + 1])

        @block.tensor
        def _(pe):
            for k in range(DC):
                pe.wait_ge(squares, n * DC + k + 1)
                mm = pe.matmul(m.bank[4][:, :], m.ones, work[:, k, :], start=(k == 0), stop=(k == DC - 1))
            mm.then_inc(total, 1)

        @block.vector
        def _(dve):
            dve.wait_ge(root, n + 1)
            m.chain(dve, dve.reciprocal(rstd[:, :], rstd[:, :]))
            for k in range(DC):
                dve.scalar_tensor_tensor(out=dst[:, k, :], in0=src[:, k, :], scalar=scale[:, k:k + 1],
                                         in1=rstd[:, :], op0=ALU.mult, op1=ALU.mult).then_inc(scaled, 1)


def stage_norm_split(nc, m, name, src, dst, scale, shift=None, first=None):
    squares, total, root, scaled = m.norm_sems
    n = m.norms
    m.norms += 1
    high, low = dst
    with ExitStack() as own:
        rstd = own.enter_context(nc.sbuf_tensor(name + "_rstd", [P, T], F32))
        work = own.enter_context(nc.sbuf_tensor(name + "_work", [P, DC, T], F32))
        rounded = m.sem(name + "_rounded")
        block = own.enter_context(nc.Block(no_gpsimd_drain=True))

        @block.sync
        def _(sp):
            if first is not None:
                load_halves(m, sp, first, first + 2)

        @block.gpsimd
        def _(pool):
            if first is not None:
                pool_low(m, pool, first, 0)

        @block.scalar
        def _(act):
            for k in range(DC):
                act.activation(work[:, k, :], src[:, k, :], ACT.Square).then_inc(squares, 1)
            if first is not None:
                for j in range(4):
                    act_high(m, act, first, j, 0)
            act.wait_ge(total, n + 1)
            act.activation(rstd[:, :], m.bank[4][:, :], ACT.Sqrt, bias=m.eps[:, :], scale=1.0 / D).then_inc(root, 1)
            for k in range(DC):
                act.wait_ge(scaled, n * DC + k + 1)
                if shift is None:
                    rounding = act.activation(high[:, k, :], work[:, k, :], ACT.Copy)
                else:
                    rounding = act.activation(high[:, k, :], work[:, k, :], ACT.Identity, bias=shift[:, k:k + 1])
                rounding.then_inc(rounded, 1)

        @block.tensor
        def _(pe):
            for k in range(DC):
                pe.wait_ge(squares, n * DC + k + 1)
                mm = pe.matmul(m.bank[4][:, :], m.ones, work[:, k, :], start=(k == 0), stop=(k == DC - 1))
            mm.then_inc(total, 1)

        @block.vector
        def _(dve):
            dve.wait_ge(root, n + 1)
            m.chain(dve, dve.reciprocal(rstd[:, :], rstd[:, :]))
            for k in range(DC):
                dve.scalar_tensor_tensor(out=work[:, k, :], in0=src[:, k, :], scalar=scale[:, k:k + 1],
                                         in1=rstd[:, :], op0=ALU.mult, op1=ALU.mult).then_inc(scaled, 1)
            for k in range(DC):
                dve.wait_ge(rounded, k + 1)
                if shift is None:
                    dve.tensor_tensor(low[:, k, :], work[:, k, :], high[:, k, :].bitcast(F32), ALU.subtract)
                else:
                    dve.scalar_tensor_tensor(out=low[:, k, :], in0=work[:, k, :], scalar=shift[:, k:k + 1],
                                             in1=high[:, k, :].bitcast(F32), op0=ALU.add, op1=ALU.subtract)


def stage_project(nc, m, name, rotated, values, acts, vals):
    m.begin(rotated[0][0])
    with ExitStack() as own:
        straight = own.enter_context(nc.sbuf_tensor(name + "_straight", [P, T], F32))
        crossed = own.enter_context(nc.sbuf_tensor(name + "_crossed", [P, T], F32))
        block = own.enter_context(nc.Block(no_gpsimd_drain=True))
        half = P // 2

        split_ahead(m, nc, block, rotated[0][0], values[-1][0])

        @block.tensor
        def _(pe):
            for s, _, _ in rotated:
                pe_features(m, pe, s, acts)
            for s, _ in values:
                pe_tokens(m, pe, s, acts)

        @block.vector
        def _(dve):
            chain = lambda instruction: m.chain(dve, instruction)
            for s, dst, chunk in rotated:
                for j in range(4):
                    m.wait_product(dve, s, j)
                    acc = m.bank[j]
                    dve.tensor_tensor(straight[:, :], acc[:, :], m.rot_cos[:, :], ALU.mult)
                    dve.tensor_tensor(crossed[0:half, :], acc[half:P, :], m.rot_sin[half:P, :], ALU.mult)
                    chain(dve.tensor_tensor(crossed[half:P, :], acc[0:half, :], m.rot_sin[0:half, :], ALU.mult))
                    chain(dve.tensor_tensor(dst[:, chunk + j, :], straight[:, :], crossed[:, :], ALU.add))
                    dve.sem_inc(m.emptied, 1)

        @block.scalar
        def _(act):
            for s, _, _ in rotated:
                for j in range(4):
                    act_high(m, act, s + 1, j, 0)
            m.wait_emptied(act, 4 * len(rotated))
            for s, column in values:
                for j in range(4):
                    act_high(m, act, s + 1, j, 0)
                m.wait_product(act, s, 3)
                for j in range(TT):
                    act.activation(vals[:, j, column:column + 512], m.bank[j][:, :], ACT.Copy).then_inc(m.emptied, 1)
    m.end(4 * (len(rotated) + len(values)))


def head_norm_act(m, act, o_banks, ss_bank, squares, std, h, s):
    act.wait_ge(s.out_ready, h + 1)
    if h >= 1:
        act.wait_ge(s.total, h)
    for c in range(2):
        act.activation(squares[:, c, :], o_banks[c][:, :], ACT.Square).then_inc(s.squares, 1)
    act.wait_ge(s.total, h + 1)
    if h >= 1:
        act.wait_ge(s.normed, h)
    act.activation(std[:, :], ss_bank[:, :], ACT.Sqrt, bias=m.eps[:, :], scale=1.0 / DV).then_inc(s.root, 1)


def stage_retention(nc, m, qT, kT, vals, roT):
    with ExitStack() as own:
        sb = lambda name, shape: own.enter_context(nc.sbuf_tensor(name, shape, F32))
        decay = sb("decay", [P, HEADS, T])
        probs = sb("ret_probs", [P, 2, TT, T])
        squares = sb("ret_sq", [P, 2, T])
        std = sb("ret_std", [P, T])
        s = Names()
        s.decay, s.scores, s.weighted, s.out_ready, s.squares, s.total, s.root, s.normed = (
            m.sem(f"ret_{x}") for x in ("decay", "scores", "weighted", "out", "squares", "total", "root", "normed"))
        block = own.enter_context(nc.Block(no_gpsimd_drain=True))
        score = [m.bank[0][:, 0:T], m.bank[1][:, 0:T - P], m.bank[4][:, 0:T - 2 * P], m.bank[1][:, T - P:T]]
        o_banks = [[m.bank[6], m.bank[7]], [m.bank[3], m.bank[5]]]
        ss_bank = m.bank[2]

        @block.sync
        def _(sp):
            sp.dma_start(decay[:, :, :], m.dram.decay).then_inc(s.decay, 16)
            sp.wait_ge(s.decay, 16)

        @block.tensor
        def _(pe):
            def scores(h):
                if h >= 1:
                    pe.wait_ge(s.weighted, TT * h)
                for j in range(TT):
                    pe.matmul(score[j], kT[:, h, j * P:(j + 1) * P], qT[:, h, j * P:T],
                              start=True, stop=True).then_inc(s.scores, 1)

            scores(0)
            for h in range(HEADS):
                if h + 1 < HEADS:
                    scores(h + 1)
                pe.wait_ge(s.weighted, TT * (h + 1))
                if h >= 2:
                    pe.wait_ge(s.normed, h - 1)
                for c in range(2):
                    for j in range(TT):
                        mm = pe.matmul(o_banks[h % 2][c][:, j * P:T], vals[:, j, h * DV + c * P:h * DV + (c + 1) * P],
                                       probs[:, h % 2, j, j * P:T], start=(j == 0), stop=(j == TT - 1))
                mm.then_inc(s.out_ready, 1)
                pe.wait_ge(s.squares, 2 * (h + 1))
                if h >= 1:
                    pe.wait_ge(s.root, h)
                for c in range(2):
                    mm = pe.matmul(ss_bank[:, :], m.ones, squares[:, c, :], start=(c == 0), stop=(c == 1))
                mm.then_inc(s.total, 1)

        @block.scalar
        def _(act):
            for h in range(HEADS):
                head_norm_act(m, act, o_banks[h % 2], ss_bank, squares, std, h, s)

        @block.vector
        def _(dve):
            chain = lambda instruction: m.chain(dve, instruction)
            dve.wait_ge(s.decay, 16)

            def weigh(h):
                if h >= 2:
                    dve.wait_ge(s.out_ready, h - 1)
                for j in range(TT):
                    dve.wait_ge(s.scores, TT * h + (1 if j == 0 else TT))
                    dve.tensor_tensor(probs[:, h % 2, j, j * P:T], score[j],
                                      decay[:, h, 0:T - j * P], ALU.mult).then_inc(s.weighted, 1)

            weigh(0)
            for h in range(HEADS):
                if h + 1 < HEADS:
                    weigh(h + 1)
                dve.wait_ge(s.root, h + 1)
                chain(dve.reciprocal(std[:, :], std[:, :]))
                for c in range(2):
                    last = dve.tensor_tensor(roT[:, 2 * h + c, :], o_banks[h % 2][c][:, :], std[:, :], ALU.mult)
                last.then_inc(s.normed, 1)


def stage_linear(nc, m, name, jobs, source=None, modulates=False):
    m.begin(jobs[0][0])
    gates = {"times_silu": ACT.Silu, "sigmoid": ACT.Sigmoid}
    with ExitStack() as own:
        gate = own.enter_context(nc.sbuf_tensor(name + "_gate", [P, 2, T], F32))
        gate_ready, gate_used, g0 = m.gate_ready, m.gate_used, m.gates
        final, f0 = m.tile_final, m.finals
        high_count, low_count = m.acts_high, m.acts_low
        block = own.enter_context(nc.Block(no_gpsimd_drain=True))
        tiles = [(job, j) for job in jobs for j in range(4)]
        h0 = m.act_splits
        first, last = jobs[0][0], jobs[-1][0]
        MOD_TILES = 16
        if modulates:
            ada = own.enter_context(nc.sbuf_tensor("ada_half", [P, 2, 2 * D], F32))
            c_act = own.enter_context(nc.sbuf_tensor("c_act_again", [P, D], F32))
            junk = own.enter_context(nc.sbuf_tensor("ada_junk_again", [P, D], F32))

        @block.sync
        def _(sp):
            def ada_half(t):
                if t >= 2:
                    sp.wait_ge(m.ada_used, 4 + t - 1)
                sp.dma_start(ada[:, t % 2, :], m.dram.w_ada[4 + t // 2][:, (t % 2) * 2 * D:(t % 2 + 1) * 2 * D]
                             ).then_inc(m.ada_loaded[1 + t % 2], 16)

            if modulates:
                sp.dma_start(c_act[:, :], m.dram.c.to_broadcast([P, D])).then_inc(m.ada_loaded[0], 16)
            for i, s in enumerate(range(first + 2, last + 3)):
                for t in range(4 * i, 4 * i + 4):
                    if modulates and t < MOD_TILES:
                        ada_half(t)
                if s < S_MOE:
                    load_halves(m, sp, s, s + 1)

        @block.gpsimd
        def _(pool):
            for s in range(first + 1, min(last + 2, S_MOE)):
                pool_low(m, pool, s, 0)

        @block.tensor
        def _(pe):
            for s, acts, needed, _, _, _ in jobs:
                if needed:
                    pe.wait_ge(low_count, h0 + needed)
                pe_features(m, pe, s, acts)

        @block.scalar
        def _(act):
            g = f = 0
            if modulates:
                act.wait_ge(m.ada_loaded[0], 16 * 3)
                act.activation(c_act[:, :], c_act[:, :], ACT.Silu).then_inc(m.c_ready, 1)
            if source is not None:
                split_acts(m, act, None, source[0], source[1], source[2], (high_count, low_count))
            for (s, _, _, kind, ops, into), j in tiles:
                if kind in gates:
                    m.wait_product(act, s, j)
                    if g >= 2:
                        act.wait_ge(gate_used, g0 + g - 1)
                    act.activation(gate[:, g % 2, :], m.bank[j][:, :], gates[kind]).then_inc(gate_ready, 1)
                    g += 1
                if into is not None:
                    f += 1
                    act.wait_ge(final, f0 + f)
                    act.activation(into[0][:, ops[1] + j, :], ops[0][:, ops[1] + j, :], ACT.Copy).then_inc(high_count, 1)
                if s + 1 < S_MOE:
                    act_high(m, act, s + 1, j, 0)

        @block.vector
        def _(dve):
            chain = lambda instruction: m.chain(dve, instruction)
            g, h = 0, h0
            if source is not None:
                split_acts(m, None, dve, source[0], source[1], source[2], (high_count, low_count), h0)
                h += DC
            for (s, _, _, kind, ops, into), j in tiles:
                dst, at = ops[0], ops[1] + j
                out = dst[:, at, :]
                m.wait_product(dve, s, j)
                if kind in gates:
                    dve.wait_ge(gate_ready, g0 + g + 1)
                    if kind == "times_silu":
                        chain(dve.tensor_tensor(out, out, gate[:, g % 2, :], ALU.mult))
                    else:
                        chain(dve.tensor_copy(out, gate[:, g % 2, :]))
                    dve.sem_inc(gate_used, 1)
                    g += 1
                elif kind == "times":
                    chain(dve.tensor_tensor(out, m.bank[j][:, :], out, ALU.mult))
                elif kind == "add_times":
                    other = ops[2][:, at, :]
                    chain(dve.tensor_tensor(other, m.bank[j][:, :], other, ALU.mult))
                    chain(dve.tensor_tensor(out, out, other, ALU.add))
                elif kind == "add_scaled":
                    chain(dve.scalar_tensor_tensor(out=out, in0=m.bank[j][:, :], scalar=ops[2][:, at:at + 1],
                                                   in1=out, op0=ALU.mult, op1=ALU.add))
                dve.sem_inc(m.emptied, 1)
                if into is not None:
                    dve.sem_inc(final, 1)
                    dve.wait_ge(high_count, h + 1)
                    h += 1
                    dve.tensor_tensor(into[1][:, at, :], out, into[0][:, at, :].bitcast(F32), ALU.subtract).then_inc(low_count, 1)
                t = m.tile(s, j)
                if modulates and t < MOD_TILES:
                    if t == 0:
                        dve.wait_ge(m.c_ready, 2)
                    dve.wait_ge(m.ada_loaded[1 + t % 2], 16 * (t // 2 + 2))
                    for i in range(2):
                        n = 16 + 2 * t + i
                        chain(dve.tensor_tensor_reduce(
                            out=junk[:, :], in0=ada[:, t % 2, i * D:(i + 1) * D], in1=c_act[:, :], scale=1.0,
                            scalar=0.0, op0=ALU.mult, op1=ALU.add, accum_out=m.raw[:, n:n + 1]))
                    dve.sem_inc(m.ada_used, 1)
                    if t == MOD_TILES - 1:
                        modulate(m, dve, 16, 48, 1, 32)
    m.gates += sum(4 for job in jobs if job[3] in gates)
    splits = sum(4 for job in jobs if job[5] is not None)
    m.finals += splits
    m.act_splits += splits + (DC if source is not None else 0)
    m.end(len(tiles))


def stage_diff(nc, m, qT, kT, vals, doT):
    units = [(h, t) for h in range(HEADS) for t in range(TT)]
    with ExitStack() as own:
        sb = lambda name, shape: own.enter_context(nc.sbuf_tensor(name, shape, F32))
        p = sb("diff_p", [P, 2, 2, T])
        aT = sb("diff_aT", [P, TT, T])
        st = sb("diff_st", [P, 2, 8])
        squares = sb("diff_sq", [P, 2, T])
        std = sb("diff_std", [P, T])
        s = Names()
        (s.scores, s.maxed, s.probs, s.mixed, s.turned, s.turned_sb, s.out_ready, s.squares, s.total, s.root,
         s.normed) = (m.sem(f"diff_{x}") for x in ("scores", "maxed", "probs", "mixed", "turned", "turned_sb", "out",
                                                    "squares", "total", "root", "normed"))
        block = own.enter_context(nc.Block(no_gpsimd_drain=True))
        s_bank = lambda u, c: m.bank[2 * (u % 2) + c]
        t_bank, ss_bank = m.bank[4], m.bank[5]
        o_bank = [m.bank[6], m.bank[7]]

        @block.tensor
        def _(pe):
            def scores(u):
                h, t = units[u]
                if u >= 2:
                    pe.wait_ge(s.probs, 2 * (u - 1))
                for c in range(2):
                    mm = pe.matmul(s_bank(u, c)[:, 0:(t + 1) * P], qT[:, 2 * h + c, t * P:(t + 1) * P],
                                   kT[:, 2 * h + c, 0:(t + 1) * P], start=True, stop=True)
                mm.then_inc(s.scores, 1)

            def turn(u):
                h, t = units[u]
                pe.wait_ge(s.mixed, u + 1)
                if u >= 1:
                    pe.wait_ge(s.turned_sb, u)
                for j in range(t + 1):
                    mm = pe.transpose(t_bank[:, j * P:(j + 1) * P], p[:, u % 2, 0, j * P:(j + 1) * P], m.ident)
                mm.then_inc(s.turned, 1)

            def output(h):
                pe.wait_ge(s.turned_sb, TT * (h + 1))
                if h >= 1:
                    pe.wait_ge(s.normed, h)
                for c in range(2):
                    for j in range(TT):
                        mm = pe.matmul(o_bank[c][:, j * P:T], vals[:, j, h * DV + c * P:h * DV + (c + 1) * P],
                                       aT[:, j, j * P:T], start=(j == 0), stop=(j == TT - 1))
                mm.then_inc(s.out_ready, 1)

            def total(h):
                pe.wait_ge(s.squares, 2 * (h + 1))
                if h >= 1:
                    pe.wait_ge(s.root, h)
                for c in range(2):
                    mm = pe.matmul(ss_bank[:, :], m.ones, squares[:, c, :], start=(c == 0), stop=(c == 1))
                mm.then_inc(s.total, 1)

            scores(0)
            scores(1)
            for u, (h, t) in enumerate(units):
                if t == 0 and h >= 1:
                    output(h - 1)
                turn(u)
                if u + 2 < len(units):
                    scores(u + 2)
                if t == 1 and h >= 1:
                    total(h - 1)
            output(HEADS - 1)
            total(HEADS - 1)

        @block.scalar
        def _(act):
            def squares_of(h):
                act.wait_ge(s.out_ready, h + 1)
                if h >= 1:
                    act.wait_ge(s.total, h)
                for c in range(2):
                    act.activation(squares[:, c, :], o_bank[c][:, :], ACT.Square).then_inc(s.squares, 1)

            def root_of(h):
                act.wait_ge(s.total, h + 1)
                if h >= 1:
                    act.wait_ge(s.normed, h)
                act.activation(std[:, :], ss_bank[:, :], ACT.Sqrt, bias=m.eps[:, :], scale=1.0 / DV).then_inc(s.root, 1)

            def exponents(u):
                h, t = units[u]
                act.wait_ge(s.maxed, u + 1)
                if u >= 2:
                    act.wait_ge(s.mixed, u - 1)
                for c in range(2):
                    act.activation(p[:, u % 2, c, 0:(t + 1) * P], s_bank(u, c)[:, 0:(t + 1) * P], ACT.Exp,
                                   bias=st[:, u % 2, 2 + c:3 + c], scale=ATT_SCALE,
                                   accum_out=st[:, u % 2, 4 + c:5 + c]).then_inc(s.probs, 1)

            exponents(0)
            for u, (h, t) in enumerate(units):
                if u + 1 < len(units):
                    exponents(u + 1)
                act.wait_ge(s.turned, u + 1)
                if t == 0 and h >= 1:
                    act.wait_ge(s.out_ready, h)
                act.activation(aT[:, 0:t + 1, t * P:(t + 1) * P],
                               t_bank[:, 0:(t + 1) * P].rearrange("p (j q) -> p j q", q=P), ACT.Copy).then_inc(s.turned_sb, 1)
                if t == 0 and h >= 1:
                    squares_of(h - 1)
                if t == 2 and h >= 1:
                    root_of(h - 1)
            squares_of(HEADS - 1)
            root_of(HEADS - 1)

        @block.vector
        def _(dve):
            chain = lambda instruction: m.chain(dve, instruction)

            def normed(h):
                dve.wait_ge(s.root, h + 1)
                chain(dve.reciprocal(std[:, :], std[:, :]))
                for c in range(2):
                    last = dve.scalar_tensor_tensor(out=doT[:, 2 * h + c, :], in0=o_bank[c][:, :],
                                                    scalar=m.dn[:, c:c + 1], in1=std[:, :], op0=ALU.mult, op1=ALU.mult)
                last.then_inc(s.normed, 1)

            def softmax_max(u):
                h, t = units[u]
                dve.wait_ge(s.scores, u + 1)
                if u >= 2:
                    dve.wait_ge(s.probs, 2 * (u - 1))
                for c in range(2):
                    bank = s_bank(u, c)
                    link = dve.tensor_tensor(bank[:, t * P:(t + 1) * P], bank[:, t * P:(t + 1) * P], m.causal, ALU.add)
                    if c:
                        chain(link)
                for c in range(2):
                    link = dve.tensor_reduce(st[:, u % 2, c:c + 1], s_bank(u, c)[:, 0:(t + 1) * P], AX.X, ALU.max)
                    if c:
                        chain(link)
                dve.tensor_scalar(st[:, u % 2, 2:4], st[:, u % 2, 0:2], -ATT_SCALE, None, ALU.mult).then_inc(s.maxed, 1)

            softmax_max(0)
            for u, (h, t) in enumerate(units):
                if u + 1 < len(units):
                    softmax_max(u + 1)
                w = (t + 1) * P
                dve.wait_ge(s.probs, 2 * (u + 1))
                chain(dve.reciprocal(st[:, u % 2, 6:8], st[:, u % 2, 4:6]))
                mixed = p[:, u % 2, 0, 0:w]
                dve.tensor_scalar(mixed, mixed, st[:, u % 2, 6:7], None, ALU.mult)
                chain(dve.tensor_scalar(st[:, u % 2, 7:8], st[:, u % 2, 7:8], m.neg_lam[:, :], None, ALU.mult))
                dve.scalar_tensor_tensor(out=mixed, in0=p[:, u % 2, 1, 0:w], scalar=st[:, u % 2, 7:8], in1=mixed,
                                         op0=ALU.mult, op1=ALU.add).then_inc(s.mixed, 1)
                if t == 3 and h >= 1:
                    normed(h - 1)
            normed(HEADS - 1)


def stage_route(nc, m, hT):
    E = EXPERTS
    with ExitStack() as own:
        sb = lambda name, shape, dt=F32: own.enter_context(nc.sbuf_tensor("rt_" + name, shape, dt))
        w_r = sb("w", [P, DC, 36])
        b_r = sb("b", [P, 36])
        logits = sb("logits", [P, TT, 36])
        group = sb("group", [P, TT, 8])
        top = sb("top", [P, TT, 8])
        top_e = sb("top_e", [P, TT, 8])
        where = sb("where", [P, TT, 8], U32)
        where_e = sb("where_e", [P, TT, 8], U32)
        gidx = sb("gidx", [P, TT])
        gexp = sb("gexp", [P, TT, GROUPS])
        gsum = sb("gsum", [P, TT])
        gmask = sb("gmask", [P, TT, GROUPS])
        e_in = sb("e_in", [P, TT, E])
        picked = sb("picked", [P, 2, TT])
        hot = sb("hot", [P, 2, TT, E])
        both = sb("both", [P, TT, E])
        rank = sb("rank", [P, TT, E])
        count = sb("count", [P, E])
        over = sb("over", [P, E])
        scan = sb("scan", [P, 2, E])
        tmp = sb("tmp", [P, TT, E])
        r = sb("r", [P, 2, TT])
        q = sb("q", [P, 2, TT])
        ov = sb("ov", [P, 2, TT])
        one = sb("one", [P, 2, TT])
        dest = sb("dest", [P, 2, TT])
        dest_t = sb("dest_t", [P, 2, TT], U32)
        ids = sb("ids", [P, TT], I32)
        zeros = sb("zeros", [P, BLOCKS], I32)
        whose = sb("whose", [P, 2, 8])
        whose_t = sb("whose_t", [P, 8, E])
        rows = sb("rows", [P, 2, D])
        blank = sb("blank", [P, D])

        loads, lg, bias_done, gx_ready, gx_done, hot_ready, ranked, dest_ready, zeroed, scattered, table = (
            m.sem(f"rt_{x}") for x in ("loads", "lg", "bias", "gx_ready", "gx_done", "hot", "ranked", "dest", "zeroed",
                                       "scattered", "table"))
        turned, rows_ready = m.sem("rt_turned"), m.sem("rt_rows")
        rows_out = [m.sem(f"rt_rows_out{i}") for i in range(2)]
        block = own.enter_context(nc.Block(no_gpsimd_drain=True))
        d = m.dram
        iota = m.const[:, C_IOTA:C_IOTA + P]

        @block.sync
        def _(sp):
            sp.dma_start(w_r[:, :, :], d.w_router).then_inc(loads, 16)
            sp.dma_start(b_r[:, :], d.b_router.to_broadcast([P, 36])).then_inc(loads, 16)
            for t in range(TT):
                sp.wait_ge(rows_ready, 2 * (t + 1))
                sp.dma_start(d.h_rows[t * P:(t + 1) * P, :], rows[:, t % 2, :]).then_inc(rows_out[t % 2], 16)
            for i in range(2):
                sp.wait_ge(rows_out[i], 16 * TT // 2)

        @block.tensor
        def _(pe):
            pe.wait_ge(loads, 32)
            for t in range(TT):
                for k in range(DC):
                    mm = pe.matmul(m.bank[0][:, t * 36:t * 36 + 36], hT[:, k, t * P:(t + 1) * P], w_r[:, k, :],
                                   start=(k == 0), stop=(k == DC - 1))
            mm.then_inc(lg, 1)
            for t in range(TT):
                if t >= 1:
                    pe.wait_ge(rows_ready, 2 * t)
                for k in range(DC):
                    mm = pe.transpose(m.bank[4 + k // 4][:, (k % 4) * P:(k % 4 + 1) * P], hT[:, k, t * P:(t + 1) * P],
                                      m.ident)
                    if k % 4 == 3:
                        mm.then_inc(turned, 1)
            pe.wait_ge(hot_ready, 1)
            for t in range(TT):
                for u in range(t + 1):
                    mm = pe.matmul(m.bank[1][:, t * E:(t + 1) * E], m.before if u == t else m.ones, both[:, u, :],
                                   start=(u == 0), stop=(u == t))
            for u in range(TT):
                mm = pe.matmul(m.bank[2][:, 0:E], m.ones, both[:, u, :], start=(u == 0), stop=(u == TT - 1))
            mm.then_inc(ranked, 1)

        @block.scalar
        def _(act):
            for t in range(TT):
                if t >= 2:
                    act.wait_ge(rows_out[t % 2], 16 * (t // 2))
                for i in range(2):
                    act.wait_ge(turned, 2 * t + i + 1)
                    act.activation(rows[:, t % 2, i * 512:(i + 1) * 512], m.bank[4 + i][:, :], ACT.Copy).then_inc(rows_ready, 1)
            act.wait_ge(gx_ready, 1)
            act.activation(gexp[:, :, :], gexp[:, :, :], ACT.Exp).then_inc(gx_done, 1)
            act.activation(m.pair_w[:, 1, :], m.pair_w[:, 1, :], ACT.Exp).then_inc(gx_done, 1)

        @block.vector
        def _(dve):
            chain = lambda instruction: m.chain(dve, instruction)
            chain(dve.memset(group[:, :, :], LOWEST))
            dve.wait_ge(lg, 1)
            dve.wait_ge(loads, 32)
            chain(dve.tensor_tensor(logits[:, :, :], m.bank[0][:, 0:4 * 36].rearrange("p (t e) -> p t e", e=36),
                                    bcast(b_r[:, :], 1, TT), ALU.add))
            chain(dve.tensor_copy(group[:, :, 0:GROUPS], logits[:, :, 0:GROUPS]))
            for t in range(TT):
                last = dve.max(out=top[:, t, :], in_=group[:, t, :])
            chain(last)
            for t in range(TT):
                last = dve.max_index(where[:, t, :], top[:, t, :], group[:, t, :])
            chain(last)
            chain(dve.tensor_copy(gidx[:, :], where[:, :, 0]))
            chain(dve.tensor_tensor(gmask[:, :, :], bcast(iota[:, 0:GROUPS], 1, TT), bcast(gidx[:, :], 2, GROUPS), ALU.is_equal))
            chain(dve.tensor_scalar(gmask[:, :, :], gmask[:, :, :], 1.0, 1.0e30, ALU.subtract, ALU.mult))
            for t in range(TT):
                last = dve.tensor_tensor(e_in[:, t, :].rearrange("p (g e) -> p g e", g=GROUPS),
                                         logits[:, t, GROUPS:36].rearrange("p (g e) -> p g e", g=GROUPS),
                                         bcast(gmask[:, t, :], 2, E // GROUPS), ALU.add)
            chain(last)
            for t in range(TT):
                last = dve.max(out=top_e[:, t, :], in_=e_in[:, t, :])
            chain(last)
            for t in range(TT):
                last = dve.max_index(where_e[:, t, :], top_e[:, t, :], e_in[:, t, :])
            chain(last)
            chain(dve.tensor_copy(picked[:, :, :], where_e[:, :, 0:2].rearrange("p t k -> p k t")))
            for k in range(2):
                last = dve.tensor_tensor(hot[:, k, :, :], bcast(iota[:, 0:E], 1, TT), bcast(picked[:, k, :], 2, E), ALU.is_equal)
            chain(last)
            chain(dve.tensor_tensor(both[:, :, :], hot[:, 0, :, :], hot[:, 1, :, :], ALU.add))
            dve.sem_inc(hot_ready, 1)
            chain(dve.tensor_tensor(gexp[:, :, :], logits[:, :, 0:GROUPS], bcast(top[:, :, 0], 2, GROUPS), ALU.subtract))
            chain(dve.tensor_tensor(m.pair_w[:, 1, :], top_e[:, :, 1], top_e[:, :, 0], ALU.subtract))
            dve.sem_inc(gx_ready, 1)
            dve.wait_ge(gx_done, 2)
            chain(dve.tensor_reduce(gsum[:, :], gexp[:, :, :], AX.X, ALU.add))
            chain(dve.tensor_scalar(m.pair_w[:, 0, :], m.pair_w[:, 1, :], 1.0, None, ALU.add))
            chain(dve.tensor_tensor(gsum[:, :], gsum[:, :], m.pair_w[:, 0, :], ALU.mult))
            chain(dve.reciprocal(m.pair_w[:, 0, :], gsum[:, :]))
            chain(dve.tensor_tensor(m.pair_w[:, 1, :], m.pair_w[:, 1, :], m.pair_w[:, 0, :], ALU.mult))
            dve.wait_ge(ranked, 1)
            chain(dve.tensor_copy(rank[:, :, :], m.bank[1][:, 0:TT * E].rearrange("p (t e) -> p t e", e=E)))
            chain(dve.tensor_copy(count[:, :], m.bank[2][:, 0:E]))
            chain(dve.tensor_scalar(over[:, :], count[:, :], float(SLOTS), None, ALU.is_gt))
            for b in range(2, T // SLOTS):
                chain(dve.scalar_tensor_tensor(out=over[:, :], in0=count[:, :], scalar=float(SLOTS * b), in1=over[:, :],
                                               op0=ALU.is_gt, op1=ALU.add))
            chain(dve.tensor_copy(scan[:, 0, :], over[:, :]))
            a = 0
            step = 1
            while step < E:
                chain(dve.tensor_copy(scan[:, 1 - a, 0:step], scan[:, a, 0:step]))
                chain(dve.tensor_tensor(scan[:, 1 - a, step:E], scan[:, a, step:E], scan[:, a, 0:E - step], ALU.add))
                a = 1 - a
                step *= 2
            ends = scan[:, a, :]
            chain(dve.tensor_tensor(whose_t[:, :, :], bcast(ends, 1, 8), bcast(iota[:, 0:8], 2, E), ALU.is_le))
            chain(dve.tensor_reduce(whose[:, 0, :], whose_t[:, :, :], AX.X, ALU.add))
            chain(dve.tensor_copy(m.steer[:, 0:OVER], whose[:, 0, 0:OVER]))
            chain(dve.tensor_copy(m.steer[:, OVER:OVER + 1], ends[:, E - 1:E]))
            starts = scan[:, 1 - a, :]
            chain(dve.tensor_tensor(starts, ends, over[:, :], ALU.subtract))
            for k in range(2):
                chain(dve.tensor_tensor(tmp[:, :, :], rank[:, :, :], hot[:, k, :, :], ALU.mult))
                chain(dve.tensor_reduce(r[:, k, :], tmp[:, :, :], AX.X, ALU.add))
                chain(dve.tensor_tensor(tmp[:, :, :], bcast(starts, 1, TT), hot[:, k, :, :], ALU.mult))
                chain(dve.tensor_reduce(ov[:, k, :], tmp[:, :, :], AX.X, ALU.add))
            chain(dve.tensor_scalar(q[:, :, :], r[:, :, :], float(SLOTS), None, ALU.is_ge))
            chain(dve.tensor_scalar(ov[:, :, :], ov[:, :, :], float(E - 1), None, ALU.add))
            chain(dve.tensor_tensor(ov[:, :, :], ov[:, :, :], picked[:, :, :], ALU.subtract))
            chain(dve.tensor_tensor(ov[:, :, :], ov[:, :, :], q[:, :, :], ALU.mult))
            for b in range(2, T // SLOTS):
                chain(dve.scalar_tensor_tensor(out=q[:, :, :], in0=r[:, :, :], scalar=float(SLOTS * b), in1=q[:, :, :],
                                               op0=ALU.is_ge, op1=ALU.add))
            chain(dve.tensor_tensor(ov[:, :, :], ov[:, :, :], picked[:, :, :], ALU.add))
            chain(dve.tensor_tensor(ov[:, :, :], ov[:, :, :], q[:, :, :], ALU.add))
            chain(dve.scalar_tensor_tensor(out=one[:, :, :], in0=q[:, :, :], scalar=-float(SLOTS), in1=r[:, :, :],
                                           op0=ALU.mult, op1=ALU.add))
            chain(dve.scalar_tensor_tensor(out=dest[:, :, :], in0=ov[:, :, :], scalar=float(SLOTS), in1=one[:, :, :],
                                           op0=ALU.mult, op1=ALU.add))
            chain(dve.tensor_copy(m.pair_row[:, :, :], dest[:, :, :]))
            chain(dve.scalar_tensor_tensor(out=dest[:, :, :], in0=one[:, :, :], scalar=float(BLOCKS), in1=ov[:, :, :],
                                           op0=ALU.mult, op1=ALU.add))
            chain(dve.tensor_copy(dest_t[:, :, :], dest[:, :, :]))
            chain(dve.tensor_copy(ids[:, :], m.const[:, C_TOKEN:C_TOKEN + TT]))
            dve.sem_inc(dest_ready, 1)

        @block.gpsimd
        def _(pool):
            own_wait = m.sem("rt_zero_sb")
            pool.memset(zeros[:, :], 0).then_inc(own_wait, 1)
            pool.wait_ge(own_wait, 1)
            pool.dma_start(d.slot_token.rearrange("(p b) o -> p (b o)", b=BLOCKS), zeros[:, :]).then_inc(zeroed, 16)
            pool.memset(blank[:, :], 0.0).then_inc(own_wait, 1)
            pool.wait_ge(own_wait, 2)
            for b in range(EXPERTS, BLOCKS):
                pool.dma_start(d.y_rows[b * SLOTS:(b + 1) * SLOTS, :], blank[:, :]).then_inc(zeroed, 16)
            pool.wait_ge(zeroed, 16 * (1 + BLOCKS - EXPERTS))
            pool.wait_ge(dest_ready, 1)
            for k in range(2):
                for t in range(TT):
                    pool.indirect_dma_start(
                        out=d.slot_token, out_offset=bass.IndirectOffsetOnAxis(ap=dest_t[:, k, t:t + 1], axis=0),
                        in_=ids[:, t:t + 1], in_offset=None).then_inc(scattered, 16)
            pool.wait_ge(scattered, 16 * 2 * TT)
            pool.dma_start(m.tokens[:, :], d.slot_token.rearrange("(p b) o -> p (b o)", b=BLOCKS)).then_inc(table, 16)
            pool.wait_ge(table, 16)


def stage_experts(nc, m):
    F = 512
    turns = EXPERTS // 4
    with ExitStack() as own:
        sb = lambda name, shape, dt=F32: own.enter_context(nc.sbuf_tensor("moe_" + name, shape, dt))
        x = sb("x", [P, 2, D])
        x_high = sb("x_high", [P, 2, D], F32R)
        x_low = sb("x_low", [P, 2, D], F32R)
        gate = sb("gate", [P, F])
        hid = sb("hid", [P, F])
        hid_high = sb("hid_high", [P, F], F32R)
        hid_low = sb("hid_low", [P, F], F32R)
        y = sb("y", [P, 2, D])
        x_in = [m.sem(f"moe_x{i}") for i in range(2)]
        y_out = [m.sem(f"moe_y{i}") for i in range(2)]
        xt_mm, xt_high, xt_low, gated, hid_ready, hidt_mm, hidt_high, hidt_low, y_sb = (
            m.sem(f"moe_{v}") for v in ("xt_mm", "xt_high", "xt_low", "gated", "hid", "hidt_mm", "hidt_high", "hidt_low", "y_sb"))
        block = own.enter_context(nc.Block(no_gpsimd_drain=True))
        d = m.dram
        quarter = SLAB // 4

        def slabs_before(turn, c):
            return turn * 48 + 4 * (S_MOE + c)

        @block.sync
        def _(sp):
            load_expert_slabs(m, sp, 2, 3 * EXPERTS)

        @block.gpsimd
        def _(pool):
            def store(e):
                pool.wait_ge(y_sb, 2 * e + 2)
                pool.dma_start(d.y_rows[e * SLOTS:(e + 1) * SLOTS, :], y[:, e % 2, :]).then_inc(y_out[e % 2], 16)

            for e in range(EXPERTS):
                if e >= 2:
                    pool.wait_ge(xt_mm, 2 * (e - 1))
                pool.indirect_dma_start(
                    out=x[:, e % 2, :], out_offset=None, in_=d.h_rows,
                    in_offset=bass.IndirectOffsetOnAxis(ap=m.tokens[:, e:e + 1], axis=0)).then_inc(x_in[e % 2], 16)
                if e >= 2:
                    store(e - 2)
            store(EXPERTS - 2)
            store(EXPERTS - 1)
            for i in range(2):
                pool.wait_ge(y_out[i], 16 * EXPERTS // 2)

        @block.tensor
        def _(pe):
            def turn_x(turn, i):
                slot = i % 2
                pe.wait_ge(x_in[slot], turn * 32 + (8 * i + 16 - 8 * slot))
                if not isinstance(turn, int) or turn + i >= 1:
                    pe.wait_ge(xt_low, turn * 8 + 2 * i)
                for k in range(DC):
                    mm = pe.transpose(m.bank[4 + k // 4][:, (k % 4) * P:(k % 4 + 1) * P],
                                      x[:, slot, k * P:(k + 1) * P], m.ident)
                    if k % 4 == 3:
                        mm.then_inc(xt_mm, 1)

            def first(turn, i):
                pe.wait_ge(xt_low, turn * 8 + (2 * i + 2))
                for w in range(2):
                    c = 3 * i + w
                    for q in range(4):
                        pe.wait_ge(m.lows, slabs_before(turn, c) + (q + 1))
                        for k in (2 * q, 2 * q + 1):
                            at, cols = slice(k * P, (k + 1) * P), slice(k * F, (k + 1) * F)
                            mm = three_passes(pe, m.bank[w][:, :], [x_high[:, i % 2, at], x_low[:, i % 2, at]],
                                              [m.high[:, c % 2, cols], m.low[:, c % 2, cols]], k == 0, k == DC - 1)
                    mm.then_inc(m.products, 4)

            def second(turn, i):
                c = 3 * i + 2
                pe.wait_ge(hid_ready, turn * 4 + (i + 1))
                for k in range(4):
                    mm = pe.transpose(m.bank[6][:, k * P:(k + 1) * P], hid[:, k * P:(k + 1) * P], m.ident)
                mm.then_inc(hidt_mm, 1)
                pe.wait_ge(hidt_low, turn * 4 + (i + 1))
                if not isinstance(turn, int) or turn + i >= 1:
                    pe.wait_ge(y_sb, turn * 8 + 2 * i)
                for k in range(4):
                    pe.wait_ge(m.lows, slabs_before(turn, c) + (k + 1))
                    for half in range(2):
                        at, cols = slice(k * P, (k + 1) * P), slice(k * D + half * F, k * D + (half + 1) * F)
                        mm = three_passes(pe, m.bank[2 + half][:, :], [hid_high[:, at], hid_low[:, at]],
                                          [m.high[:, c % 2, cols], m.low[:, c % 2, cols]], k == 0, k == 3)
                mm.then_inc(m.products, 4)

            def expert(turn, i, last=False):
                first(turn, i)
                if not last:
                    turn_x(turn, i + 1)
                second(turn, i)

            turn_x(0, 0)
            for i in range(4):
                expert(0, i)
            with pe.Fori(1, turns - 1) as turn:
                for i in range(4):
                    expert(turn, i)
            for i in range(4):
                expert(turns - 1, i, last=(i == 3))

        @block.scalar
        def _(act):
            def highs(turn, c):
                slot = c % 2
                if not isinstance(turn, int) or turn + c // 2 >= 1:
                    act.wait_ge(m.products, slabs_before(turn, c - 1))
                for j in range(4):
                    if j % 2 == 0:
                        act.wait_ge(m.half_loaded[2 * slot + j // 2],
                                    turn * 96 + (16 * (c // 2 + 1) + (16 * S_MOE if slot == 0 else 0)))
                    act.activation(m.high[:, slot, j * quarter:(j + 1) * quarter],
                                   m.half_slab[:, 2 * slot + j // 2, (j % 2) * quarter:(j % 2 + 1) * quarter],
                                   ACT.Copy).then_inc(m.highs, 1)

            def turned(turn, i):
                slot = i % 2
                for n in range(2):
                    act.wait_ge(xt_mm, turn * 8 + (2 * i + n + 1))
                    if n == 0 and (not isinstance(turn, int) or 4 * turn + i >= 2):
                        act.wait_ge(m.products, slabs_before(turn, 3 * (i - 2) + 2))
                    act.activation(x_high[:, slot, n * F:(n + 1) * F], m.bank[4 + n][:, :], ACT.Copy).then_inc(xt_high, 1)

            def expert(turn, i, last=False):
                highs(turn, 3 * i + 1)
                act.wait_ge(m.products, slabs_before(turn, 3 * i + 1))
                if not isinstance(turn, int) or turn + i >= 1:
                    act.wait_ge(hid_ready, turn * 4 + i)
                act.activation(gate[:, :], m.bank[0][:, :], ACT.Silu).then_inc(gated, 1)
                highs(turn, 3 * i + 2)
                if not last:
                    turned(turn, i + 1)
                act.wait_ge(hidt_mm, turn * 4 + (i + 1))
                act.activation(hid_high[:, :], m.bank[6][:, :], ACT.Copy).then_inc(hidt_high, 1)
                if not last:
                    highs(turn, 3 * i + 3)

            turned(0, 0)
            highs(0, 0)
            for i in range(4):
                expert(0, i)
            with act.Fori(1, turns - 1) as turn:
                for i in range(4):
                    expert(turn, i)
            for i in range(4):
                expert(turns - 1, i, last=(i == 3))

        @block.vector
        def _(dve):
            def lows(turn, c):
                slot = c % 2
                for j in range(4):
                    part = slice(j * quarter, (j + 1) * quarter)
                    dve.wait_ge(m.highs, slabs_before(turn, c) + (j + 1))
                    dve.tensor_tensor(m.low[:, slot, part],
                                      m.half_slab[:, 2 * slot + j // 2, (j % 2) * quarter:(j % 2 + 1) * quarter],
                                      m.high[:, slot, part].bitcast(F32), ALU.subtract).then_inc(m.lows, 1)

            def turned(turn, i):
                for n in range(2):
                    part = slice(n * F, (n + 1) * F)
                    dve.wait_ge(xt_high, turn * 8 + (2 * i + n + 1))
                    dve.tensor_tensor(x_low[:, i % 2, part], m.bank[4 + n][:, :], x_high[:, i % 2, part].bitcast(F32),
                                      ALU.subtract).then_inc(xt_low, 1)

            def expert(turn, i, last=False):
                lows(turn, 3 * i + 1)
                lows(turn, 3 * i + 2)
                dve.wait_ge(gated, turn * 4 + (i + 1))
                dve.wait_ge(m.products, slabs_before(turn, 3 * i + 2))
                if not isinstance(turn, int) or turn + i >= 1:
                    dve.wait_ge(hidt_mm, turn * 4 + i)
                dve.tensor_tensor(hid[:, :], gate[:, :], m.bank[1][:, :], ALU.mult).then_inc(hid_ready, 1)
                if not last:
                    turned(turn, i + 1)
                dve.wait_ge(hidt_high, turn * 4 + (i + 1))
                dve.tensor_tensor(hid_low[:, :], m.bank[6][:, :], hid_high[:, :].bitcast(F32), ALU.subtract).then_inc(hidt_low, 1)
                if not last:
                    lows(turn, 3 * i + 3)
                slot = i % 2
                if not isinstance(turn, int) or 4 * turn + i >= 2:
                    dve.wait_ge(y_out[slot], turn * 32 + (8 * i - 8 * slot))
                dve.wait_ge(m.products, slabs_before(turn, 3 * i + 3))
                for half in range(2):
                    dve.tensor_copy(y[:, slot, half * F:(half + 1) * F], m.bank[2 + half][:, :]).then_inc(y_sb, 1)

            turned(0, 0)
            lows(0, 0)
            for i in range(4):
                expert(0, i)
            with dve.Fori(1, turns - 1) as turn:
                for i in range(4):
                    expert(turn, i)
            for i in range(4):
                expert(turns - 1, i, last=(i == 3))


def stage_combine(nc, m, xT):
    with ExitStack() as own:
        rows = own.enter_context(nc.sbuf_tensor("cmb_rows", [P, 2, 2, D], F32))
        arrived = [m.sem(f"cmb_in{i}") for i in range(2)]
        mixed, turned, added = (m.sem(f"cmb_{v}") for v in ("mixed", "turned", "added"))
        block = own.enter_context(nc.Block(no_gpsimd_drain=True))

        @block.gpsimd
        def _(pool):
            for t in range(TT):
                if t >= 2:
                    pool.wait_ge(turned, 2 * (t - 1))
                for k in range(2):
                    pool.indirect_dma_start(
                        out=rows[:, t % 2, k, :], out_offset=None, in_=m.dram.y_rows,
                        in_offset=bass.IndirectOffsetOnAxis(ap=m.pair_row[:, k, t:t + 1], axis=0)
                    ).then_inc(arrived[t % 2], 16)

        @block.vector
        def _(dve):
            chain = lambda instruction: m.chain(dve, instruction)

            def mix(t):
                dve.wait_ge(arrived[t % 2], 32 * (t // 2 + 1))
                y0, y1 = rows[:, t % 2, 0, :], rows[:, t % 2, 1, :]
                chain(dve.tensor_scalar(y0, y0, m.pair_w[:, 0, t:t + 1], None, ALU.mult))
                dve.scalar_tensor_tensor(out=y0, in0=y1, scalar=m.pair_w[:, 1, t:t + 1], in1=y0,
                                         op0=ALU.mult, op1=ALU.add).then_inc(mixed, 1)

            mix(0)
            for t in range(TT):
                if t + 1 < TT:
                    mix(t + 1)
                for k in range(DC):
                    dve.wait_ge(turned, 2 * t + k // 4 + 1)
                    out = xT[:, k, t * P:(t + 1) * P]
                    dve.scalar_tensor_tensor(out=out, in0=m.bank[2 * (t % 2) + k // 4][:, (k % 4) * P:(k % 4 + 1) * P],
                                             scalar=m.mod[:, 40 + k:41 + k], in1=out, op0=ALU.mult,
                                             op1=ALU.add).then_inc(added, 1)

        @block.tensor
        def _(pe):
            for t in range(TT):
                pe.wait_ge(mixed, t + 1)
                if t >= 2:
                    pe.wait_ge(added, DC * (t - 1))
                for k in range(DC):
                    mm = pe.transpose(m.bank[2 * (t % 2) + k // 4][:, (k % 4) * P:(k % 4 + 1) * P],
                                      rows[:, t % 2, 0, k * P:(k + 1) * P], m.ident)
                    if k % 4 == 3:
                        mm.then_inc(turned, 1)


def stage_in2(nc, m, hT, qT, kT, vals, poolT, d_pool):
    m.begin(S_IN2)
    with ExitStack() as own:
        sb = lambda name, shape: own.enter_context(nc.sbuf_tensor("in2_" + name, shape, F32))
        squares = sb("sq", [P, 2, T])
        std = sb("std", [P, 2, T])
        run = sb("run", [P, 2, T])
        tail = sb("tail", [P, 16])
        sq_ready, total, root, normed = (m.sem(f"in2_{v}") for v in ("sq", "total", "root", "normed"))
        block = own.enter_context(nc.Block(no_gpsimd_drain=True))
        heads = [(S_IN2, j) for j in range(4)] + [(S_IN2 + 2, 0)]

        @block.sync
        def _(sp):
            load_halves(m, sp, S_IN2 + 2, S_IN2 + 5)

        @block.gpsimd
        def _(pool):
            for s in range(S_IN2 + 1, S_IN2 + 4):
                pool_low(m, pool, s, s % 2)

        @block.tensor
        def _(pe):
            def norm(n):
                pe.wait_ge(sq_ready, n + 1)
                if n >= 2:
                    pe.wait_ge(root, n - 1)
                pe.matmul(m.bank[4 + n % 2][:, :], m.halves, squares[:, n % 2, :], start=True, stop=True).then_inc(total, 1)

            pe_features(m, pe, S_IN2, hT)
            for n in range(4):
                norm(n)
            pe_features(m, pe, S_IN2 + 1, hT)
            pe_features(m, pe, S_IN2 + 2, hT, tiles=1)
            norm(4)
            slot = (S_IN2 + 2) % 2
            pe.wait_ge(m.lows, split_number(S_IN2 + 3))
            m.wait_bank(pe, S_IN2 + 2, 1)
            for t in range(TT):
                for k in range(DC):
                    tok, at = slice(t * P, (t + 1) * P), slice(D + k * P, D + (k + 1) * P)
                    mm = three_passes(pe, m.bank[1][:, tok], [hT[0][:, k, tok], hT[1][:, k, tok]],
                                      [m.high[:, slot, at], m.low[:, slot, at]], k == 0, k == DC - 1)
            mm.then_inc(m.products, 3)

        @block.scalar
        def _(act):
            for n, (s, j) in enumerate(heads):
                if n == 4:
                    for s1 in (S_IN2 + 2, S_IN2 + 3):
                        for j1 in range(4):
                            act_high(m, act, s1, j1, s1 % 2)
                m.wait_product(act, s, j)
                if n >= 2:
                    act.wait_ge(total, n - 1)
                act.activation(squares[:, n % 2, :], m.bank[j][:, :], ACT.Square).then_inc(sq_ready, 1)
                if n < 4:
                    act_high(m, act, S_IN2 + 1, n, (S_IN2 + 1) % 2)
                act.wait_ge(total, n + 1)
                if n >= 2:
                    act.wait_ge(normed, n - 1)
                act.activation(std[:, n % 2, :], m.bank[4 + n % 2][:, :], ACT.Sqrt, bias=m.eps[:, :],
                               scale=1.0 / HD).then_inc(root, 1)
            act.wait_ge(m.products, 4 * (S_IN2 + 3))
            act.activation(vals[:, :, :], m.bank[1][:, :].rearrange("p (t n) -> p t n", n=P), ACT.Copy)

        @block.vector
        def _(dve):
            chain = lambda instruction: m.chain(dve, instruction)

            def head(n, dst, gain):
                s, j = heads[n]
                dve.wait_ge(root, n + 1)
                chain(dve.reciprocal(std[:, n % 2, :], std[:, n % 2, :]))
                chain(dve.scalar_tensor_tensor(out=dst, in0=m.bank[j][:, :], scalar=gain, in1=std[:, n % 2, :],
                                               op0=ALU.mult, op1=ALU.mult))
                dve.sem_inc(normed, 1)
                dve.sem_inc(m.emptied, 1)

            chain(dve.tensor_scalar(m.small[:, 0:1], m.small[:, 0:1], float(HD) ** -0.5, None, ALU.mult))
            for n in range(4):
                head(n, qT[:, n, :], m.small[:, 0:1])
            for g in range(4):
                m.wait_product(dve, S_IN2 + 1, g)
                chain(dve.tensor_copy(poolT[:, g, :], m.bank[g][:, :]))
                dve.sem_inc(m.emptied, 1)
            head(4, kT[:, :], m.small[:, 1:2])
            for g in range(4):
                window = 2 << g
                src = poolT[:, g, :]
                step = 1
                a = 0
                while step < window:
                    chain(dve.tensor_copy(run[:, a, 0:step], src[:, 0:step]))
                    chain(dve.tensor_tensor(run[:, a, step:T], src[:, step:T], src[:, 0:T - step], ALU.add))
                    src = run[:, a, :]
                    a = 1 - a
                    step *= 2
                chain(dve.scalar_tensor_tensor(out=d_pool[:, g, :], in0=src, scalar=1.0 / window, in1=poolT[:, g, :],
                                               op0=ALU.mult, op1=ALU.subtract))
                chain(dve.tensor_tensor(tail[:, :], src[:, 0:16], m.const[:, C_COUNT + 16 * g:C_COUNT + 16 * (g + 1)], ALU.mult))
                chain(dve.tensor_tensor(d_pool[:, g, 0:16], tail[:, :], poolT[:, g, 0:16], ALU.subtract))
    m.end(9)


def stage_window(nc, m, qT, kT, vals, d_pool, cat):
    with ExitStack() as own:
        sb = lambda name, shape: own.enter_context(nc.sbuf_tensor("swa_" + name, shape, F32))
        H = SWA_HEADS
        bias = sb("bias", [P, H, BAND])
        sc = sb("sc", [P, H, BAND])
        pT = sb("pT", [P, 2 * H, P])
        mx = sb("mx", [P, 2, H // 2])
        es = sb("es", [P, 2, H // 2])
        den = sb("den", [P, 2, H // 2])
        pool_w = sb("pool_w", [P, 4, P])
        loads, scores, shifted, exped, probs, turned, turned_sb, out_ready, out_sb, sinks_e, pooled, scored = (
            m.sem(f"swa_{v}") for v in ("loads", "scores", "shifted", "exped", "probs", "turned", "turned_sb", "out",
                                        "out_sb", "sinks", "pooled", "scored"))
        block = own.enter_context(nc.Block(no_gpsimd_drain=True))
        d = m.dram

        @block.sync
        def _(sp):
            for h in range(H):
                sp.dma_start(bias[:, h, :], d.bias_band[h]).then_inc(loads, 16)
            sp.dma_start(pool_w[:, :, :], d.pool_w).then_inc(loads, 16)
            sp.wait_ge(loads, 16 * (H + 1))

        units = [(t, half) for t in range(TT) for half in range(2)]

        def first_key(t):
            return P if t == 0 else 0

        @block.tensor
        def _(pe):
            pe.wait_ge(loads, 16 * (H + 1))
            for g in range(4):
                mm = pe.matmul(m.bank[g][:, :], pool_w[:, g, :], d_pool[:, g, :], start=True, stop=True)
            mm.then_inc(pooled, 1)
            pe.wait_ge(out_sb, 1)

            def score(u):
                t, half = units[u]
                lo = first_key(t)
                if u >= 2:
                    pe.wait_ge(scored, u - 1)
                r = HD * half
                for c in range(4):
                    mm = pe.matmul(m.bank[2 * half + c // 2][:, (c % 2) * BAND + lo:(c % 2 + 1) * BAND],
                                   qT[r:r + HD, c, t * P:(t + 1) * P],
                                   kT[r:r + HD, (t - 1) * P + lo:(t + 1) * P], start=True, stop=True)
                mm.then_inc(scores, 1)

            score(0)
            score(1)
            for u, (t, half) in enumerate(units):
                first = first_key(t) // P
                pe.wait_ge(probs, u + 1)
                if u >= 1:
                    pe.wait_ge(turned_sb, u)
                for c in range(4):
                    for b in range(first, 2):
                        mm = pe.transpose(m.bank[4 + c // 2][:, (2 * (c % 2) + b) * P:(2 * (c % 2) + b + 1) * P],
                                          sc[:, 4 * half + c, b * P:(b + 1) * P], m.ident)
                mm.then_inc(turned, 1)
                if u + 2 < len(units):
                    score(u + 2)
                pe.wait_ge(turned_sb, u + 1)
                if u >= 2:
                    pe.wait_ge(out_sb, u)
                r = HD * half
                for c in range(4):
                    for b in range(first, 2):
                        mm = pe.matmul(m.bank[6 + half][r:r + HD, c * P:(c + 1) * P],
                                       vals[:, t - 1 + b, r:r + HD], pT[:, 8 * half + 2 * c + b, :],
                                       start=(b == first), stop=(b == 1))
                mm.then_inc(out_ready, 1)

        @block.scalar
        def _(act):
            def exponents(u):
                t, half = units[u]
                lo = first_key(t)
                act.wait_ge(shifted, u + 1)
                own_sc = sc[:, 4 * half:4 * half + 4, lo:]
                act.activation(own_sc, own_sc, ACT.Exp).then_inc(exped, 1)
                act.activation(es[:, half, :], es[:, half, :], ACT.Exp).then_inc(exped, 1)

            exponents(0)
            for u, (t, half) in enumerate(units):
                if u + 1 < len(units):
                    exponents(u + 1)
                first = first_key(t) // P
                act.wait_ge(turned, u + 1)
                if u >= 2:
                    act.wait_ge(out_ready, u - 1)
                act.activation(pT[:, 8 * half:8 * half + 8, :].rearrange("p (h b) q -> p h b q", b=2)[:, :, first:, :],
                               m.psum[:, 4:6, :].rearrange("p k (h b q) -> p (k h) b q", b=2, q=P)[:, :, first:, :],
                               ACT.Copy).then_inc(turned_sb, 1)

        @block.vector
        def _(dve):
            chain = lambda instruction: m.chain(dve, instruction)
            dve.wait_ge(pooled, 1)
            for g in range(4):
                last = dve.tensor_scalar(cat[:, 4 + g, :], m.bank[g][:, :], m.small[:, 2 + g:3 + g], None, ALU.mult)
            last.then_inc(out_sb, 1)
            dve.wait_ge(loads, 16 * (H + 1))
            chain(dve.tensor_tensor(bias[:, :, :], bias[:, :, :],
                                    bcast(m.const[:, C_MASK:C_MASK + BAND], 1, H), ALU.add))

            def shift(u):
                t, half = units[u]
                lo = first_key(t)
                own_sc, mine = sc[:, 4 * half:4 * half + 4, lo:], slice(4 * half, 4 * half + 4)
                dve.wait_ge(scores, u + 1)
                if u >= 2:
                    dve.wait_ge(turned, u - 1)
                chain(dve.tensor_tensor(own_sc, m.psum[:, 2 * half:2 * half + 2, :].rearrange(
                    "p k (h j) -> p (k h) j", j=BAND)[:, :, lo:], bias[:, mine, lo:], ALU.add))
                dve.sem_inc(scored, 1)
                chain(dve.tensor_reduce(mx[:, half, :], own_sc, AX.X, ALU.max))
                chain(dve.tensor_tensor(mx[:, half, :], mx[:, half, :], m.sinks[:, mine], ALU.max))
                dve.tensor_tensor(own_sc, own_sc, bcast(mx[:, half, :], 2, BAND - lo), ALU.subtract)
                dve.tensor_tensor(es[:, half, :], m.sinks[:, mine], mx[:, half, :], ALU.subtract).then_inc(shifted, 1)

            def output(u):
                t, half = units[u]
                r = HD * half
                dve.wait_ge(out_ready, u + 1)
                dve.tensor_copy(cat[r:r + HD, 0:4, t * P:(t + 1) * P],
                                m.bank[6 + half][r:r + HD, :].rearrange("p (h q) -> p h q", q=P)).then_inc(out_sb, 1)

            shift(0)
            for u, (t, half) in enumerate(units):
                if u + 1 < len(units):
                    shift(u + 1)
                own_sc = sc[:, 4 * half:4 * half + 4, first_key(t):]
                dve.wait_ge(exped, 2 * (u + 1))
                chain(dve.tensor_reduce(den[:, half, :], own_sc, AX.X, ALU.add))
                chain(dve.tensor_tensor(den[:, half, :], den[:, half, :], es[:, half, :], ALU.add))
                chain(dve.reciprocal(den[:, half, :], den[:, half, :]))
                dve.tensor_tensor(own_sc, own_sc, bcast(den[:, half, :], 2, BAND - first_key(t)), ALU.mult).then_inc(probs, 1)
                if u >= 1:
                    output(u - 1)
            output(len(units) - 1)


def stage_peer_u(nc, m, hT, xT):
    H, K = PH, TOPK
    HALF = PK // 8
    NB = 64
    with ExitStack() as own:
        sb = lambda name, shape, dt=F32: own.enter_context(nc.sbuf_tensor("pu_" + name, shape, dt))
        gl = xT[:, 0:4, :].rearrange("p (a c) t -> p a c t", a=2)
        hot1 = xT[:, 4:6, :].rearrange("p a (c k) -> p (a c) k", k=PK)
        hot2 = xT[:, 6:8, :].rearrange("p a (c k) -> p (a c) k", k=PK)
        e_turned = sb("e_turned", [P, 3, T])
        iota = m.const[:, C_IOTA:C_IOTA + P]
        loads, scored, score_sb, picked, turned, turned_sb, act_ready, act_out = (
            m.sem(f"pu_{v}") for v in ("loads", "scored", "score_sb", "picked", "turned", "turned_sb", "act", "act_out"))
        gl_out = [m.sem(f"pu_gl{i}") for i in range(2)]
        x_out = m.sem("pu_x_out")
        d = m.dram
        first = 4 * S_U

        def u_chunk(pe, slot, j):
            for k in range(DC):
                at = slice((j * DC + k) * P, (j * DC + k + 1) * P)
                mm = three_passes(pe, m.bank[j % 2][:, :], [m.high[:, slot, at], m.low[:, slot, at]],
                                  [hT[0][:, k, :], hT[1][:, k, :]], k == 0, k == DC - 1)
            mm.then_inc(m.products, 1)

        with ExitStack() as half:
            hb = lambda name, shape, dt=F32: half.enter_context(nc.sbuf_tensor("pk_" + name, shape, dt))
            qT = hb("q", [P, 2 * H, T])
            stage_linear_split(nc, m, "wq", [(S_WQ + i, hT, "copy", qT, 4 * i) for i in range(4)])
            subkeys = hb("subkeys", [P, 2 * H, PK])
            sc = hb("sc", [P, 2 * H, PK])
            sc2 = hb("sc2", [P, 2 * H, PK])
            val = hb("val", [P, 2 * H, K])
            idx = hb("idx", [P, 2 * H, K], U32)
            idf = hb("idf", [P, 2 * H, K])
            best = hb("best", [P, H, K])
            pos = hb("pos", [P, H, K], U32)
            part = hb("part", [P, H, K], U32)
            partf = hb("partf", [P, 2, H, K])
            res = hb("res", [P, 3, H, K])
            gs = hb("gs", [P, H])
            exp_ready, exp_done = m.sem("pk_exp_ready"), m.sem("pk_exp_done")
            block = half.enter_context(nc.Block(no_gpsimd_drain=True))

            @block.sync
            def _(sp):
                sp.dma_start(d.x_rows, xT[:, :, :]).then_inc(x_out, 16)
                sp.dma_start(subkeys[:, :, :], d.subkeys).then_inc(loads, 16)
                load_halves(m, sp, S_U + 2, S_U + HALF + 2)
                sp.wait_ge(x_out, 16)

            @block.gpsimd
            def _(pool):
                with pool.Fori(S_U + 1, S_U + HALF + 1, 2) as s:
                    pool_low(m, pool, s, (S_U + 1) % 2)
                    pool_low(m, pool, s + 1, S_U % 2)

            @block.tensor
            def _(pe):
                pe.wait_ge(loads, 16)

                def scores(t):
                    if t >= 1:
                        pe.wait_ge(score_sb, t)
                    for n in range(2 * H):
                        mm = pe.matmul(m.bank[2 + n // 4][:, (n % 4) * PK:(n % 4 + 1) * PK], qT[:, n, t * P:(t + 1) * P],
                                       subkeys[:, n, :], start=True, stop=True)
                    mm.then_inc(scored, 1)

                def turn(t):
                    pe.wait_ge(picked, t + 1)
                    if t >= 1:
                        pe.wait_ge(turned_sb, t)
                    for i in range(3):
                        mm = pe.transpose(m.bank[6][:, i * P:(i + 1) * P], res[:, i, :, :].rearrange("p h k -> p (h k)"), m.ident)
                    mm.then_inc(turned, 1)

                def u_slab(s, chunk):
                    for j in range(4):
                        pe.wait_ge(m.lows, split_number(s) + j + 1)
                        if chunk + j >= 2:
                            pe.wait_ge(act_ready, chunk + j - 1)
                        u_chunk(pe, s % 2, j)

                scores(0)
                for n in range(HALF):
                    u_slab(S_U + n, n * 4)
                    if n % 4 == 3 and n < HALF - 1 and n // 4 + 1 < TT:
                        turn(n // 4)
                        scores(n // 4 + 1)
                turn(TT - 1)

            def gelu_slab(act, n):
                if n == 0:
                    act.wait_ge(x_out, 16)
                for j in range(4):
                    act_high(m, act, S_U + n + 1, j, (S_U + n + 1) % 2)
                    act.wait_ge(m.products, 4 * n + (first + j + 1))
                    if n >= 1 and j % 2 == 0:
                        act.wait_ge(gl_out[j // 2], 16 * n)
                    act.activation(gl[:, j // 2, j % 2, :], m.bank[j % 2][:, :], ACT.Gelu).then_inc(act_ready, 1)
                    if j % 2 == 1:
                        act.wait_ge(act_ready, 4 * n + j + 1)
                        act.dma_start(d.gelu[n][:, j - 1:j + 1, :], gl[:, j // 2, :, :]).then_inc(gl_out[j // 2], 16)

            @block.scalar
            def _(act):
                for n in range(HALF):
                    if n % 4 == 0:
                        t = n // 4
                        act.wait_ge(scored, t + 1)
                        if t >= 1:
                            act.wait_ge(picked, t)
                        act.activation(sc[:, :, :], m.psum[:, 2:6, :].rearrange("p b (n k) -> p (b n) k", k=PK),
                                       ACT.Copy).then_inc(score_sb, 1)
                    gelu_slab(act, n)
                    if n % 4 == 2:
                        t = n // 4
                        act.wait_ge(exp_ready, t + 1)
                        act.activation(best[:, :, :], best[:, :, :], ACT.Exp).then_inc(exp_done, 1)
                    if n % 4 == 3:
                        t = n // 4
                        act.wait_ge(turned, t + 1)
                        act.activation(e_turned[:, :, t * P:(t + 1) * P],
                                       m.bank[6][:, 0:3 * P].rearrange("p (i q) -> p i q", q=P), ACT.Copy).then_inc(turned_sb, 1)

            @block.vector
            def _(dve):
                chain = lambda instruction: m.chain(dve, instruction)

                def top16(n, source, spare, values, places):
                    for i in range(n):
                        last = dve.max(out=values[:, i, 0:8], in_=source(i))
                    chain(last)
                    for i in range(n):
                        dve.max_index(places[:, i, 0:8], values[:, i, 0:8], source(i))
                        last = dve.match_replace(out=spare(i), in_to_replace=values[:, i, 0:8], in_values=source(i),
                                                 imm_value=LOWEST)
                    chain(last)
                    for i in range(n):
                        last = dve.max(out=values[:, i, 8:16], in_=spare(i))
                    chain(last)
                    for i in range(n):
                        last = dve.max_index(places[:, i, 8:16], values[:, i, 8:16], spare(i))
                    chain(last)

                for t in range(TT):
                    dve.wait_ge(score_sb, t + 1)
                    top16(2 * H, lambda i: sc[:, i, :], lambda i: sc2[:, i, :], val, idx)
                    chain(dve.tensor_copy(idf[:, :, :], idx[:, :, :]))
                    cand = sc[:, :, :].rearrange("p (h a) k -> p h (a k)", a=2)
                    cand2 = sc2[:, :, :].rearrange("p (h a) k -> p h (a k)", a=2)
                    for h in range(H):
                        last = dve.tensor_tensor(cand[:, h, :].rearrange("p (i j) -> p i j", j=K),
                                                 bcast(val[:, 2 * h, :], 2, K), bcast(val[:, 2 * h + 1, :], 1, K), ALU.add)
                    chain(last)
                    top16(H, lambda i: cand[:, i, :], lambda i: cand2[:, i, :], best, pos)
                    chain(dve.tensor_scalar(part[:, :, :], pos[:, :, :], 4, None, ALU.logical_shift_right))
                    chain(dve.tensor_copy(partf[:, 0, :, :], part[:, :, :]))
                    chain(dve.tensor_scalar(part[:, :, :], pos[:, :, :], 15, None, ALU.bitwise_and))
                    chain(dve.tensor_copy(partf[:, 1, :, :], part[:, :, :]))
                    pick = sc[:, :, :].rearrange("p (h a) k -> p h (a k)", a=2)
                    for which in range(2):
                        for h in range(H):
                            last = dve.tensor_tensor(pick[:, h, :].rearrange("p (i j) -> p i j", j=K),
                                                     bcast(partf[:, which, h, :], 2, K), bcast(iota[:, 0:K], 1, K), ALU.is_equal)
                        chain(last)
                        for h in range(H):
                            one = pick[:, h, :].rearrange("p (i j) -> p i j", j=K)
                            last = dve.tensor_tensor(one, one, bcast(idf[:, 2 * h + which, :], 1, K), ALU.mult)
                        chain(last)
                        if which == 0 and t >= 1:
                            dve.wait_ge(turned, t)
                        chain(dve.tensor_reduce(res[:, which, :, :], pick[:, :, :].rearrange("p h (i j) -> p h i j", j=K),
                                                AX.X, ALU.add))
                    chain(dve.tensor_copy(gs[:, :], best[:, :, 0]))
                    chain(dve.tensor_tensor(best[:, :, :], best[:, :, :], bcast(gs[:, :], 2, K), ALU.subtract))
                    dve.sem_inc(exp_ready, 1)
                    dve.wait_ge(exp_done, t + 1)
                    chain(dve.tensor_reduce(gs[:, :], best[:, :, :], AX.X, ALU.add))
                    chain(dve.reciprocal(gs[:, :], gs[:, :]))
                    dve.tensor_tensor(res[:, 2, :, :], best[:, :, :], bcast(gs[:, :], 2, K), ALU.mult).then_inc(picked, 1)

        with ExitStack() as half:
            hb = lambda name, shape, dt=F32: half.enter_context(nc.sbuf_tensor("pg_" + name, shape, dt))
            table = hb("table", [P, 2, PK, NB])
            hot_ready, gates_mm, gates_sb = (m.sem(f"pg_{v}") for v in ("hot", "mm", "sb"))
            table_out = [m.sem(f"pg_out{i}") for i in range(2)]
            block = half.enter_context(nc.Block(no_gpsimd_drain=True))
            QUADS = T // 4
            STEPS = QUADS // (4 * HALF)
            assert STEPS * 4 * HALF == QUADS and NB % 32 == 0
            turns = HALF // 4

            @block.sync
            def _(sp):
                load_halves(m, sp, S_U + HALF + 2, S_V + 2)

            @block.gpsimd
            def _(pool):
                with pool.Fori(S_U + HALF + 1, S_V + 1, 2) as s:
                    pool_low(m, pool, s, (S_U + 1) % 2)
                    pool_low(m, pool, s + 1, S_U % 2)
                for i in range(2):
                    pool.wait_ge(gl_out[i], 16 * 2 * HALF)

            @block.tensor
            def _(pe):
                with pe.Fori(0, turns) as turn:
                    for i in range(4):
                        n = turn * 4 + (HALF + i)
                        for j in range(4):
                            pe.wait_ge(m.lows, n * 4 + (split_number(S_U) + j + 1))
                            pe.wait_ge(act_ready, n * 4 + (j - 1))
                            u_chunk(pe, (S_U + i) % 2, j)
                            for b in range(STEPS):
                                at = (4 * i + j) * STEPS + b
                                quad = turn * (16 * STEPS) + at
                                pe.wait_ge(hot_ready, quad + 1)
                                pe.wait_ge(gates_sb, quad + 1)
                                for c in range(4):
                                    mm = pe.matmul(m.bank[4 + at % 4][:, c * PK:(c + 1) * PK], hot2[:, 4 * (at % 2) + c, :],
                                                   hot1[:, 4 * (at % 2) + c, :], start=True, stop=True)
                                mm.then_inc(gates_mm, 1)

            @block.vector
            def _(dve):
                dve.sem_inc(gates_mm, 2)
                dve.sem_inc(gates_sb, 4)
                for i in range(2):
                    dve.sem_inc(table_out[i], 16)
                with dve.Fori(0, turns) as turn:
                    for at in range(16 * STEPS):
                        quad = turn * (16 * STEPS) + at
                        dve.wait_ge(gates_mm, quad + 1)
                        for c in range(4):
                            token = turn * (64 * STEPS) + (4 * at + c)
                            dve.tensor_scalar(hot2[:, 4 * (at % 2) + c, :], iota, e_turned[:, 1, bass.ds(token, 1)],
                                              None, ALU.is_equal)
                            last = dve.tensor_scalar(hot1[:, 4 * (at % 2) + c, :], iota, e_turned[:, 0, bass.ds(token, 1)],
                                                     e_turned[:, 2, bass.ds(token, 1)], ALU.is_equal, ALU.mult)
                        last.then_inc(hot_ready, 1)

            @block.scalar
            def _(act):
                parts = 16 * STEPS // (NB // 4)
                with act.Fori(0, turns) as turn:
                    for i in range(4):
                        n = turn * 4 + (HALF + i)
                        for j in range(4):
                            act_high(m, act, n + (S_U + 1), j, (S_U + i + 1) % 2)
                            act.wait_ge(m.products, 4 * n + (first + j + 1))
                            if j % 2 == 0:
                                act.wait_ge(gl_out[j // 2], 16 * n)
                            act.activation(gl[:, j // 2, j % 2, :], m.bank[j % 2][:, :], ACT.Gelu).then_inc(act_ready, 1)
                            if j % 2 == 1:
                                act.wait_ge(act_ready, 4 * n + (j + 1))
                                act.dma_start(d.gelu[bass.ds(n, 1)].rearrange("o p c t -> (o p) c t")[:, j - 1:j + 1, :],
                                              gl[:, j // 2, :, :]).then_inc(gl_out[j // 2], 16)
                            for b in range(STEPS):
                                at = (4 * i + j) * STEPS + b
                                quad = turn * (16 * STEPS) + at
                                part = at // (NB // 4)
                                q = at % (NB // 4)
                                if q == 0:
                                    act.wait_ge(table_out[part % 2], (turn * parts + (part - part % 2)) * 8 + 16)
                                act.wait_ge(gates_mm, quad + 3)
                                act.activation(table[:, part % 2, :, 4 * q:4 * q + 4].rearrange("p e c -> p c e"),
                                               m.bank[4 + at % 4][:, :].rearrange("p (c e) -> p c e", e=PK),
                                               ACT.Copy).then_inc(gates_sb, 1)
                                if q == NB // 4 - 1:
                                    act.wait_ge(gates_sb, quad + 5)
                                    t0 = (turn * parts + part) * NB
                                    act.dma_start(d.gates[:, :, bass.ds(t0, NB)], table[:, part % 2, :, :]).then_inc(table_out[part % 2], 16)
                for i in range(2):
                    act.wait_ge(table_out[i], 16 + 16 * turns * parts // 2)


def stage_peer_v(nc, m, h, xT):
    with ExitStack() as own:
        sb = lambda name, shape, dt=F32: own.enter_context(nc.sbuf_tensor("pv_" + name, shape, dt))
        gl = sb("gl", [P, 2, 4, T])
        gt = sb("gt", [P, 2, 4, T])
        coef = sb("coef", [P, 2, 4, T])
        coef_high, coef_low = (part[:, :, :].rearrange("p (a c) t -> p a c t", a=2) for part in h)
        zero = sb("zero", [P, T])
        gl_in = [m.sem(f"pv_gl{i}") for i in range(2)]
        gt_in = [m.sem(f"pv_gt{i}") for i in range(2)]
        x_in, zeroed, coef_ready, high_ready, low_ready, out_ready, done, stored = (
            m.sem(f"pv_{v}") for v in ("x_in", "zeroed", "coef", "high", "low", "out", "done", "stored"))
        block = own.enter_context(nc.Block(no_gpsimd_drain=True))
        N = PK // 4
        d = m.dram
        FIRST = 4 * S_V

        @block.sync
        def _(sp):
            sp.dma_start(xT[:, :, :], d.x_rows).then_inc(x_in, 16)
            load_halves(m, sp, S_V + 2, S_END)
            for k in range(DC):
                sp.wait_ge(done, k + 1)
                sp.dma_start(d.out[:, k, :], xT[:, k, :]).then_inc(stored, 16)
            sp.wait_ge(stored, 16 * DC)

        @block.gpsimd
        def _(pool):
            with pool.Fori(S_V + 1, S_END - 1, 2) as s:
                pool_low(m, pool, s, (S_V + 1) % 2)
                pool_low(m, pool, s + 1, S_V % 2)
            pool_low(m, pool, S_END - 1, (S_END - 1) % 2)

        @block.scalar
        def _(act):
            def one(n, i, ahead=True):
                act.wait_ge(coef_ready, 4 * n + 4)
                gl_src = d.gelu[n] if isinstance(n, int) else d.gelu[bass.ds(n, 1)].rearrange("o p c t -> (o p) c t")
                act.dma_start(gl[:, i, :, :], gl_src).then_inc(gl_in[i], 16)
                act.dma_start(gt[:, i, :, :], d.gates[:, bass.ds(n * 4, 4), :]).then_inc(gt_in[i], 16)

            def highs(n, i):
                for j in range(4):
                    act.wait_ge(coef_ready, 4 * n + (j + 9))
                    if j == 0 and (not isinstance(n, int) or n >= 2):
                        act.wait_ge(m.products, 4 * n + (FIRST - 4))
                    act.activation(coef_high[:, i, j, :], coef[:, i, j, :], ACT.Copy).then_inc(high_ready, 1)

            def slab(n, i):
                for j in range(4):
                    act_high(m, act, n + (S_V + 1), j, (S_V + i + 1) % 2)

            one(0, 0)
            one(1, 1)
            highs(0, 0)
            slab(0, 0)
            one(2, 0)
            highs(1, 1)
            slab(1, 1)
            with act.Fori(2, N - 2, 2) as n:
                one(n + 1, 1)
                highs(n, 0)
                slab(n, 0)
                one(n + 2, 0)
                highs(n + 1, 1)
                slab(n + 1, 1)
            one(N - 1, 1)
            highs(N - 2, 0)
            slab(N - 2, 0)
            highs(N - 1, 1)

        @block.vector
        def _(dve):
            dve.memset(zero[:, :], 0.0).then_inc(zeroed, 1)
            dve.sem_inc(coef_ready, 8)

            def product(n, i):
                dve.wait_ge(gl_in[i], n * 8 + (16 - 8 * i))
                dve.wait_ge(gt_in[i], n * 8 + (16 - 8 * i))
                for j in range(4):
                    if not isinstance(n, int) or n >= 2:
                        dve.wait_ge(low_ready, 4 * n + (j - 7))
                    dve.tensor_tensor(coef[:, i, j, :], gl[:, i, j, :], gt[:, i, j, :], ALU.mult).then_inc(coef_ready, 1)

            def lows(n, i):
                for j in range(4):
                    dve.wait_ge(high_ready, 4 * n + (j + 1))
                    dve.tensor_tensor(coef_low[:, i, j, :], coef[:, i, j, :], coef_high[:, i, j, :].bitcast(F32),
                                      ALU.subtract).then_inc(low_ready, 1)

            product(0, 0)
            product(1, 1)
            lows(0, 0)
            lows(1, 1)
            with dve.Fori(2, N, 2) as n:
                product(n, 0)
                product(n + 1, 1)
                lows(n, 0)
                lows(n + 1, 1)
            dve.wait_ge(x_in, 16)
            for k in range(DC):
                dve.wait_ge(out_ready, k + 1)
                dve.tensor_tensor(xT[:, k, :], m.bank[k][:, :], xT[:, k, :], ALU.add).then_inc(done, 1)

        @block.tensor
        def _(pe):
            pe.wait_ge(zeroed, 1)
            for k in range(DC):
                pe.matmul(m.bank[k][:, :], zero[:, 0:P], zero[:, :], start=True, stop=False)
            with pe.Fori(0, N, 2) as pair:
                for i in range(2):
                    n = pair + i
                    for j in range(4):
                        pe.wait_ge(m.lows, n * 4 + (split_number(S_V) + j + 1))
                        pe.wait_ge(low_ready, n * 4 + (j + 1))
                        for k in range(DC):
                            at = slice(j * D + k * P, j * D + (k + 1) * P)
                            mm = three_passes(pe, m.bank[k][:, :], [m.high[:, (S_V + i) % 2, at], m.low[:, (S_V + i) % 2, at]],
                                              [coef_high[:, i, j, :], coef_low[:, i, j, :]], False, False)
                        mm.then_inc(m.products, 1)
            for k in range(DC):
                pe.matmul(m.bank[k][:, :], zero[:, 0:P], zero[:, :], start=False, stop=True).then_inc(out_ready, 1)


def stage_overflow(nc, m):
    F = 512
    with ExitStack() as own:
        sb = lambda name, shape, dt=F32: own.enter_context(nc.sbuf_tensor("ov_" + name, shape, dt))
        w = sb("w", [P, 3, SLAB])
        x = sb("x", [P, D])
        xT = sb("xT", [P, D])
        gate = sb("gate", [P, F])
        hid = sb("hid", [P, F])
        hidT = sb("hidT", [P, F])
        y = sb("y", [P, D])
        ids = sb("ids", [P, 1], I32)
        w_in = [m.sem(f"ov_w{i}") for i in range(3)]
        ids_ready, x_in, xt_mm, xt_sb, gu, gated, hid_ready, hidt_mm, hidt_sb, y_mm, y_sb, y_out = (
            m.sem(f"ov_{v}") for v in ("ids", "x", "xt_mm", "xt_sb", "gu", "gated", "hid", "hidt_mm", "hidt_sb",
                                       "y_mm", "y_sb", "y_out"))
        carrier = m.sem("ov_carrier")
        block = own.enter_context(nc.Block(no_gpsimd_drain=True))
        d = m.dram

        def each(engine, body):
            number = engine.value_load(m.steer[0:1, OVER:OVER + 1], min_val=0, max_val=OVER)
            with engine.Fori(0, OVER) as b:
                with engine.If(b < number):
                    body(b)

        @block.sync
        def _(sp):
            sp.sem_inc(gu, 2)
            sp.sem_inc(y_mm, 1)

            def body(b):
                e = sp.value_load(m.steer[0:1, bass.ds(b, 1)], min_val=0, max_val=EXPERTS - 1)
                for i in range(3):
                    if i < 2:
                        sp.wait_ge(gu, b * 2 + (i + 1))
                    else:
                        sp.wait_ge(y_mm, b + 1)
                    sp.dma_start(w[:, i, :], m.weights[bass.ds(e * 3 + (S_MOE + i), 1)].rearrange("a p n -> (a p) n")
                                 ).then_inc(w_in[i], 16)
            each(sp, body)

        @block.gpsimd
        def _(pool):
            def gather():
                pool.indirect_dma_start(out=x[:, :], out_offset=None, in_=d.h_rows,
                                        in_offset=bass.IndirectOffsetOnAxis(ap=ids[:, 0:1], axis=0)).then_inc(x_in, 16)

            def body(b):
                pool.wait_ge(xt_mm, b + 1)
                pool.wait_ge(ids_ready, b + 2)
                pool.sem_inc(carrier, 1)
                gather()
                pool.wait_ge(x_in, b * 16 + 32)
                pool.sem_inc(carrier, 1)

            pool.wait_ge(ids_ready, 1)
            gather()
            pool.wait_ge(x_in, 16)
            each(pool, body)

        @block.tensor
        def _(pe):
            def body(b):
                pe.wait_ge(x_in, b * 16 + 16)
                for k in range(DC):
                    mm = pe.transpose(m.bank[4 + k // 4][:, (k % 4) * P:(k % 4 + 1) * P], x[:, k * P:(k + 1) * P], m.ident)
                mm.then_inc(xt_mm, 1)
                pe.wait_ge(xt_sb, b * 2 + 2)
                for i in range(2):
                    pe.wait_ge(w_in[i], b * 16 + 16)
                    for k in range(DC):
                        mm = pe.matmul(m.bank[i][:, :], xT[:, k * P:(k + 1) * P], w[:, i, k * F:(k + 1) * F],
                                       start=(k == 0), stop=(k == DC - 1))
                    mm.then_inc(gu, 1)
                pe.wait_ge(hid_ready, b + 1)
                for k in range(4):
                    mm = pe.transpose(m.bank[6][:, k * P:(k + 1) * P], hid[:, k * P:(k + 1) * P], m.ident)
                mm.then_inc(hidt_mm, 1)
                pe.wait_ge(hidt_sb, b + 1)
                pe.wait_ge(w_in[2], b * 16 + 16)
                for half in range(2):
                    for k in range(4):
                        mm = pe.matmul(m.bank[2 + half][:, :], hidT[:, k * P:(k + 1) * P],
                                       w[:, 2, k * D + half * F:k * D + (half + 1) * F], start=(k == 0), stop=(k == 3))
                mm.then_inc(y_mm, 1)
                pe.wait_ge(y_sb, b * 2 + 2)
            each(pe, body)

        @block.scalar
        def _(act):
            act.sem_inc(y_out, 16)

            def body(b):
                act.wait_ge(xt_mm, b + 1)
                for i in range(2):
                    act.activation(xT[:, i * F:(i + 1) * F], m.bank[4 + i][:, :], ACT.Copy).then_inc(xt_sb, 1)
                act.wait_ge(gu, b * 2 + 3)
                act.activation(gate[:, :], m.bank[0][:, :], ACT.Silu).then_inc(gated, 1)
                act.wait_ge(hidt_mm, b + 1)
                act.activation(hidT[:, :], m.bank[6][:, :], ACT.Copy).then_inc(hidt_sb, 1)
                act.wait_ge(y_sb, b * 2 + 2)
                act.dma_start(d.y_rows[bass.ds(b * SLOTS + EXPERTS * SLOTS, SLOTS), :], y[:, :]).then_inc(y_out, 16)
                act.wait_ge(y_out, b * 16 + 32)
                act.sem_inc(carrier, 1)
            each(act, body)

        @block.vector
        def _(dve):
            dve.tensor_copy(ids[:, :], m.tokens[:, EXPERTS:EXPERTS + 1]).then_inc(ids_ready, 1)

            def body(b):
                dve.wait_ge(gated, b + 1)
                dve.wait_ge(gu, b * 2 + 4)
                dve.tensor_tensor(hid[:, :], gate[:, :], m.bank[1][:, :], ALU.mult).then_inc(hid_ready, 1)
                dve.wait_ge(x_in, b * 16 + 16)
                dve.tensor_copy(ids[:, :], m.tokens[:, bass.ds(b + (EXPERTS + 1), 1)]).then_inc(ids_ready, 1)
                dve.wait_ge(y_mm, b + 2)
                dve.wait_ge(y_out, b * 16 + 16)
                for half in range(2):
                    dve.tensor_copy(y[:, half * F:(half + 1) * F], m.bank[2 + half][:, :]).then_inc(y_sb, 1)
            each(dve, body)


def program(nc, d):
    with ExitStack() as ctx:
        m = Names()
        m.dram = d
        m.weights = d.weights
        m.sem = lambda name: ctx.enter_context(nc.semaphore(name))
        keep = lambda name, shape, dt=F32: ctx.enter_context(nc.sbuf_tensor(name, shape, dt))
        m.psum = ctx.enter_context(nc.psum_tensor("psum", [P, 8, 512], F32))
        m.bank = [m.psum[:, i, :] for i in range(8)]
        m.tile_final, m.finals = m.sem("tile_final"), 0
        m.acts_high, m.acts_low, m.act_splits = m.sem("acts_high"), m.sem("acts_low"), 0
        m.half_loaded = [m.sem(f"half_loaded{i}") for i in range(4)]
        m.highs, m.lows = m.sem("slab_highs"), m.sem("slab_lows")
        m.products = m.sem("products")
        m.chain = Chain(m.sem("vector_order"))
        m.emptied, m.emptied_after = m.sem("banks_emptied"), 0
        m.gate_ready, m.gate_used, m.gates = m.sem("gate_ready"), m.sem("gate_used"), 0
        m.norm_sems, m.norms = [m.sem(f"norm_{x}") for x in ("squares", "total", "root", "scaled")], 0
        m.const = keep("const", [P, C_END])
        m.ident = m.const[:, C_IDENT:C_IDENT + P]
        m.ones = m.const[:, C_ONES:C_ONES + P]
        m.halves = m.const[:, C_HALVES:C_HALVES + P]
        m.causal = m.const[:, C_CAUSAL:C_CAUSAL + P]
        m.before = m.const[:, C_BEFORE:C_BEFORE + P]
        m.vec = keep("vec", [P, 5, DC])
        m.small = keep("small", [P, 6])
        m.sinks = keep("sinks", [P, SWA_HEADS])
        m.dn = keep("dn", [P, 2])
        m.mod = keep("mod", [P, 48])
        m.b_ada, m.raw = keep("b_ada", [P, 48]), keep("mod_raw", [P, 48])
        m.ada_loaded, m.ada_used, m.c_ready = [m.sem(f"ada_loaded{i}") for i in range(3)], m.sem("ada_used"), m.sem("c_ready")
        m.scale = keep("scale", [P, 2, DC])
        m.eps = keep("eps", [P, 1])
        m.neg_lam = keep("neg_lam", [P, 1])
        m.tokens = keep("tokens", [P, BLOCKS], I32)
        m.pair_row = keep("pair_row", [P, 2, TT], I32)
        m.pair_w = keep("pair_w", [P, 2, TT])
        m.steer = keep("steer", [P, 8], I32)
        m.xT = keep("xT", [P, DC, T])
        xT = m.xT

        with ExitStack() as first:
            fb = lambda name, shape, dt=F32: first.enter_context(nc.sbuf_tensor(name, shape, dt))
            m.rot_cos = fb("rot_cos", [P, T])
            m.rot_sin = fb("rot_sin", [P, T])
            stage_modulation(nc, m)
            m.half_slab = fb("half_slab_1", [P, 2, SLAB // 2])
            m.high = fb("slab_high_1", [P, 1, SLAB], F32R)
            m.low = fb("slab_low_1", [P, 1, SLAB], F32R)
            m.split_slots = 1
            h = [fb("h_high_1", [P, DC, T], F32R), fb("h_low_1", [P, DC, T], F32R)]
            stage_norm_split(nc, m, "norm_mix", xT, h, m.scale[:, 0, :], m.mod[:, 0:8], first=0)
            merged = fb("merged", [P, DC, T])
            roT = fb("roT", [P, DC, T])
            with ExitStack() as qkv:
                qb = lambda name, shape: qkv.enter_context(nc.sbuf_tensor(name, shape, F32))
                qT, kT, vals = qb("ret_q", [P, 4, T]), qb("ret_k", [P, 4, T]), qb("ret_v", [P, TT, D])
                stage_project(nc, m, "retp", [(S_RQ, qT, 0), (S_RK, kT, 0)], [(S_RV, 0), (S_RV + 1, 512)], h, vals)
                stage_retention(nc, m, qT, kT, vals, roT)
            with ExitStack() as parts:
                ro = [parts.enter_context(nc.sbuf_tensor(name, [P, DC, T], F32R)) for name in ("ro_high", "ro_low")]
                stage_linear(nc, m, "ret_out", [
                    (S_RG, h, 0, "times_silu", (roT, 0), ro), (S_RG + 1, h, 0, "times_silu", (roT, 4), ro),
                    (S_GR, h, 0, "sigmoid", (merged, 0), None), (S_GR + 1, h, 0, "sigmoid", (merged, 4), None),
                    (S_RO, ro, DC, "times", (merged, 0), None), (S_RO + 1, ro, DC, "times", (merged, 4), None)],
                    modulates=True)
            with ExitStack() as qkv:
                qb = lambda name, shape: qkv.enter_context(nc.sbuf_tensor(name, shape, F32))
                qT, kT, vals = qb("diff_q", [P, DC, T]), qb("diff_k", [P, DC, T]), qb("diff_v", [P, TT, D])
                stage_project(nc, m, "diffp", [(S_DQ, qT, 0), (S_DQ + 1, qT, 4), (S_DK, kT, 0), (S_DK + 1, kT, 4)],
                              [(S_DV, 0), (S_DV + 1, 512)], h, vals)
                stage_diff(nc, m, qT, kT, vals, roT)
            with ExitStack() as parts:
                do = [parts.enter_context(nc.sbuf_tensor(name, [P, DC, T], F32R)) for name in ("do_high", "do_low")]
                other = parts.enter_context(nc.sbuf_tensor("diff_gate", [P, DC, T], F32))
                stage_linear(nc, m, "mix_out", [
                    (S_GD, h, 0, "sigmoid", (other, 0), None), (S_GD + 1, h, 0, "sigmoid", (other, 4), None),
                    (S_DO, do, DC, "add_times", (merged, 0, other), h),
                    (S_DO + 1, do, DC, "add_times", (merged, 4, other), h),
                    (S_OUT, h, 2 * DC, "add_scaled", (xT, 0, m.mod[:, 16:24]), None),
                    (S_OUT + 1, h, 2 * DC, "add_scaled", (xT, 4, m.mod[:, 16:24]), None)], source=(roT, do[0], do[1]))
        block_one = ctx.enter_context(ExitStack())
        m.half_slab = block_one.enter_context(nc.sbuf_tensor("half_slab_moe", [P, 4, SLAB // 2], F32))
        m.high, m.low = (block_one.enter_context(nc.sbuf_tensor(name, [P, 2, SLAB], F32R)) for name in ("slab_high_moe", "slab_low_moe"))
        hT = block_one.enter_context(nc.sbuf_tensor("hT", [P, DC, T], F32))
        stage_norm(nc, m, "norm_ffn", xT, hT, m.scale[:, 1, :], m.mod[:, 24:32], prefetch=True)
        stage_route(nc, m, hT)
        stage_experts(nc, m)
        stage_overflow(nc, m)
        stage_combine(nc, m, xT)
        stage_norm(nc, m, "norm_final", xT, xT, m.vec[:, 2, :], work=hT)
        block_one.close()

        m.half_slab = keep("half_slab", [P, 2, SLAB // 2])
        m.high = keep("slab_high", [P, 2, SLAB], F32R)
        m.low = keep("slab_low", [P, 2, SLAB], F32R)
        m.split_slots = 2
        h = [keep("h_high", [P, DC, T], F32R), keep("h_low", [P, DC, T], F32R)]
        stage_norm_split(nc, m, "norm1", xT, h, m.vec[:, 3, :], first=S_IN2)
        with ExitStack() as second:
            wb = lambda name, shape: second.enter_context(nc.sbuf_tensor(name, shape, F32))
            cat = wb("cat", [P, DC, T])
            with ExitStack() as attention:
                ab = lambda name, shape: attention.enter_context(nc.sbuf_tensor(name, shape, F32))
                qT, kT, vals = ab("swa_q", [P, 4, T]), ab("swa_k", [P, T]), ab("swa_v", [P, TT, P])
                d_pool = ab("d_pool", [P, 4, T])
                with ExitStack() as pool:
                    poolT = pool.enter_context(nc.sbuf_tensor("pooled", [P, 4, T], F32))
                    stage_in2(nc, m, h, qT, kT, vals, poolT, d_pool)
                stage_window(nc, m, qT, kT, vals, d_pool, cat)
            stage_linear_split(nc, m, "out2", [(S_OUT2, h, "add", xT, 0), (S_OUT2 + 1, h, "add", xT, 4)], source=cat)
        stage_norm_split(nc, m, "norm2", xT, h, m.vec[:, 4, :])
        stage_peer_u(nc, m, h, xT)
        stage_peer_v(nc, m, h, xT)


def kernel(**inputs):
    import numpy as np
    import concourse.bacc as bacc
    from concourse.bass_utils import run_bass_kernel_spmd

    a = {k: np.asarray(v) for k, v in inputs.items()}

    def rows_of(w, tiles=4):
        return w.reshape(DC, P, tiles, P).transpose(1, 2, 0, 3).reshape(P, -1)

    def wide(w):
        return w.reshape(-1, P, w.shape[1]).transpose(1, 0, 2).reshape(P, -1)

    def cut(w):
        return [w[:, i:i + 512] for i in range(0, w.shape[1], 512)]

    w_in, w_in2 = a["w_in"][0], a["w_in_2"][0]
    col = cut(w_in)
    slabs = [rows_of(c) for c in col[0:2]] + [wide(c) for c in col[2:4]] + [rows_of(c) for c in col[4:6]]
    slabs += [rows_of(c) for c in col[12:14]] + [rows_of(c) for c in cut(a["w_ret_o"][0])]
    slabs += [rows_of(c) for c in col[6:10]] + [wide(c) for c in col[10:12]]
    slabs += [rows_of(c) for c in col[14:16]] + [rows_of(c) for c in cut(a["w_diff_o"][0])]
    slabs += [rows_of(c) for c in cut(a["w_out"][0])]
    for e in range(EXPERTS):
        slabs += [wide(a["w_exp_gate"][0, e]), wide(a["w_exp_up"][0, e]), wide(a["w_exp_down"][0, e])]
    order = np.concatenate([np.arange(HD) + HD * h for j in range(4) for h in (j, j + 4)])
    slabs.append(rows_of(w_in2[:, order]))
    slabs.append(rows_of(w_in2[:, 768:1280]))
    kv = np.zeros((P, SLAB), np.float32)
    kv[:, 0:D] = rows_of(w_in2[:, 512:640], 1)
    kv[:, D:2 * D] = wide(w_in2[:, 640:768])
    slabs.append(kv)
    w_out2 = a["w_out_2"][0]
    w_out2 = np.concatenate([w_out2[order], w_out2[512:]], axis=0)
    slabs += [rows_of(c) for c in cut(w_out2)] + [rows_of(c) for c in cut(a["peer_wq_2"][0])]
    u_t = a["peer_u_2"][0].T
    slabs += [rows_of(c) for c in cut(u_t)]
    v = a["peer_v_2"][0].reshape(PK // 4, 4, P, D).transpose(0, 2, 1, 3).reshape(PK // 4, P, SLAB)
    weights = np.concatenate([np.stack(slabs), v])

    def cols(v):
        return np.ascontiguousarray(v.reshape(-1, P).T)

    r = np.arange(P)
    const = np.zeros((P, C_END), np.float32)
    const[:, C_IDENT:C_IDENT + P] = np.eye(P)
    const[:, C_ONES:C_ONES + P] = 1.0
    const[:, C_HALVES:C_HALVES + P] = (r[:, None] // HD) == (r[None, :] // HD)
    const[:, C_CAUSAL:C_CAUSAL + P] = np.where(r[None, :] <= r[:, None], 0.0, NEG)
    const[:, C_BEFORE:C_BEFORE + P] = r[:, None] < r[None, :]
    const[:, C_IOTA:C_IOTA + P] = r[None, :]
    inv = np.float32(10000.0) ** (-np.arange(0, P, 2, dtype=np.float32) / np.float32(P))
    const[:, C_INV] = np.tile(inv, 2)
    const[:, C_SIGN] = np.where(r < P // 2, 1.0, -1.0)
    const[:, C_TOKEN:C_TOKEN + TT] = r[:, None] + P * np.arange(TT)[None, :]
    for g in range(4):
        const[:, C_COUNT + 16 * g:C_COUNT + 16 * (g + 1)] = 1.0 / np.minimum(np.arange(16) + 1, 2 << g)
    j = np.arange(BAND)[None, :]
    chunk = r[:, None] // 64
    const[:, C_MASK:C_MASK + BAND] = np.where((j // 64 >= chunk) & (j // 64 <= chunk + 2), 0.0, NEG)
    gamma = 1.0 - 2.0 ** (-5.0 - np.arange(HEADS))
    rel = np.arange(T)[None, :] - r[:, None]
    decay = np.where(rel[None] >= 0, np.exp(np.log(gamma)[:, None, None] * np.maximum(rel, 0)[None]), 0.0) * ATT_SCALE
    decay = decay.transpose(1, 0, 2).astype(np.float32)
    dist = np.arange(VEC) - 255
    n = np.abs(dist)
    large = 8 + np.searchsorted(8.0 * 2.0 ** (np.arange(1, 8) / 2.0), n, side="right")
    bucket = np.where(dist > 0, 16, 0) + np.where(n < 8, n, np.minimum(large, 15))
    buckets = (np.arange(32)[:, None] == bucket[None, :]).astype(np.float32)

    arrays = {
        "weights": weights,
        "x": a["x"][0].T.reshape(DC, P, T).transpose(1, 0, 2),
        "c": a["c"],
        "positions": a["positions"],
        "w_ada": a["w_ada"][0].T.reshape(12, 4, P, D).transpose(0, 2, 1, 3).reshape(12, P, SLAB),
        "b_ada": cols(a["b_ada"][0]),
        "const": const,
        "decay": decay,
        "buckets": buckets,
        "vec": np.stack([cols(a[k].reshape(-1)) for k in ("norm_mix", "norm_ffn", "norm_final", "norm1_g_2", "norm2_g_2")], axis=1),
        "diff_norm": cols(a["diff_norm"][0]),
        "rel_bias": a["rel_bias_2"],
        "lam_q1": a["lam_q1"], "lam_k1": a["lam_k1"], "lam_q2": a["lam_q2"], "lam_k2": a["lam_k2"],
        "small": np.concatenate([np.tile(a["q_norm_g_2"][0], 2)[:, None], np.tile(a["k_norm_g_2"][0], 2)[:, None],
                                 cols(a["pool_scale_2"][0])], axis=1),
        "sinks": a["attn_sinks_2"],
        "pool_w": a["pool_w_2"][0].transpose(1, 0, 2),
        "w_router": np.concatenate([a["w_router_group"][0], a["w_router_expert"][0]], axis=1).reshape(DC, P, 36).transpose(1, 0, 2),
        "b_router": np.concatenate([a["b_router_group"], a["b_router_expert"]], axis=1),
        "subkeys": a["peer_subkeys_2"][0].reshape(2 * PH, PK, P).transpose(2, 0, 1),
    }
    arrays = {k: np.ascontiguousarray(v) for k, v in arrays.items()}

    nc = bacc.Bacc("TRN2", target_bir_lowering=False, num_devices=1)
    d = Names()
    for name, v in arrays.items():
        d.__dict__[name] = nc.dram_tensor("in_" + name, v.shape, mybir.dt.from_np(v.dtype), kind="ExternalInput").ap()
    d.lams = [d.lam_q1, d.lam_k1, d.lam_q2, d.lam_k2]
    scratch = lambda name, shape, dt=F32: nc.dram_tensor(name, shape, dt, kind="Internal").ap()
    d.by_distance = scratch("by_distance_rows", (SWA_HEADS, P, VEC))
    d.bias_band = [bass.AP(d.by_distance.tensor, h * P * VEC + P - 1, [[VEC - 1, P], [1, BAND]]) for h in range(SWA_HEADS)]
    d.h_rows = scratch("h_rows", (T, D))
    d.y_rows = scratch("y_rows", (BLOCKS * SLOTS, D))
    d.slot_token = scratch("slot_token", (BLOCKS * SLOTS, 1), I32)
    d.x_rows = scratch("x_rows", (P, DC, T))
    d.gelu = scratch("gelu_rows", (PK // 4, P, 4, T))
    d.gates = scratch("gates_rows", (P, PK, T))
    out = nc.dram_tensor("y", (P, DC, T), F32, kind="ExternalOutput").ap()
    d.out = out
    program(nc, d)
    result = run_bass_kernel_spmd(nc, [{"in_" + k: v for k, v in arrays.items()}], core_ids=[0])
    y = result.results[0]["y"]
    return y.transpose(1, 0, 2).reshape(D, T).T.reshape(1, T, D)
```
